# Optimizing a Trainium2 kernel written in Bass

```python
import jax
import jax.numpy as jnp
from jax import lax
import numpy as np

D_MODEL = 1024
BATCH = 1
SEQ = 512
DEPTH = 1
DEC_BATCH = 8
DEC_SEQ = 1
PAST_LEN = 4096
PAGE_SIZE = 128

N_META = 16
RWKV_WIDTH = D_MODEL // 2
RWKV_HEAD_DIM = 64
RWKV_HEADS = RWKV_WIDTH // RWKV_HEAD_DIM
DECAY_LORA = 64
AAA_LORA = 64
GATE_LORA = 128
SHIFT_WIDTH = 3 * RWKV_WIDTH + DECAY_LORA + AAA_LORA + GATE_LORA
LNX_EPS = 64e-5
RET_WIDTH = D_MODEL // 2
RET_HEADS = 4
RET_KEY_DIM = RET_WIDTH // RET_HEADS
RET_VAL_DIM = RET_WIDTH // RET_HEADS
RET_CHUNK = 128
ROPE_BASE = 10000.0
IN_WIDTH = SHIFT_WIDTH + 4 * RET_WIDTH + 2 * D_MODEL
N_GROUPS = 4
EXPERTS_PER_GROUP = 4
N_EXPERTS = N_GROUPS * EXPERTS_PER_GROUP
TOP_K = 2
EXPERT_FF = 256
RMS_EPS = 1e-6

kernel_name = "rwkv7_retention_hier_moe_step"

F32 = jnp.float32

def rmsnorm(x, g):
    xf = x.astype(F32)
    y = xf * lax.rsqrt(jnp.mean(xf * xf, axis=-1, keepdims=True) + RMS_EPS)
    return (y * g.astype(F32)).astype(x.dtype)

def rope(x, pos):
    half = x.shape[-1] // 2
    inv = ROPE_BASE ** (-jnp.arange(half, dtype=F32) / half)
    ang = pos.astype(F32)[:, None] * inv[None, :]
    c = jnp.cos(ang)[None, :, None, :]
    s = jnp.sin(ang)[None, :, None, :]
    xf = x.astype(F32)
    x1, x2 = xf[..., 0::2], xf[..., 1::2]
    return jnp.stack([x1 * c - x2 * s, x1 * s + x2 * c], axis=-1).reshape(x.shape)

def rwkv_recurrence(r, w, k, v, kk, a, s0):
    def step(S, inp):
        r_t, w_t, k_t, v_t, kk_t, a_t = inp
        sa = jnp.einsum('bhvk,bhk->bhv', S, -kk_t)
        S = (S * w_t[:, :, None, :]
             + sa[..., None] * (kk_t * a_t)[:, :, None, :]
             + v_t[..., None] * k_t[:, :, None, :])
        y = jnp.einsum('bhvk,bhk->bhv', S, r_t)
        return S, y
    xs = tuple(jnp.moveaxis(t, 1, 0) for t in (r, w, k, v, kk, a))
    s_end, ys = lax.scan(step, s0, xs)
    return jnp.moveaxis(ys, 0, 1), s_end

def retention_chunk(q, k, v, s0, log_gamma):
    C = q.shape[1]
    idx = jnp.arange(C, dtype=F32)
    diff = idx[:, None] - idx[None, :]
    lg = log_gamma[:, None, None]
    decay = jnp.where(diff[None] >= 0, jnp.exp(jnp.maximum(diff, 0.0)[None] * lg), 0.0)
    scores = jnp.einsum('bihd,bjhd->bhij', q, k) * decay[None]
    intra = jnp.einsum('bhij,bjhv->bihv', scores, v)
    q_dec = jnp.exp((idx[None, :] + 1.0) * log_gamma[:, None])
    cross = jnp.einsum('bihd,bhdv->bihv', q, s0) * q_dec.T[None, :, :, None]
    k_dec = jnp.exp((C - 1.0 - idx[None, :]) * log_gamma[:, None])
    s_new = (jnp.exp(C * log_gamma)[None, :, None, None] * s0
             + jnp.einsum('bjhd,bjhv,hj->bhdv', k, v, k_dec))
    return intra + cross, s_new

def retention_blocks(q, k, v, s0, log_gamma, n_lead):
    if n_lead == 0:
        return retention_chunk(q, k, v, s0, log_gamma)
    B = q.shape[0]
    o_lead, S = retention_chunk(q[:, :n_lead], k[:, :n_lead], v[:, :n_lead], s0, log_gamma)
    t_rest = q.shape[1] - n_lead
    nc = t_rest // RET_CHUNK

    def to_chunks(t):
        return jnp.moveaxis(t[:, n_lead:].reshape(B, nc, RET_CHUNK, t.shape[2], t.shape[3]), 1, 0)

    def step(S, c):
        o, S = retention_chunk(c[0], c[1], c[2], S, log_gamma)
        return S, o

    S, o_rest = lax.scan(step, S, (to_chunks(q), to_chunks(k), to_chunks(v)))
    o_rest = jnp.moveaxis(o_rest, 0, 1).reshape(B, t_rest, q.shape[2], v.shape[3])
    return jnp.concatenate([o_lead, o_rest], axis=1), S

def mixer(u, pos, shift0, wkv0, ret0, n_lead, p):
    B, T, _ = u.shape
    proj = u @ p['w_in']
    s_cols = proj[..., :SHIFT_WIDTH]
    ret_cols = proj[..., SHIFT_WIDTH:SHIFT_WIDTH + 4 * RET_WIDTH]
    gate_cols = proj[..., SHIFT_WIDTH + 4 * RET_WIDTH:]

    prev = jnp.concatenate([shift0[:, None, :].astype(s_cols.dtype), s_cols[:, :-1]], axis=1)
    xs = s_cols + p['shift_mu'] * (prev - s_cols)
    new_shift = s_cols[:, -1]
    W = RWKV_WIDTH
    r, k, v, wd, ad, gd = jnp.split(
        xs, [W, 2 * W, 3 * W, 3 * W + DECAY_LORA, 3 * W + DECAY_LORA + AAA_LORA], axis=-1)
    w_raw = -jax.nn.softplus(-(p['decay_w0'] + jnp.tanh(wd) @ p['decay_up'])) - 0.5
    decay = jnp.exp(-jnp.exp(w_raw.astype(F32)))
    a = jax.nn.sigmoid(p['aaa_a0'] + ad @ p['aaa_up'])
    g = jax.nn.sigmoid(gd) @ p['gate_up']

    def heads(t):
        return t.astype(F32).reshape(B, T, RWKV_HEADS, RWKV_HEAD_DIM)

    kk = heads(k * p['k_k'])
    kk = kk / jnp.maximum(jnp.sqrt(jnp.sum(kk * kk, axis=-1, keepdims=True)), 1e-12)
    k_mod = heads(k * (1.0 + (a - 1.0) * p['k_a']))
    r_h, v_h, a_h, w_h = heads(r), heads(v), heads(a), heads(decay)
    y, wkv_new = rwkv_recurrence(r_h, w_h, k_mod, v_h, kk, a_h, wkv0.astype(F32))
    mu = jnp.mean(y, axis=-1, keepdims=True)
    var = jnp.mean(jnp.square(y - mu), axis=-1, keepdims=True)
    yn = ((y - mu) * lax.rsqrt(var + LNX_EPS)).reshape(B, T, W)
    yn = yn * p['lnx_w'].astype(F32) + p['lnx_b'].astype(F32)
    bonus = jnp.sum(r_h * k_mod * p['r_k'].astype(F32), axis=-1, keepdims=True) * v_h
    ya = (yn + bonus.reshape(B, T, W)) * g.astype(F32)
    branch_a = ya.astype(u.dtype) @ p['w_branch_a']

    q_r, k_r, v_r, g_r = jnp.split(ret_cols, 4, axis=-1)
    q_r = rope(q_r.reshape(B, T, RET_HEADS, RET_KEY_DIM), pos)
    k_r = rope(k_r.reshape(B, T, RET_HEADS, RET_KEY_DIM), pos) * (RET_KEY_DIM ** -0.5)
    v_r = v_r.astype(F32).reshape(B, T, RET_HEADS, RET_VAL_DIM)
    log_gamma = jnp.log(1.0 - 2.0 ** (-5.0 - jnp.arange(RET_HEADS, dtype=F32)))
    o, ret_new = retention_blocks(q_r, k_r, v_r, ret0.astype(F32), log_gamma, n_lead)
    o = o * lax.rsqrt(jnp.mean(o * o, axis=-1, keepdims=True) + RMS_EPS)
    o = jax.nn.silu(g_r.astype(F32)) * o.reshape(B, T, RET_WIDTH)
    branch_b = o.astype(u.dtype) @ p['w_branch_b']

    g_a, g_b = jnp.split(gate_cols, 2, axis=-1)
    merged = jax.nn.sigmoid(g_a) * branch_a + jax.nn.sigmoid(g_b) * branch_b
    return merged @ p['w_out'], new_shift, wkv_new, ret_new

def hier_moe(u, p):
    B, T, _ = u.shape
    lg = (u @ p['router_group_w'] + p['router_group_b']).astype(F32)
    pg = jax.nn.softmax(lg, axis=-1)
    grp = jnp.argmax(lg, axis=-1)
    p_grp = jnp.take_along_axis(pg, grp[..., None], axis=-1)
    le = (u @ p['router_expert_w'] + p['router_expert_b']).astype(F32)
    le = le.reshape(B, T, N_GROUPS, EXPERTS_PER_GROUP)
    le_sel = jnp.take_along_axis(le, grp[..., None, None], axis=-2)[..., 0, :]
    top_v, top_i = lax.top_k(le_sel, TOP_K)
    w_top = jax.nn.softmax(top_v, axis=-1)
    within = jnp.sum(jax.nn.one_hot(top_i, EXPERTS_PER_GROUP, dtype=F32) * w_top[..., None], axis=-2)
    combine = (jax.nn.one_hot(grp, N_GROUPS, dtype=F32)[..., :, None]
               * within[..., None, :] * p_grp[..., None]).reshape(B, T, N_EXPERTS)
    h = (jax.nn.silu(jnp.einsum('btd,edf->btef', u, p['expert_w_gate']))
         * jnp.einsum('btd,edf->btef', u, p['expert_w_up']))
    h = h * combine[..., None].astype(h.dtype)
    return jnp.einsum('btef,efd->btd', h, p['expert_w_down'])

def layer(x, pos, shift0, wkv0, ret0, n_lead, p):
    m, s_new, w_new, r_new = mixer(rmsnorm(x, p['norm1_g']), pos, shift0, wkv0, ret0, n_lead, p)
    x = x + m
    x = x + hier_moe(rmsnorm(x, p['norm2_g']), p)
    return x, s_new, w_new, r_new

def setup_inputs(seed: int = 0) -> dict:
    key = jax.random.key(seed)
    ks = jax.random.split(key, 40)
    n = lambda i, shape, s: jax.random.normal(ks[i], shape, F32) * s
    L = DEPTH
    return {
        'x_prompt': n(0, (BATCH, SEQ, D_MODEL), 1.0),
        'x_sample': n(1, (DEC_BATCH, DEC_SEQ, D_MODEL), 1.0),
        'state_wkv': n(2, (L, DEC_BATCH, RWKV_HEADS, RWKV_HEAD_DIM, RWKV_HEAD_DIM), 1.0),
        'state_shift': n(3, (L, DEC_BATCH, SHIFT_WIDTH), 1.0),
        'state_ret': n(4, (L, DEC_BATCH, RET_HEADS, RET_KEY_DIM, RET_VAL_DIM), 0.5),
        'meta_tokens': n(5, (N_META, D_MODEL), 1.0),
        'norm1_g': 1.0 + n(6, (L, D_MODEL), 0.05),
        'w_in': n(7, (L, D_MODEL, IN_WIDTH), D_MODEL ** -0.5),
        'shift_mu': jax.random.uniform(ks[8], (L, SHIFT_WIDTH), F32),
        'decay_w0': jax.random.uniform(ks[9], (L, RWKV_WIDTH), F32, -6.0, 1.0),
        'decay_up': n(10, (L, DECAY_LORA, RWKV_WIDTH), 0.1),
        'aaa_a0': n(11, (L, RWKV_WIDTH), 0.1),
        'aaa_up': n(12, (L, AAA_LORA, RWKV_WIDTH), 0.5 * AAA_LORA ** -0.5),
        'gate_up': n(13, (L, GATE_LORA, RWKV_WIDTH), GATE_LORA ** -0.5),
        'k_k': 0.85 + n(14, (L, RWKV_WIDTH), 0.05),
        'k_a': 1.0 + n(15, (L, RWKV_WIDTH), 0.05),
        'r_k': n(16, (L, RWKV_HEADS, RWKV_HEAD_DIM), 0.1),
        'lnx_w': 1.0 + n(17, (L, RWKV_WIDTH), 0.05),
        'lnx_b': n(18, (L, RWKV_WIDTH), 0.01),
        'w_branch_a': n(19, (L, RWKV_WIDTH, D_MODEL), RWKV_WIDTH ** -0.5),
        'w_branch_b': n(20, (L, RET_WIDTH, D_MODEL), RET_WIDTH ** -0.5),
        'w_out': n(21, (L, D_MODEL, D_MODEL), D_MODEL ** -0.5),
        'norm2_g': 1.0 + n(22, (L, D_MODEL), 0.05),
        'router_group_w': n(23, (L, D_MODEL, N_GROUPS), D_MODEL ** -0.5),
        'router_group_b': n(24, (L, N_GROUPS), 0.01),
        'router_expert_w': n(25, (L, D_MODEL, N_EXPERTS), D_MODEL ** -0.5),
        'router_expert_b': n(26, (L, N_EXPERTS), 0.01),
        'expert_w_gate': n(27, (L, N_EXPERTS, D_MODEL, EXPERT_FF), D_MODEL ** -0.5),
        'expert_w_up': n(28, (L, N_EXPERTS, D_MODEL, EXPERT_FF), D_MODEL ** -0.5),
        'expert_w_down': n(29, (L, N_EXPERTS, EXPERT_FF, D_MODEL), EXPERT_FF ** -0.5),
        'final_norm_g': 1.0 + n(30, (D_MODEL,), 0.05),
    }

def reference(x_prompt, x_sample, state_wkv, state_shift, state_ret, meta_tokens,
              norm1_g, w_in, shift_mu, decay_w0, decay_up, aaa_a0, aaa_up, gate_up,
              k_k, k_a, r_k, lnx_w, lnx_b, w_branch_a, w_branch_b, w_out, norm2_g,
              router_group_w, router_group_b, router_expert_w, router_expert_b,
              expert_w_gate, expert_w_up, expert_w_down, final_norm_g):
    Bp, Tp, _ = x_prompt.shape
    Bs, Ts, _ = x_sample.shape
    meta = jnp.broadcast_to(meta_tokens.astype(x_prompt.dtype)[None], (Bp, N_META, D_MODEL))
    xp = jnp.concatenate([meta, x_prompt], axis=1)
    xs = x_sample
    pos_p = jnp.arange(N_META + Tp, dtype=jnp.int32)
    pos_s = PAST_LEN + jnp.arange(Ts, dtype=jnp.int32)
    zero_shift = jnp.zeros((Bp, SHIFT_WIDTH), x_prompt.dtype)
    zero_wkv = jnp.zeros((Bp, RWKV_HEADS, RWKV_HEAD_DIM, RWKV_HEAD_DIM), F32)
    zero_ret = jnp.zeros((Bp, RET_HEADS, RET_KEY_DIM, RET_VAL_DIM), F32)
    wkv_p, shift_p, ret_p, wkv_s, shift_s, ret_s = [], [], [], [], [], []
    for l in range(DEPTH):
        p = {
            'norm1_g': norm1_g[l], 'w_in': w_in[l], 'shift_mu': shift_mu[l],
            'decay_w0': decay_w0[l], 'decay_up': decay_up[l], 'aaa_a0': aaa_a0[l],
            'aaa_up': aaa_up[l], 'gate_up': gate_up[l], 'k_k': k_k[l], 'k_a': k_a[l],
            'r_k': r_k[l], 'lnx_w': lnx_w[l], 'lnx_b': lnx_b[l],
            'w_branch_a': w_branch_a[l], 'w_branch_b': w_branch_b[l], 'w_out': w_out[l],
            'norm2_g': norm2_g[l], 'router_group_w': router_group_w[l],
            'router_group_b': router_group_b[l], 'router_expert_w': router_expert_w[l],
            'router_expert_b': router_expert_b[l], 'expert_w_gate': expert_w_gate[l],
            'expert_w_up': expert_w_up[l], 'expert_w_down': expert_w_down[l],
        }
        xp, sp, wp, rp = layer(xp, pos_p, zero_shift, zero_wkv, zero_ret, N_META, p)
        xs, ss, ws, rs = layer(xs, pos_s, state_shift[l], state_wkv[l], state_ret[l], 0, p)
        wkv_p.append(wp); shift_p.append(sp); ret_p.append(rp)
        wkv_s.append(ws); shift_s.append(ss); ret_s.append(rs)
    y_prompt = rmsnorm(xp[:, N_META:], final_norm_g)
    y_sample = rmsnorm(xs, final_norm_g)
    return (y_prompt, y_sample,
            jnp.stack(wkv_p, 0), jnp.stack(shift_p, 0), jnp.stack(ret_p, 0),
            jnp.stack(wkv_s, 0), jnp.stack(shift_s, 0), jnp.stack(ret_s, 0))


_drawn_inputs = setup_inputs


def setup_inputs(seed=0):
    import zlib

    import numpy as np

    out = dict(_drawn_inputs(seed))
    spreads = {}
    factors = {'lnx_b': 5.41, 'router_group_b': 7.312, 'router_expert_b': 8.0}
    for name, (base, spread) in spreads.items():
        noise = np.random.default_rng([zlib.crc32(name.encode()), seed]).standard_normal(out[name].shape)
        drawn = base * np.exp(spread * noise) if base else spread * noise
        out[name] = jnp.asarray(drawn.astype(out[name].dtype))
    for name, factor in factors.items():
        out[name] = (out[name] * factor).astype(out[name].dtype)
    return out
```

```python
import math
from contextlib import ExitStack

import numpy as np
import concourse.bass as bass
from concourse import mybir

F32 = mybir.dt.float32
I32 = mybir.dt.int32
BF16 = mybir.dt.bfloat16
ALU = mybir.AluOpType
ACT = mybir.ActivationFunctionType
AX = mybir.AxisListType

P = 128
D = 1024
KD = D // P
META, SEQ, NB = 16, 512, 8
TP = META + SEQ
T = TP + NB
HT = T // 2
PAST = 4096
NP = 4
RH = 4
C = 64
CHUNKS = [(c * C, min(C, TP - c * C)) for c in range((TP + C - 1) // C)]
LEVELS = [1, 2, 4, 8, 16, 32]
DECAY = math.exp(-0.5)
EPS = 1e-6
LNX_EPS = 64e-5
NE, NG, EPG, FF = 16, 4, 4, 256
SLOTS = P
TT = (T + P - 1) // P
LASTT = T - (TT - 1) * P
ROUNDS = (T + SLOTS - 1) // SLOTS
ROWS = NE * SLOTS
SHIFT_TILES = 14
RET0, GA0, GB0 = 14, 30, 38

VEC = {}
_n = 0
for _name, _w in [("norm1_g", KD), ("mu", SHIFT_TILES), ("w0", NP), ("a0", NP), ("kk", NP), ("ka", NP),
                  ("rk", NP), ("lnw", NP), ("lnb", NP), ("norm2_g", KD)]:
    VEC[_name] = _n
    _n += _w
NVEC = _n

CON = {}
_n = 0
for _name, _w in [("ident", P), ("bones", P), ("ones", P), ("tri", P), ("reset", TP), ("lev", len(LEVELS) * C),
                  ("lev0", C), ("eye", C), ("ai", 2 * C), ("tie", 16), ("expert", NE),
                  ("valid", TT),
                  ("perm", P), ("smask", NB), ("cos", T), ("sin", T), ("dec", RH * TP), ("dend", TT * RH)]:
    CON[_name] = (_n, _w)
    _n += _w
NCON = _n
NKEEP = CON["perm"][0]


def constants():
    t = np.zeros((P, NCON), np.float32)

    def put(name, a):
        o, w = CON[name]
        a = np.asarray(a, np.float32).reshape(a.shape[0], -1)
        t[:a.shape[0], o:o + w] = a

    p = np.arange(P)
    put("ident", np.eye(P))
    put("bones", (p[:, None] // 64 == p[None] // 64))
    put("ones", np.ones((P, P)))
    perm = np.zeros((P, P))
    for i in range(P // 2):
        perm[2 * i + 1, 2 * i] = -1
        perm[2 * i, 2 * i + 1] = 1
    put("perm", perm)
    put("tri", p[:, None] < p[None])
    pos = np.concatenate([np.arange(TP), np.full(NB, PAST)]).astype(np.float32)
    inv = np.float32(10000.0) ** (-np.arange(64, dtype=np.float32) / np.float32(64))
    ang = (pos[None] * inv[p // 2][:, None]).astype(np.float32)
    put("cos", np.cos(ang))
    put("sin", np.sin(ang))
    lg = np.log(1.0 - 2.0 ** (-5.0 - np.arange(RH)))
    diff = np.arange(TP)[None] - p[:, None]
    put("dec", np.stack([np.where(diff >= 0, np.exp(np.maximum(diff, 0) * g), 0) for g in lg], 1))
    tok = np.arange(TT)[None, :] * P + p[:, None]
    put("dend", np.stack([np.where(tok < TP, np.exp(np.maximum(TP - 1 - tok, 0) * g), 0) for g in lg], 2))
    put("reset", np.broadcast_to(np.arange(TP) % C != 0, (P, TP)))
    row, col = p % 64, np.arange(C)

    def half(b, r, c):
        return (r // (2 * b) == c // (2 * b)) & (r // b % 2 == 1) & (c // b % 2 == 0)

    put("lev", np.stack([half(b, col[None], row[:, None]) for b in LEVELS], 1))
    put("lev0", half(1, row[:, None], col[None]))
    put("eye", row[:, None] == col[None])
    strict, incl = row[:, None] < col[None], row[:, None] <= col[None]
    put("ai", np.stack([strict, incl], 1))
    put("smask", (p[:, None] - META == np.arange(NB)[None]))
    put("tie", np.broadcast_to((np.arange(4)[None] < np.arange(4)[:, None]).reshape(-1), (P, 16)))
    put("valid", tok < T)
    put("expert", np.broadcast_to(np.arange(NE), (P, NE)))
    return t


GAMMA = [float(1.0 - 2.0 ** (-5.0 - h)) for h in range(RH)]

RB = []
for _h in range(RH):
    for _r in range(2):
        _js = [j for j in range(TT) if j * P < (_r + 1) * (TP // 2)]
        for _j in _js:
            _i0 = max(_r * (TP // 2), _j * P)
            RB.append((_h, _r, _j, _i0, (_r + 1) * (TP // 2), _j == _js[0], _j == _js[-1]))


def order():
    s = [("j_norm", 0, 0), ("j_norm", 0, 1), ("norm_end",)]

    def proj(m):
        return [("j_proj", m, 0), ("j_proj", m, 1)]

    for j in range(16):
        s += proj(RET0 + j)
        if 1 <= j <= 8:
            s += [("j_rope", j - 1, 0), ("j_rope", j - 1, 1)]
    s += [("j_vt", t) for t in range(TT)] + [("j_kt", t) for t in range(TT)]
    s += [("rs_new", h) for h in range(RH)] + [("j_ros", h) for h in range(RH)]
    for n in range(len(RB)):
        s.append(("j_score", n))
        if n:
            s.append(("att", n - 1))
    s.append(("att", len(RB) - 1))
    s += [("j_rst", h) for h in range(RH)]
    for h in range(RH):
        s += [("j_orms", h, 0), ("j_orms", h, 1)]
    for m in [12, 13, 4, 5, 6, 7, 0, 1, 2, 3, 8, 9, 10, 11]:
        s += proj(m)
        if m == 4:
            s.append(("lora_in",))
    for p in range(NP):
        for k in ("w", "a", "g"):
            s += [("j_lora", k, p, 0), ("j_lora", k, p, 1)]
    s += [("kk_in", p) for p in range(NP)]
    fill = []
    for m in range(8):
        fill += proj(GB0 + m) + [("j_bb", m, 0), ("j_bb", m, 1)]
    for m in range(8):
        fill += proj(GA0 + m)

    def take(n):
        out, fill[:] = fill[:n], fill[n:]
        return out

    for p in range(NP):
        s += [("j_kkn", p, 0), ("j_kkn", p, 1)] + take(1)
    for p in range(NP):
        s += [("bon_in", p), ("j_bon", p, 0), ("j_bon", p, 1)] + take(1)
    s += [("wk_prep", 0)]
    for c, (_, w) in enumerate(CHUNKS):
        s += [("wk_a", c)]
        if c + 1 < len(CHUNKS):
            s += [("wk_prep", c + 1)]
        s += take(1)
        for b in LEVELS[1:]:
            if b < w:
                s += [("wk_x", c, b)] + take(FILL) + [("wk_t", c, b)] + (take(1) if b in (4, 16) else [])
        s += [("wk_r", c), ("wk_sa", c)] + take(1) + [("wk_s", c)]
    s += fill
    s += [("smp", i) for i in range(2)]
    for p in range(NP):
        s += [("j_mean", p, 0), ("j_mean", p, 1)]
    for p in range(NP):
        s += [("j_var", p, 0), ("j_var", p, 1)]
    for m in range(8):
        s += [("j_ba", m, 0), ("j_ba", m, 1)]
    for m in range(8):
        s += [("j_out", m, 0), ("j_out", m, 1)]
    return s


FILL = 1
STEPS = order()
JOBS = {s: n for n, s in enumerate([s for s in STEPS if s[0].startswith("j_")])}
WTILES = [({"j_proj": "in", "j_bb": "bb", "j_ba": "ba", "j_out": "out"}[s[0]], s[1])
          for s in STEPS if s[0] in ("j_proj", "j_bb", "j_ba", "j_out") and s[2] == 0]
WJOB = {"in": "j_proj", "bb": "j_bb", "ba": "j_ba", "out": "j_out"}
WIDX = {k: n for n, k in enumerate(WTILES)}
NW = 3


def bank_of(step):
    return JOBS[step] % 2


def hybrid_step(nc, I, O):
    with ExitStack() as ctx:
        E = ctx.enter_context
        sem_names = set()

        def sem(name):
            assert name not in sem_names
            sem_names.add(name)
            return E(nc.semaphore(name))

        NARENA = 51500
        arena = E(nc.sbuf_tensor("arena", [P, NARENA], F32))
        top = [0]

        def at(n, *dims, start=None):
            if start is None:
                start = top[0]
                top[0] += n
            assert start + n <= NARENA, (start, n)
            a = arena[:, start:start + n]
            if len(dims) == 2:
                return a.rearrange("p (a b) -> p a b", a=dims[0])
            if len(dims) == 3:
                return a.rearrange("p (a b c) -> p a b c", a=dims[0], b=dims[1])
            if len(dims) == 4:
                return a.rearrange("p (a b c d) -> p a b c d", a=dims[0], b=dims[1], c=dims[2])
            return a

        con = at(NKEEP)
        vec = at(NVEC)
        up_wa = at(512)
        up_g = at(512)
        u = at(KD * T, KD, T)
        u_end = top[0]
        wt = at(NW * 1024, NW, 8, P)
        ret_o = at(RH * T, RH, T)
        tmp = at(4 * T, 4, T)
        base = top[0]
        con1 = at(NCON - NKEEP)
        ret = at(16 * T, 16, T)
        v_tok = at(TT * 512, TT, RH, P)
        k_tok = at(TT * 512, TT, RH, P)
        k_smp = at(512, RH, P)
        sc = at(3 * HT, 3, HT)
        vb = at(1024, NB, P)
        s_new = at(RH * 1024, RH, NB, P)
        o_smp = at(512, RH, P)
        o_diag = at(1024, NB, P)
        ret_st = at(512, RH, P)
        top1 = top[0]
        top[0] = base
        r_f = at(NP * T, NP, T)
        k_f = at(NP * T, NP, T)
        v_f = at(NP * T, NP, T)
        wad = at(T)
        gd = at(T)
        ly = at(NP * T, NP, T)
        b_f = at(NP * T, NP, T)
        kk_f = at(NP * T, NP, T)
        g_f = at(NP * T, NP, T)
        bon = at(NP * T, NP, T)
        raw0 = top[0]
        raw = at(2 * (T + 1), 2, T + 1)
        top[0] = raw0
        ep = at(2 * NP * (C + 1), 2, NP, C + 1)
        en = at(NP * C, NP, C)
        ar = at(2 * NP * 2 * C, 2, NP, 2, C)
        bk = at(2 * 2 * NP * C, 2, 2, NP, C)
        bkp = at(2 * NP * C, 2, NP, C)
        lev = at(6 * NP * C, 6, NP, C)
        tp = at(2 * NP * C, 2, NP, C)
        br = at(NP * C, NP, C)
        kq = at(NP * 2 * C, NP, 2, C)
        tok = at(3 * NP * C, 3, NP, C)
        xl = at(NP * C, NP, C)
        rr = at(NP * C, NP, C)
        sa = at(NP * C, NP, C)
        st = at(2 * NP * C, 2, NP, C)
        stp = at(NP * C, NP, C)
        chunk_end = top[0]
        top[0] = raw0
        ws = at(2048, NP, NB, 64)
        t1 = at(2048, NP, NB, 64)
        t2 = at(2048, NP, NB, 64)
        wsmp = at(NP * NB, NP, NB)
        top[0] = chunk_end
        merged = at(KD * T, KD, T)
        sga = at(KD * T, KD, T)
        sh = at(SHIFT_TILES * 9, SHIFT_TILES, 9)
        eps = at(1)
        lnx_eps = at(1)
        shs = at(SHIFT_TILES * NB, SHIFT_TILES, NB)
        shd = at(SHIFT_TILES * NB, SHIFT_TILES, NB)

        def cc(name, *dims, rows=P):
            o, w = CON[name]
            a = con[0:rows, o:o + w] if o < NKEEP else con1[0:rows, o - NKEEP:o - NKEEP + w]
            if len(dims) == 2:
                return a.rearrange("p (a b) -> p a b", a=dims[0])
            if len(dims) == 3:
                return a.rearrange("p (a b c) -> p a b c", a=dims[0], b=dims[1])
            return a

        def vv(name, i):
            o = VEC[name] + i
            return vec[:, o:o + 1]

        ident, bones, ones, perm = cc("ident"), cc("bones"), cc("ones"), cc("perm")

        psum = E(nc.psum_tensor("psum", [P, 4096], F32))

        def bank(b, n=512, rows=P):
            return psum[0:rows, 512 * b:512 * b + n]

        s_load = sem("s_load")
        s_w = [sem(f"s_w{i}") for i in range(NW)]
        s_job = sem("s_job")
        s_free = [sem(f"s_free{i}") for i in range(2)]
        s_act = sem("s_act")
        s_dve = sem("s_dve")
        s_pool = sem("s_pool")
        s_sq = sem("s_sq")
        s_rms = sem("s_rms")
        s_u = sem("s_u")
        s_raw = sem("s_raw")
        s_shift = sem("s_shift")
        s_sig = sem("s_sig")
        s_kq = sem("s_kq")
        s_vb = sem("s_vb")
        s_rsp = sem("s_rsp")
        s_sn = sem("s_sn")
        s_roq = sem("s_roq")
        s_od = sem("s_od")
        s_osq = sem("s_osq")
        s_ph = sem("s_ph")
        s_smr = sem("s_smr")
        s_ws = sem("s_ws")
        s_vsr = sem("s_vsr")
        s_att = sem("s_att")
        s_atf = [sem(f"s_atf{i}") for i in range(2)]
        s_lin = sem("s_lin")
        s_kkt = sem("s_kkt")
        s_kks = sem("s_kks")
        s_kkd = sem("s_kkd")
        s_bont = sem("s_bont")
        s_e = sem("s_e")
        s_ab = sem("s_ab")
        s_abp = sem("s_abp")
        s_pab = sem("s_pab")
        s_tri = sem("s_tri")
        s_toks = sem("s_toks")
        s_px = sem("s_px")
        s_xl = sem("s_xl")
        s_pt = sem("s_pt")
        s_tt = sem("s_tt")
        s_pr = sem("s_pr")
        s_rr = sem("s_rr")
        s_psa = sem("s_psa")
        s_sa = sem("s_sa")
        s_ps = sem("s_ps")
        s_st = sem("s_st")
        s_y = sem("s_y")
        s_gb = sem("s_gb")
        s_m1 = sem("s_m1")
        s_sw = sem("s_sw")
        s_sld = sem("s_sld")
        s_smt = sem("s_smt")
        s_smp = sem("s_smp")
        s_var = sem("s_var")
        s_vsd = sem("s_vsd")
        s_ya = sem("s_ya")
        s_mg = sem("s_mg")
        s_xr = sem("s_xr")
        s_x2 = sem("s_x2")
        s_out = sem("s_out")
        s_rets = sem("s_rets")
        s_rst = sem("s_rst")

        def job(step):
            return JOBS[step]

        def job_done(eng, step):
            eng.wait_ge(s_job, JOBS[step] + 1)

        def job_read(eng, step):
            n = JOBS[step]
            eng.wait_ge(s_free[n % 2], n // 2 + 1)

        def job_ps(step, n=HT, rows=P):
            return bank(JOBS[step] % 2, n, rows)

        def cols(hf):
            return slice(hf * HT, (hf + 1) * HT)

        NCH = len(CHUNKS)
        NLEV = [sum(1 for b in LEVELS[1:] if b < w) for _, w in CHUNKS]
        LEV0 = [sum(NLEV[:c]) for c in range(NCH)]

        def wk(c, s):
            t0, w = CHUNKS[c]
            return t0, w, slice(64 * s, 64 * s + 64), slice(64 * s, 64 * s + w)

        def bc(a, n):
            return a.unsqueeze(len(a.shape)).broadcast_to(list(a.shape) + [n])

        def pairs(a):
            return a.unsqueeze(1).broadcast_to([a.shape[0], NP] + list(a.shape[1:]))

        mixer = nc.Block()
        block = mixer.__enter__()

        @block.sync
        def _(sp):
            for dst, src in ((u, I["x"]), (con, I["con"][:, 0:NKEEP]), (con1, I["con"][:, NKEEP:NCON]), (vec, I["vec"]), (shs, I["sh0"]),
                             (up_wa, I["up_wa"]), (up_g, I["up_g"])):
                sp.dma_start(dst, src).then_inc(s_load, 16)

            def weights(i):
                kind, m = WTILES[i]
                if i >= NW:
                    k0, m0 = WTILES[i - NW]
                    job_done(sp, (WJOB[k0], m0, 1))
                nk = 8 if kind in ("in", "out") else 4
                sp.dma_start(wt[:, i % NW, 0:nk, :], I["w_" + kind][m]).then_inc(s_w[i % NW], 16)

            for i in range(len(WTILES)):
                if i == NW:
                    sp.dma_start(s_new, I["rets0"]).then_inc(s_rets, 16)
                if i == 16 + NW:
                    for h in range(RH):
                        job_read(sp, ("j_rst", h))
                    sp.dma_start(O["retp"], ret_st).then_inc(s_out, 16)
                    sp.wait_ge(s_sn, RH)
                    sp.wait_ge(s_roq, RH)
                    sp.dma_start(O["rets"], s_new).then_inc(s_out, 16)
                if i == WIDX[("ba", NW)]:
                    for q in range(2):
                        job_done(sp, ("j_proj", GA0 + 7, q))
                    sp.dma_start(u, I["x"]).then_inc(s_xr, 16)
                    sp.wait_ge(s_y, NCH)
                    sp.wait_ge(s_st, NCH + 1)
                    sp.dma_start(ws, I["wkv0"]).then_inc(s_sld, 16)
                    sp.dma_start(O["wkvp"], st[:, NCH % 2]).then_inc(s_out, 16)
                    sp.wait_ge(s_raw, SHIFT_TILES)
                    sp.dma_start(O["shift"], sh).then_inc(s_out, 16)
                if i == WIDX[("out", 2)]:
                    sp.wait_ge(s_ws, 1)
                    sp.dma_start(O["wkvs"], ws).then_inc(s_out, 16)
                weights(i)
            sp.wait_ge(s_out, 16 * 5)

        @block.tensor
        def _(pe):
            mm = nc.tensor.matmul

            def open_job(step):
                n = JOBS[step]
                if n >= 2:
                    pe.wait_ge(s_free[n % 2], n // 2)
                return job_ps(step)

            def weight(step, kind):
                i = WIDX[(kind, step[1])]
                if step[2] == 0:
                    pe.wait_ge(s_w[i % NW], 16 * (i // NW + 1))
                return wt[:, i % NW]

            def products(step, kind, nk, rhs):
                ps = open_job(step)
                w = weight(step, kind)
                for k in range(nk):
                    last = mm(ps, w[:, k, :], rhs[:, k, cols(step[2])], start=(k == 0), stop=(k == nk - 1))
                last.then_inc(s_job, 1)

            pe.wait_ge(s_load, 112)
            for step in STEPS:
                kind = step[0]
                if kind == "j_norm":
                    ps = open_job(step)
                    for k in range(KD):
                        if step[2] == 0:
                            pe.wait_ge(s_sq, k + 1)
                        last = mm(ps, ones, merged[:, k, cols(step[2])], start=(k == 0), stop=(k == KD - 1))
                    last.then_inc(s_job, 1)
                elif kind == "j_proj":
                    if step == ("j_proj", RET0, 0):
                        pe.wait_ge(s_u, KD)
                    products(step, "in", KD, u)
                elif kind == "j_rope":
                    _, j, hf = step
                    job_read(pe, ("j_proj", RET0 + j, hf))
                    ps = open_job(step)
                    mm(ps, perm, ret[:, j, cols(hf)], start=True, stop=True).then_inc(s_job, 1)
                elif kind in ("j_vt", "j_kt"):
                    t = step[1]
                    n = LASTT if t == TT - 1 else P
                    open_job(step)
                    ps = bank(bank_of(step), 512, n)
                    if kind == "j_vt":
                        job_read(pe, ("j_proj", RET0 + 11, 0))
                        job_read(pe, ("j_proj", RET0 + 11, 1))
                    else:
                        pe.wait_ge(s_kq, 16)
                    for h in range(RH):
                        src = ret[:, (8 if kind == "j_vt" else 4) + h, t * P:t * P + n]
                        last = nc.tensor.transpose(ps[:, h * P:(h + 1) * P], src, ident)
                    last.then_inc(s_job, 1)
                elif kind == "rs_new":
                    h = step[1]
                    pe.wait_ge(s_vb, h + 1)
                    if h:
                        pe.wait_ge(s_sn, h)
                    job_read(pe, ("j_kt", TT - 1))
                    for q in range(2):
                        last = mm(bank(4 + q), k_smp[0:LASTT, h, :], vb[0:LASTT, 4 * q:4 * q + 4, :],
                                  start=True, stop=True)
                    last.then_inc(s_rsp, 1)
                    pe.wait_ge(s_sn, h + 1)
                    if h:
                        pe.wait_ge(s_od, h)
                    for q in range(2):
                        last = mm(bank(6 + q, 512, NB), ret[:, h, TP:T], s_new[:, h, 4 * q:4 * q + 4, :],
                                  start=True, stop=True)
                    last.then_inc(s_roq, 1)
                elif kind == "j_ros":
                    h = step[1]
                    open_job(step)
                    pe.wait_ge(s_od, h + 1)
                    mm(job_ps(step, NB), o_smp[0:NB, h, :], ident[0:NB, 0:NB], start=True,
                       stop=True).then_inc(s_job, 1)
                elif kind == "j_score":
                    h, r, j, i0, i1, first, last_ = RB[step[1]]
                    n = min(P, TP - j * P)
                    open_job(step)
                    mm(job_ps(step, i1 - i0, n), ret[:, 4 + h, j * P:j * P + n], ret[:, h, i0:i1],
                       start=True, stop=True).then_inc(s_job, 1)
                elif kind == "att":
                    b = step[1]
                    h, r, j, i0, i1, first, last_ = RB[b]
                    n = min(P, TP - j * P)
                    g = 2 * h + r
                    if first and g >= 2:
                        pe.wait_ge(s_atf[g % 2], g // 2)
                    job_read(pe, ("j_score", b))
                    o0 = i0 - r * (TP // 2)
                    x = mm(bank(2 + g % 2)[:, o0:TP // 2], v_tok[0:n, j, h, :], sc[0:n, b % 3, 0:i1 - i0],
                           start=first, stop=last_)
                    x.then_inc(s_att, 1)
                elif kind == "j_rst":
                    h = step[1]
                    open_job(step)
                    for j in range(TT):
                        n = LASTT if j == TT - 1 else P
                        last = mm(job_ps(step, P), k_tok[0:n, j, h, :], v_tok[0:n, j, h, :], start=(j == 0),
                                  stop=(j == TT - 1))
                    last.then_inc(s_job, 1)
                elif kind == "j_orms":
                    ps = open_job(step)
                    pe.wait_ge(s_osq, step[1] + 1)
                    mm(ps, ones, tmp[:, step[1] % 2, cols(step[2])], start=True, stop=True).then_inc(s_job, 1)
                elif kind == "j_lora":
                    _, k, p, hf = step
                    ps = open_job(step)
                    pe.wait_ge(s_lin, 2)
                    rows = {"w": slice(0, 64), "a": slice(64, P), "g": slice(0, P)}[k]
                    w, x = (up_g, gd) if k == "g" else (up_wa, wad)
                    mm(ps, w[rows, p * P:(p + 1) * P], x[rows, cols(hf)], start=True, stop=True)\
                        .then_inc(s_job, 1)
                elif kind in ("j_kkn", "j_bon"):
                    _, p, hf = step
                    ps = open_job(step)
                    pe.wait_ge(s_kkt if kind == "j_kkn" else s_bont, p + 1)
                    mm(ps, bones, tmp[:, p, cols(hf)] if kind == "j_kkn" else tmp[:, p % 2, cols(hf)],
                       start=True, stop=True).then_inc(s_job, 1)
                elif kind == "j_bb":
                    if step[1:] == (0, 0):
                        pe.wait_ge(s_att, len(RB))
                        pe.wait_ge(s_ph, 1)
                    products(step, "bb", NP, ret_o)
                elif kind == "wk_a":
                    c = step[1]
                    t0, w, _, _ = wk(c, 0)
                    q = c % 2
                    pe.wait_ge(s_ab, c + 1)
                    if c:
                        pe.wait_ge(s_tri, 4 * c)
                        pe.wait_ge(s_tt, LEV0[c])
                        pe.wait_ge(s_rr, c)
                        pe.wait_ge(s_sa, c)
                        pe.wait_ge(s_st, c + 1)
                        pe.wait_ge(s_y, c)
                        pe.wait_ge(s_toks, 3 * c)
                    for s in range(2):
                        _, _, full, part = wk(c, s)
                        for p in range(NP):
                            rhs = ar[full, q, p, :, 0:w]
                            o = psum[part, 1024 + 128 * p:1024 + 128 * p + 128]\
                                .rearrange("p (a b) -> p a b", a=2)[:, :, 0:w]
                            mm(o, bk[full, q, 0, p, 0:w], rhs, start=True, stop=True)
                            o = psum[part, 1536 + 128 * p:1536 + 128 * p + 128]\
                                .rearrange("p (a b) -> p a b", a=2)[:, :, 0:w]
                            mm(o, bk[full, q, 1, p, 0:w], rhs, start=True, stop=True)
                            last = mm(psum[part, 2048 + 64 * p:2048 + 64 * p + w], ar[full, q, p, 0, 0:w],
                                      bk[full, q, 0, p, 0:w], start=True, stop=True)
                    last.then_inc(s_pab, 1)
                    for i in range(3):
                        b = 7 - i
                        if i == 1:
                            pe.wait_ge(s_abp, c + 1)
                        for p in range(NP):
                            src = v_f[:, p, t0:t0 + w] if i == 0 else bkp[:, i - 1, p, 0:w]
                            last = nc.tensor.transpose(bank(b, 512, w)[:, p * P:(p + 1) * P], src, ident)
                        last.then_inc(s_px, 1)
                elif kind == "wk_x":
                    _, c, b = step
                    l = LEVELS.index(b)
                    if b == 2:
                        pe.wait_ge(s_tri, 4 * c + 4)
                    else:
                        pe.wait_ge(s_tt, LEV0[c] + l - 1)
                    for s in range(2):
                        _, w, full, part = wk(c, s)
                        for p in range(NP):
                            last = mm(psum[part, 2048 + 64 * p:2048 + 64 * p + w], lev[part, l, p, 0:w],
                                      tp[part, 0, p, 0:w], start=True, stop=True)
                    last.then_inc(s_pt, 1)
                elif kind == "wk_t":
                    _, c, b = step
                    l = LEVELS.index(b)
                    pe.wait_ge(s_xl, LEV0[c] + l)
                    if b == 2:
                        pe.wait_ge(s_toks, 3 * c + 3)
                    for s in range(2):
                        _, w, full, part = wk(c, s)
                        for p in range(NP):
                            if 2 * b < w:
                                mm(psum[part, 2560 + 64 * p:2560 + 64 * p + w], tp[part, 1, p, 0:w],
                                   xl[part, p, 0:w], start=True, stop=True)
                            last = mm(psum[part, 2816 + 64 * p:2816 + 64 * p + w], xl[part, p, 0:w],
                                      tp[part, 1, p, 0:w], start=True, stop=True)
                    last.then_inc(s_pr, 1)
                elif kind == "wk_r":
                    c = step[1]
                    q = c % 2
                    pe.wait_ge(s_st, c + 1)
                    pe.wait_ge(s_toks, 3 * c + 3)
                    for s in range(2):
                        _, w, full, part = wk(c, s)
                        for p in range(NP):
                            o = psum[part, 3072 + 64 * p:3072 + 64 * p + 64]
                            mm(o, ar[full, q, p, 0, 0:w], st[full, q, p, :], start=True, stop=False)
                            last = mm(o, kq[part, p, 0, 0:w], tok[part, 0, p, :], start=False, stop=True)
                    last.then_inc(s_psa, 1)
                elif kind == "wk_sa":
                    c = step[1]
                    pe.wait_ge(s_tt, LEV0[c] + NLEV[c])
                    pe.wait_ge(s_rr, c + 1)
                    for s in range(2):
                        _, w, full, part = wk(c, s)
                        for p in range(NP):
                            last = mm(psum[part, 3328 + 64 * p:3328 + 64 * p + 64], tp[part, 1, p, 0:w],
                                      rr[part, p, :], start=True, stop=True)
                    last.then_inc(s_psa, 1)
                elif kind == "wk_s":
                    c = step[1]
                    q = c % 2
                    pe.wait_ge(s_sa, c + 1)
                    for s in range(2):
                        _, w, full, part = wk(c, s)
                        for p in range(NP):
                            o = psum[full, 3584 + 64 * p:3584 + 64 * p + 64]
                            mm(o, tok[part, 1, p, :], sa[part, p, :], start=True, stop=False)
                            last = mm(o, tok[part, 2, p, :], tok[part, 0, p, :], start=False, stop=True)
                    last.then_inc(s_ps, 1)
                    for s in range(2):
                        _, w, full, part = wk(c, s)
                        for p in range(NP):
                            o = psum[full, 3072 + 64 * p:3072 + 64 * p + w]
                            mm(o, st[full, q, p, :], ar[full, q, p, 1, 0:w], start=True, stop=False)
                            mm(o, sa[part, p, :], br[part, p, 0:w], start=False, stop=False)
                            last = mm(o, tok[part, 0, p, :], kq[part, p, 1, 0:w], start=False, stop=True)
                    last.then_inc(s_ps, 1)
                elif kind == "smp":
                    i = step[1]
                    for k in ([0, 1] if i == 0 else [2]):
                        pe.wait_ge(s_smt, k + 1)
                        if k:
                            pe.wait_ge(s_smr, k)
                        for q in range(4):
                            last = mm(bank(2 + q), bones, (t2 if k == 1 else t1)[:, q, :, :], start=True, stop=True)
                        last.then_inc(s_smp, 1)
                elif kind in ("j_mean", "j_var"):
                    _, p, hf = step
                    ps = open_job(step)
                    if kind == "j_mean":
                        pe.wait_ge(s_y, NCH + 1)
                    else:
                        pe.wait_ge(s_vsd, p + 1)
                    mm(ps, bones, (ly if kind == "j_mean" else tmp)[:, p, cols(hf)], start=True,
                       stop=True).then_inc(s_job, 1)
                elif kind == "j_ba":
                    if step[1:] == (0, 0):
                        pe.wait_ge(s_ya, NP)
                    products(step, "ba", NP, ly)
                elif kind == "j_out":
                    if step[1:] == (0, 0):
                        pe.wait_ge(s_mg, KD)
                    products(step, "out", KD, merged)

        SHIFT_ORDER = [s_[1] for s_ in STEPS if s_[0] == "j_proj" and s_[1] < SHIFT_TILES and s_[2] == 0]

        def shifted(m):
            return [r_f, k_f, v_f][m // 4][:, m % 4, :] if m < 12 else (wad, gd)[m - 12]

        @block.scalar
        def _(act):
            own = [0]

            def run(ins, s=None):
                if s is None:
                    own[0] += 1
                    ins.then_inc(s_act, 1)
                    act.wait_ge(s_act, own[0])
                else:
                    ins.then_inc(s, 1)

            def f(out, in_, fn=ACT.Copy, s=None, **kw):
                run(nc.scalar.activation(out, in_, fn, **kw), s)

            act.wait_ge(s_load, 112)
            nsig = 0
            for step in STEPS:
                kind = step[0]
                free = s_free[JOBS[step] % 2] if step in JOBS else None
                if kind == "j_norm":
                    job_done(act, step)
                    f(tmp[:, 0, cols(step[2])], job_ps(step), ACT.Sqrt, scale=1.0 / D, bias=eps, s=free)
                elif kind == "j_proj":
                    _, m, hf = step
                    job_done(act, step)
                    if m < SHIFT_TILES:
                        i = SHIFT_ORDER.index(m)
                        if i == 0:
                            act.wait_ge(s_ph, 1)
                        if i >= 2:
                            act.wait_ge(s_shift, i - 1)
                        f(raw[:, i % 2, 1 + hf * HT:1 + (hf + 1) * HT], job_ps(step), s=free)
                        if hf:
                            job_read(act, ("j_proj", m, 0))
                            job_read(act, step)
                            f(sh[:, m, :], raw[:, i % 2, TP:TP + 9], s=s_raw)
                    elif m < RET0 + 12:
                        f(ret[:, m - RET0, cols(hf)], job_ps(step), s=free)
                    elif m < GA0:
                        f(ret[:, m - RET0, cols(hf)], job_ps(step), ACT.Sigmoid, s=s_sig)
                    elif m < GB0:
                        f(sga[:, m - GA0, cols(hf)], job_ps(step), ACT.Sigmoid, s=free)
                    else:
                        f(merged[:, m - GB0, cols(hf)], job_ps(step), ACT.Sigmoid, s=free)
                elif kind == "j_vt":
                    t = step[1]
                    n = LASTT if t == TT - 1 else P
                    job_done(act, step)
                    f(v_tok[0:n, t, :, :], bank(bank_of(step), 512, n).rearrange("p (h v) -> p h v", h=RH), s=free)
                elif kind == "j_ros":
                    job_done(act, step)
                    f(ret_o[:, step[1], TP:T], job_ps(step, NB), s=free)
                elif kind == "att":
                    b = step[1]
                    h, r, j, i0, i1, first, last_ = RB[b]
                    if last_:
                        g = 2 * h + r
                        act.wait_ge(s_att, b + 1)
                        f(ret_o[:, h, r * (TP // 2):(r + 1) * (TP // 2)], bank(2 + g % 2, TP // 2), s=s_atf[g % 2])
                elif kind == "j_rst":
                    job_done(act, step)
                    f(ret_st[:, step[1], :], job_ps(step, P), s=free)
                elif kind == "j_orms":
                    _, h, hf = step
                    job_done(act, step)
                    f(tmp[:, h % 2, cols(hf)], job_ps(step), ACT.Sqrt, scale=1.0 / P, bias=eps, s=free)
                elif kind == "lora_in":
                    act.wait_ge(s_shift, 2)
                    f(wad[0:64, :], wad[0:64, :], ACT.Tanh, s=s_lin)
                    f(gd, gd, ACT.Sigmoid, s=s_lin)
                elif kind == "j_lora":
                    _, k, p, hf = step
                    job_done(act, step)
                    if k == "g":
                        f(g_f[:, p, cols(hf)], job_ps(step), s=free)
                    else:
                        f((ly if k == "w" else b_f)[:, p, cols(hf)], job_ps(step), ACT.Sigmoid,
                          bias=vv("w0" if k == "w" else "a0", p), s=free)
                elif kind == "j_kkn":
                    job_done(act, step)
                    f(tmp[:, step[1], cols(step[2])], job_ps(step), ACT.Sqrt, s=free)
                elif kind == "wk_prep":
                    c = step[1]
                    t0, w, _, _ = wk(c, 0)
                    if c == 0:
                        act.wait_ge(s_bont, NP)
                        act.wait_ge(s_st, 1)
                    else:
                        act.wait_ge(s_ab, c)
                    if c >= 2:
                        act.wait_ge(s_st, c)
                    f(ep[:, c % 2, :, 1:w + 1], ly[:, :, t0:t0 + w], ACT.Exp, scale=-DECAY, s=s_e)
                    f(en[:, :, 0:w], ly[:, :, t0:t0 + w], ACT.Exp, scale=DECAY, s=s_e)
                elif kind == "wk_a":
                    c = step[1]
                    if c:
                        act.wait_ge(s_ps, 2 * c)
                    for i in range(3):
                        act.wait_ge(s_px, 3 * c + i + 1)
                        for s in range(2):
                            _, w, full, part = wk(c, s)
                            src = bank(7 - i, 512, w).rearrange("t (p s k) -> t p s k", p=NP, s=2)[:, :, s, :]
                            nc.scalar.activation(tok[part, i, :, :], src, ACT.Copy).then_inc(s_toks if s else s_act, 1)
                            if s == 0:
                                own[0] += 1
                        act.wait_ge(s_act, own[0])
                elif kind == "wk_x":
                    _, c, b = step
                    l = LEVELS.index(b)
                    _, w, _, _ = wk(c, 0)
                    act.wait_ge(s_pt, LEV0[c] + l)
                    f(xl[:, :, 0:w], bank(4, 256).rearrange("t (p k) -> t p k", p=NP)[:, :, 0:w], s=s_xl)
                elif kind == "wk_r":
                    c = step[1]
                    act.wait_ge(s_psa, 2 * c + 1)
                    f(rr, bank(6, 256).rearrange("t (p k) -> t p k", p=NP), s=s_rr)
                elif kind == "wk_sa":
                    c = step[1]
                    act.wait_ge(s_psa, 2 * c + 2)
                    f(sa, psum[:, 3328:3584].rearrange("t (p k) -> t p k", p=NP), s=s_sa)
                elif kind == "wk_s":
                    c = step[1]
                    t0, w, _, _ = wk(c, 0)
                    act.wait_ge(s_ps, 2 * c + 2)
                    f(ly[:, :, t0:t0 + w], bank(6, 256).rearrange("t (p k) -> t p k", p=NP)[:, :, 0:w], s=s_y)
                elif step == ("smp", 0):
                    act.wait_ge(s_y, NCH)
                    f(wsmp, ly[:, :, TP:T], ACT.Exp, scale=-DECAY, s=s_sw)
                elif kind == "j_var":
                    _, p, hf = step
                    job_done(act, step)
                    f(tmp[:, p, cols(hf)], job_ps(step), ACT.Sqrt, scale=1.0 / 64, bias=lnx_eps, s=free)

        @block.vector
        def _(dve):
            v = nc.vector
            own = [0]
            counts = {}

            def run(ins, s=None):
                s = s_dve if s is None else s
                counts[s.name] = counts.get(s.name, 0) + 1
                ins.then_inc(s, 1)
                if s.name in alone:
                    dve.wait_ge(s, counts[s.name])

            alone = {x.name for x in (s_dve, s_sq, s_u, s_shift, s_kq, s_vb, s_sn, s_od, s_osq, s_ph, s_kkt,
                                      s_bont, s_ab, s_abp, s_tri, s_tt, s_st, s_smt, s_smr, s_ws, s_vsd, s_ya,
                                      s_mg, s_x2)}

            def tt(out, a, b, op=ALU.mult, s=None):
                run(v.tensor_tensor(out, a, b, op), s)

            def stt(out, a, sc_, b, op0, op1, s=None):
                run(v.scalar_tensor_tensor(out, a, sc_, b, op0, op1), s)

            def ts(out, a, s1, s2, op0, op1=None, s=None):
                run(v.tensor_scalar(out, a, s1, s2, op0, op1) if op1 is not None
                    else v.tensor_scalar(out, a, s1, None, op0), s)

            dve.wait_ge(s_load, 112)
            run(v.memset(eps, EPS))
            run(v.memset(lnx_eps, LNX_EPS))
            for k in range(KD):
                tt(merged[:, k, :], u[:, k, :], u[:, k, :], s=s_sq)
            nsig = 0
            for step in STEPS:
                kind = step[0]
                free = s_free[JOBS[step] % 2] if step in JOBS else None
                if kind == "norm_end":
                    job_read(dve, ("j_norm", 0, 0))
                    job_read(dve, ("j_norm", 0, 1))
                    run(v.reciprocal(tmp[:, 1, :], tmp[:, 0, :]))
                    for k in range(KD):
                        stt(u[:, k, :], u[:, k, :], vv("norm1_g", k), tmp[:, 1, :], ALU.mult, ALU.mult, s=s_u)
                elif kind == "j_proj":
                    _, m, hf = step
                    if m < SHIFT_TILES and hf:
                        i = SHIFT_ORDER.index(m)
                        x = raw[:, i % 2, :]
                        o = shifted(m)
                        dve.wait_ge(s_raw, i + 1)
                        tt(tmp[:, 0, 0:TP], x[:, 0:TP], x[:, 1:TP + 1], ALU.subtract)
                        tt(shd[:, m, :], shs[:, m, :], sh[:, m, 1:9], ALU.subtract)
                        stt(o[:, TP:T], shd[:, m, :], vv("mu", m), sh[:, m, 1:9], ALU.mult, ALU.add)
                        stt(o[:, 0:TP], tmp[:, 0, 0:TP], vv("mu", m), x[:, 1:TP + 1], ALU.mult, ALU.add, s=s_shift)
                    elif RET0 + 12 <= m < GA0:
                        nsig += 1
                        dve.wait_ge(s_sig, nsig)
                        tt(ret[:, m - RET0, cols(hf)], job_ps(step), ret[:, m - RET0, cols(hf)], s=free)
                elif kind == "j_rope":
                    _, j, hf = step
                    a = 1.0 if j < RH else P ** -0.5
                    x = ret[:, j, cols(hf)]
                    job_done(dve, step)
                    stt(tmp[:, 2, 0:HT], job_ps(step), a, cc("sin")[:, cols(hf)], ALU.mult, ALU.mult, s=free)
                    stt(tmp[:, 3, 0:HT], x, a, cc("cos")[:, cols(hf)], ALU.mult, ALU.mult)
                    job_read(dve, step)
                    tt(x, tmp[:, 2, 0:HT], tmp[:, 3, 0:HT], ALU.add, s=s_kq)
                elif kind == "j_kt":
                    t = step[1]
                    n = LASTT if t == TT - 1 else P
                    ps = bank(bank_of(step), 512, n).rearrange("p (h v) -> p h v", h=RH)
                    job_done(dve, step)
                    if t == TT - 1:
                        run(v.tensor_copy(k_smp[0:n], ps))
                    tt(k_tok[0:n, t, :, :], ps, bc(cc("dend", TT, RH, rows=n)[:, t, :], P), s=free)
                elif kind == "rs_new":
                    h = step[1]
                    if h == 0:
                        job_read(dve, ("j_vt", TT - 1))
                        dve.wait_ge(s_rets, 16)
                    else:
                        dve.wait_ge(s_rsp, h)
                    tt(vb[0:LASTT], v_tok[0:LASTT, TT - 1, h, :].unsqueeze(1).broadcast_to([LASTT, NB, P]),
                       bc(cc("smask", rows=LASTT), P), s=s_vb)
                    dve.wait_ge(s_rsp, h + 1)
                    stt(s_new[:, h].rearrange("p b v -> p (b v)"), s_new[:, h].rearrange("p b v -> p (b v)"),
                        GAMMA[h], psum[:, 2048:3072], ALU.mult, ALU.add, s=s_sn)
                    dve.wait_ge(s_roq, h + 1)
                    tt(o_diag[0:NB], psum[0:NB, 3072:4096].rearrange("p (b v) -> p b v", b=NB),
                       bc(ident[0:NB, 0:NB], P))
                    run(v.tensor_reduce(o_smp[0:NB, h, :], o_diag[0:NB].rearrange("p b v -> p v b"), AX.X, ALU.add),
                        s_od)
                elif kind == "j_score":
                    n_ = step[1]
                    h, r, j, i0, i1, first, last_ = RB[n_]
                    n = min(P, TP - j * P)
                    job_done(dve, step)
                    if n_ >= 3:
                        dve.wait_ge(s_att, n_ - 2)
                    d = cc("dec", RH, TP, rows=n)[:, h, i0 - j * P:i1 - j * P]
                    tt(sc[0:n, n_ % 3, 0:i1 - i0], job_ps(step, i1 - i0, n), d, s=free)
                elif kind == "j_orms":
                    _, h, hf = step
                    if hf == 0:
                        job_read(dve, ("j_ros", h))
                        for g in range(2):
                            dve.wait_ge(s_atf[g], h + 1)
                        tt(tmp[:, h % 2, :], ret_o[:, h, :], ret_o[:, h, :], s=s_osq)
                    else:
                        job_read(dve, ("j_orms", h, 0))
                        job_read(dve, step)
                        run(v.reciprocal(tmp[:, h % 2, :], tmp[:, h % 2, :]))
                        tt(ret_o[:, h, :], ret_o[:, h, :], tmp[:, h % 2, :])
                        if h == 0:
                            for q in range(2):
                                job_read(dve, ("j_proj", GA0 - 1, q))
                        tt(ret_o[:, h, :], ret_o[:, h, :], ret[:, 12 + h, :])
                        if h == RH - 1:
                            dve.wait_ge(s_out, 32)
                            run(v.memset(raw[:, :, 0:1], 0.0), s_ph)
                elif kind == "kk_in":
                    p = step[1]
                    for hf in range(2):
                        job_read(dve, ("j_lora", "w", p, hf))
                    run(v.tensor_tensor_scan(ly[:, p, 0:TP], cc("reset"), ly[:, p, 0:TP], 0.0, ALU.mult, ALU.add))
                    ts(kk_f[:, p, :], k_f[:, p, :], vv("kk", p), None, ALU.mult)
                    tt(tmp[:, p, :], kk_f[:, p, :], kk_f[:, p, :], s=s_kkt)
                elif kind == "j_kkn" and step[2]:
                    p = step[1]
                    for hf in range(2):
                        job_read(dve, ("j_kkn", p, hf))
                    ts(tmp[:, p, :], tmp[:, p, :], 1e-12, None, ALU.max)
                    run(v.reciprocal(tmp[:, p, :], tmp[:, p, :]))
                    tt(kk_f[:, p, :], kk_f[:, p, :], tmp[:, p, :])
                elif kind == "bon_in":
                    p = step[1]
                    for hf in range(2):
                        job_read(dve, ("j_lora", "a", p, hf))
                    ts(tmp[:, 2, :], b_f[:, p, :], -1.0, vv("ka", p), ALU.add, ALU.mult)
                    stt(k_f[:, p, :], tmp[:, 2, :], 1.0, k_f[:, p, :], ALU.add, ALU.mult)
                    tt(b_f[:, p, :], kk_f[:, p, :], b_f[:, p, :])
                    if p >= 2:
                        job_done(dve, ("j_bon", p - 2, 1))
                    stt(tmp[:, p % 2, :], r_f[:, p, :], vv("rk", p), k_f[:, p, :], ALU.mult, ALU.mult, s=s_bont)
                elif kind == "j_bon":
                    _, p, hf = step
                    job_done(dve, step)
                    tt(bon[:, p, cols(hf)], job_ps(step), v_f[:, p, cols(hf)], s=free)
                elif kind == "wk_prep":
                    c = step[1]
                    q = c % 2
                    t0, w, _, _ = wk(c, 0)
                    if c == 0:
                        run(v.memset(ep[:, :, :, 0:1], 1.0))
                        run(v.memset(st[:, 0], 0.0), s_st)
                    dve.wait_ge(s_e, 2 * c + 2)
                    if c >= 2:
                        dve.wait_ge(s_ps, 2 * c - 2)
                    x = slice(t0, t0 + w)
                    tt(bk[:, q, 0, :, 0:w], b_f[:, :, x], en[:, :, 0:w])
                    tt(bk[:, q, 1, :, 0:w], k_f[:, :, x], en[:, :, 0:w])
                    stt(ar[:, q, :, 0, 0:w], kk_f[:, :, x], -1.0, ep[:, q, :, 0:w], ALU.mult, ALU.mult)
                    tt(ar[:, q, :, 1, 0:w], r_f[:, :, x], ep[:, q, :, 1:w + 1], s=s_ab)
                    if c:
                        dve.wait_ge(s_px, 3 * c)
                    for i in range(2):
                        tt(bkp[:, i, :, 0:w], bk[:, q, i, :, 0:w], bc(ep[:, q, :, w], w), s=s_abp if i else None)
                elif kind == "wk_a":
                    c = step[1]
                    t0, w, _, _ = wk(c, 0)
                    nl = NLEV[c] + 1
                    dve.wait_ge(s_pab, c + 1)
                    if c:
                        dve.wait_ge(s_ps, 2 * c)
                    b2 = bank(2).rearrange("t (p a k) -> t p a k", p=NP, a=2)
                    b3 = bank(3).rearrange("t (p a k) -> t p a k", p=NP, a=2)
                    lm = cc("lev", 6, C)
                    for l in range(nl):
                        tt(lev[:, l, :, 0:w], b2[:, :, 0, 0:w], pairs(lm[:, l, 0:w]))
                    eye = pairs(cc("eye")[:, 0:w])
                    tt(tp[:, 1, :, 0:w], lev[:, 0, :, 0:w], eye, ALU.add, s=s_tri)
                    tt(tp[:, 0, :, 0:w], bank(4, 256).rearrange("t (p k) -> t p k", p=NP)[:, :, 0:w],
                       pairs(cc("lev0")[:, 0:w]))
                    tt(tp[:, 0, :, 0:w], tp[:, 0, :, 0:w], eye, ALU.add, s=s_tri)
                    ai = cc("ai", 2, C)
                    tt(br[:, :, 0:w], b2[:, :, 1, 0:w], pairs(ai[:, 1, 0:w]), s=s_tri)
                    tt(kq[:, :, :, 0:w], b3[:, :, :, 0:w], pairs(ai[:, :, 0:w]), s=s_tri)
                elif kind == "wk_t":
                    _, c, b = step
                    l = LEVELS.index(b)
                    _, w, _, _ = wk(c, 0)
                    dve.wait_ge(s_pr, LEV0[c] + l)
                    f0 = 0 if 2 * b < w else 1
                    ps = bank(5).rearrange("t (a p k) -> t a p k", a=2, p=NP)
                    tt(tp[:, f0:2, :, 0:w], ps[:, f0:2, :, 0:w], tp[:, f0:2, :, 0:w], ALU.add, s=s_tt)
                elif kind == "wk_s":
                    c = step[1]
                    q = c % 2
                    _, w, _, _ = wk(c, 0)
                    tt(stp, st[:, q], bc(ep[:, q, :, w], C))
                    dve.wait_ge(s_ps, 2 * c + 1)
                    tt(st[:, 1 - q], bank(7, 256).rearrange("t (p k) -> t p k", p=NP), stp, ALU.add, s=s_st)
                elif kind == "j_bb":
                    _, m, hf = step
                    job_read(dve, ("j_proj", GB0 + m, hf))
                    job_done(dve, step)
                    tt(merged[:, m, cols(hf)], job_ps(step), merged[:, m, cols(hf)], s=free)
                elif kind == "smp":
                    def tok_bc(a):
                        return bc(a[:, :, TP:T], 64)

                    eye = cc("eye").unsqueeze(1).unsqueeze(1).broadcast_to([P, NP, NB, 64])
                    ps = psum[:, 1024:3072].rearrange("k (p b v) -> k p b v", p=NP, b=NB)
                    if step[1] == 0:
                        dve.wait_ge(s_sld, 16)
                        dve.wait_ge(s_sw, 1)
                        tt(t1, ws, tok_bc(kk_f), s=s_smt)
                        tt(t2, eye, tok_bc(v_f), s=s_smt)
                        tt(ws, ws, bc(wsmp, 64))
                        dve.wait_ge(s_smp, 1)
                        tt(t1, ps, tok_bc(b_f), s=s_smr)
                        tt(ws, ws, t1, ALU.subtract)
                        dve.wait_ge(s_smp, 2)
                        tt(t1, ps, tok_bc(k_f), s=s_smr)
                        tt(ws, ws, t1, ALU.add, s=s_ws)
                    else:
                        tt(t1, ws, tok_bc(r_f), s=s_smt)
                        dve.wait_ge(s_smp, 3)
                        tt(t2, ps, eye)
                        run(v.tensor_reduce(ly[:, :, TP:T], t2, AX.X, ALU.add), s_y)
                        dve.wait_ge(s_y, NCH + 1)
                elif kind == "j_mean":
                    _, p, hf = step
                    job_done(dve, step)
                    stt(ly[:, p, cols(hf)], job_ps(step), -1.0 / 64, ly[:, p, cols(hf)], ALU.mult, ALU.add, s=free)
                    if hf:
                        for q in range(2):
                            job_read(dve, ("j_mean", p, q))
                        tt(tmp[:, p, :], ly[:, p, :], ly[:, p, :], s=s_vsd)
                elif kind == "j_var" and step[2]:
                    p = step[1]
                    for hf in range(2):
                        job_read(dve, ("j_var", p, hf))
                    run(v.reciprocal(tmp[:, p, :], tmp[:, p, :]))
                    stt(ly[:, p, :], ly[:, p, :], vv("lnw", p), tmp[:, p, :], ALU.mult, ALU.mult)
                    stt(ly[:, p, :], ly[:, p, :], vv("lnb", p), bon[:, p, :], ALU.add, ALU.add)
                    tt(ly[:, p, :], ly[:, p, :], g_f[:, p, :], s=s_ya)
                elif kind == "j_ba":
                    _, m, hf = step
                    job_done(dve, step)
                    if hf == 0:
                        for q in range(2):
                            job_read(dve, ("j_proj", GA0 + m, q))
                            job_read(dve, ("j_bb", m, q))
                    tt(tmp[:, hf, 0:HT], job_ps(step), sga[:, m, cols(hf)], s=free)
                    job_read(dve, step)
                    tt(merged[:, m, cols(hf)], merged[:, m, cols(hf)], tmp[:, hf, 0:HT], ALU.add,
                       s=s_mg if hf else None)
                elif kind == "j_out":
                    _, m, hf = step
                    dve.wait_ge(s_xr, 16)
                    job_done(dve, step)
                    tt(u[:, m, cols(hf)], job_ps(step), u[:, m, cols(hf)], ALU.add, s=free)


        mixer.__exit__(None, None, None)

        top[0] = u_end
        NWE = 4
        we = at(NWE * 6144, NWE, 6144)
        w_gu = we[:, :, 0:4096].rearrange("p s (k f) -> p s k f", k=KD)
        w_dn = we[:, :, 4096:6144].rearrange("p s (f d) -> p s f d", f=2)
        x2t = at(TT * D, TT, D)
        ug0 = top[0]
        ug = at(2 * D, 2, D)
        ue = at(2 * D, 2, KD, P)
        sig = at(FF)
        hh = at(FF)
        hht = at(2 * P, 2, P)
        yo = at(2 * D, 2, D)
        yg = at(5 * D, 5, D, start=ug0)
        g_row = at(2 * D, 2, D)
        top[0] = ug0
        wr = at(KD * 20, KD, 20)
        logt = at(T)
        bias = at(20)
        lg = at(TT * 20, TT, 20)
        NS = TT * (1 + NG)
        ll = at(NS * 4, NS, 4)
        gt = at(NS * 16, NS, 4, 4)
        eq = at(NS * 16, NS, 4, 4)
        rank = at(NS * 4, NS, 4)
        mx = at(NS)
        ex = at(NS * 4, NS, 4)
        sel = at(NS * 4, NS, 4)
        sm = at(NS)
        ga = at(TT * 4, TT, 4)
        gw = at(TT * 4, TT, 4)
        f1 = at(TT * NE, TT, NE)
        f2 = at(TT * NE, TT, NE)
        wts = at(TT * NE, TT, NE)
        dest = at(TT * NE, TT, NE)
        tq = at(TT * NE, TT, NE)
        ssq = at(TT)
        rstd = at(TT)
        cnt = at(8)
        zero = E(nc.sbuf_tensor("zero", [P, ROUNDS * NE], I32))
        u2b = at(2 * D, 2, D)
        junk = yo[:, 0, :]
        assert top[0] <= ug0 + 4 * D + 3 * FF, top[0] - ug0
        oneb = E(nc.sbuf_tensor("oneb", [P, P], BF16))
        trib = E(nc.sbuf_tensor("trib", [P, P], BF16))
        selb = E(nc.sbuf_tensor("selb", [P, TT, NE], BF16))
        token = E(nc.sbuf_tensor("token", [P, TT], I32))
        d_i = E(nc.sbuf_tensor("d_i", [P, 2, TT], I32))
        c_w = E(nc.sbuf_tensor("c_w", [P, 2, TT], F32))
        d_f = E(nc.sbuf_tensor("d_f", [P, 2, TT], F32))
        in_r = E(nc.sbuf_tensor("in_r", [P, 2, TT], F32))
        cw_r = E(nc.sbuf_tensor("cw_r", [P, 2, TT], F32))
        dcl = E(nc.sbuf_tensor("dcl", [P, 2, TT], F32))
        n_rounds = E(nc.sbuf_tensor("n_rounds", [P, 1], I32))
        ids = E(nc.sbuf_tensor("ids", [P, NE], I32))
        eps2 = E(nc.sbuf_tensor("eps2", [P, 1], F32))

        u2_dram = nc.dram_tensor("u2_rows", [T, D], F32, kind="Internal").ap()
        id_dram = nc.dram_tensor("id_list", [ROUNDS * ROWS, 1], I32, kind="Internal").ap()
        y_dram = nc.dram_tensor("y_rows", [ROWS, D], F32, kind="Internal").ap()
        id_rows = id_dram.rearrange("(r e) o -> r (e o)", e=NE)
        y_view = y_dram.rearrange("(p e) d -> p e d", e=NE)

        d_ld = sem("d_ld")
        s_we = [sem(f"s_we{i}") for i in range(NWE)]
        d_wr = sem("d_wr")
        d_lt = sem("d_lt")
        d_ltc = sem("d_ltc")
        d_lg = sem("d_lg")
        d_x = sem("d_x")
        d_xc = sem("d_xc")
        d_act = sem("d_act")
        d_dve = sem("d_dve")
        d_ss = sem("d_ss")
        d_rt = sem("d_rt")
        d_ll = sem("d_ll")
        d_ex = sem("d_ex")
        d_u2 = sem("d_u2")
        d_u2w = [sem(f"d_u2w{i}") for i in range(2)]
        d_sel = sem("d_sel")
        d_pos = sem("d_pos")
        d_ids = sem("d_ids")
        d_z = sem("d_z")
        d_zw = sem("d_zw")
        d_sc = sem("d_sc")
        d_tok = sem("d_tok")
        d_n = sem("d_n")

        def rows_of(t):
            return LASTT if t == TT - 1 else P

        def load_expert(eng, e):
            eng.dma_start(we[:, e % NWE, 0:4096], I["w_gu"][e]).then_inc(s_we[e % NWE], 16)
            eng.dma_start(we[:, e % NWE, 4096:6144], I["w_dn"][e]).then_inc(s_we[e % NWE], 16)

        with nc.Block() as block:
            @block.sync
            def _(sp):
                for dst, src in ((wr, I["w_r"]), (bias, I["b_r"]), (g_row[:, 0, :], I["g2row"]),
                                 (g_row[:, 1, :], I["gfrow"])):
                    sp.dma_start(dst, src).then_inc(d_ld, 16)
                sp.wait_ge(d_z, 1)
                sp.dma_start(id_dram.rearrange("(p c) o -> p (c o)", p=P), zero[:, :]).then_inc(d_zw, 16)
                for e in range(NWE):
                    load_expert(sp, e)
                for t in range(TT):
                    sp.wait_ge(d_u2, t + 1)
                    sp.dma_start(u2_dram[t * P:t * P + rows_of(t), :], u2b[0:rows_of(t), t % 2, :])\
                        .then_inc(d_u2w[t % 2], 16)
                sp.wait_ge(d_u2w[0], 16 * 3)
                sp.wait_ge(d_u2w[1], 16 * 2)

            @block.gpsimd
            def _(pool):
                nc.gpsimd.memset(zero[:, :], 0).then_inc(d_z, 1)
                nc.gpsimd.iota(token[:, :], [[P, TT]], base=0, channel_multiplier=1).then_inc(d_tok, 1)
                pool.wait_ge(d_tok, 1)
                pool.wait_ge(d_zw, 16)
                pool.wait_ge(d_ids, 1)
                for i in range(2):
                    for t in range(TT):
                        n = rows_of(t)
                        pool.indirect_dma_start(id_dram, bass.IndirectOffsetOnAxis(ap=d_i[0:n, i, t:t + 1], axis=0),
                                                token[0:n, t:t + 1], None).then_inc(d_sc, 16)
                pool.wait_ge(d_sc, 16 * 2 * TT)

            @block.tensor
            def _(pe):
                pe.wait_ge(d_wr, 1)
                for hf in range(2):
                    for k in range(KD):
                        last = nc.tensor.matmul(bank(hf, HT, 20), wr[:, k, :], u[:, k, cols(hf)], start=(k == 0),
                                                stop=(k == KD - 1))
                last.then_inc(d_lt, 1)
                for t in range(TT):
                    n = rows_of(t)
                    if t >= 2:
                        pe.wait_ge(d_xc, t - 1)
                    for k in range(KD):
                        last = nc.tensor.transpose(psum[0:n, 2048 + 1024 * (t % 2) + P * k:2048 + 1024 * (t % 2) + P * (k + 1)],
                                                   u[:, k, t * P:t * P + n], ident)
                    last.then_inc(d_x, 1)
                    if t == 1:
                        pe.wait_ge(d_ltc, 1)
                        for q in range(TT):
                            m = rows_of(q)
                            last = nc.tensor.transpose(bank(2, 512, m)[:, 20 * q:20 * q + 20],
                                                       logt[0:20, q * P:q * P + m], ident[0:20, 0:20])
                        last.then_inc(d_lg, 1)
                pe.wait_ge(d_sel, 1)
                for t in range(TT + 1):
                    o = bank(3)[:, NE * t:NE * t + NE]
                    for q in range(min(t, TT - 1) + 1 if t < TT else TT):
                        last = nc.tensor.matmul(o, trib[:, :] if q == t else oneb[:, :], selb[:, q, :], start=(q == 0),
                                                stop=(q == min(t, TT - 1)))
                last.then_inc(d_pos, 1)

            @block.scalar
            def _(act):
                a = nc.scalar.activation
                act.wait_ge(d_lt, 1)
                a(logt[0:20, :].rearrange("p (a c) -> p a c", a=2),
                  psum[0:20, 0:1024].rearrange("p (a c) -> p a c", a=2)[:, :, 0:HT], ACT.Copy).then_inc(d_ltc, 1)
                for t in range(TT):
                    n = rows_of(t)
                    act.wait_ge(d_x, t + 1)
                    a(x2t[0:n, t, :], psum[0:n, 2048 + 1024 * (t % 2):3072 + 1024 * (t % 2)], ACT.Copy).then_inc(d_xc, 1)
                    act.wait_ge(d_xc, t + 1)
                    if t:
                        act.wait_ge(d_act, t)
                    else:
                        act.wait_ge(d_dve, 2)
                    a(junk[0:n], x2t[0:n, t, :], ACT.Square, accum_out=ssq[0:n, t:t + 1]).then_inc(d_act, 1)
                act.wait_ge(d_act, TT)
                a(rstd, ssq, ACT.Sqrt, scale=1.0 / D, bias=eps2[:, :]).then_inc(d_rt, 1)
                act.wait_ge(d_ll, 1)
                a(ex, ll, ACT.Exp).then_inc(d_ex, 1)

            @block.vector
            def _(dve):
                v = nc.vector
                own = [0]

                def run(ins, s=None):
                    if s is None:
                        own[0] += 1
                        ins.then_inc(d_dve, 1)
                        dve.wait_ge(d_dve, own[0])
                    else:
                        ins.then_inc(s, 1)
                        dve.wait_ge(s, 1)

                def tt(out, x, y, op=ALU.mult, s=None):
                    run(v.tensor_tensor(out, x, y, op), s)

                run(v.memset(eps2[:, :], EPS))
                run(v.memset(ssq, 1.0))
                run(v.memset(lg, 0.0))
                run(v.tensor_copy(trib[:, :], cc("tri")))
                run(v.tensor_copy(oneb[:, :], ones))
                dve.wait_ge(d_ld, 64)
                o2 = VEC["norm2_g"]
                tt(wr, wr, bc(vec[:, o2:o2 + KD], 20), s=d_wr)
                dve.wait_ge(d_rt, 1)
                run(v.reciprocal(rstd, rstd))
                dve.wait_ge(d_lg, 1)
                for t in range(TT):
                    n = rows_of(t)
                    run(v.scalar_tensor_tensor(lg[0:n, t, :], bank(2, 512, n)[:, 20 * t:20 * t + 20], rstd[0:n, t:t + 1],
                                               bias[0:n], ALU.mult, ALU.add))
                run(v.tensor_copy(ll[:, 0:TT, :], lg[:, :, 0:4]))
                run(v.tensor_copy(ll[:, TT:NS, :].rearrange("p (t g) e -> p t (g e)", t=TT), lg[:, :, 4:20]))
                me = bc(ll, 4)
                other = ll.unsqueeze(2).broadcast_to([P, NS, 4, 4])
                tt(gt, other, me, ALU.is_gt)
                tt(eq, other, me, ALU.is_equal)
                tt(eq, eq, cc("tie", 4, 4).unsqueeze(1).broadcast_to([P, NS, 4, 4]))
                tt(gt, gt, eq, ALU.add)
                run(v.tensor_reduce(rank, gt, AX.X, ALU.add))
                run(v.tensor_reduce(mx, ll, AX.X, ALU.max))
                tt(ll, ll, bc(mx, 4), ALU.subtract, s=d_ll)
                dve.wait_ge(d_ex, 1)
                run(v.tensor_reduce(sm[:, 0:TT], ex[:, 0:TT, :], AX.X, ALU.add))
                run(v.tensor_scalar(ga, rank[:, 0:TT, :], 0.5, None, ALU.is_lt))
                tt(ga, ga, bc(cc("valid"), 4))
                run(v.tensor_scalar(sel[:, TT:NS, :], rank[:, TT:NS, :], 1.5, None, ALU.is_lt))
                tt(ex[:, TT:NS, :], ex[:, TT:NS, :], sel[:, TT:NS, :])
                run(v.tensor_reduce(sm[:, TT:NS], ex[:, TT:NS, :], AX.X, ALU.add))
                run(v.reciprocal(sm, sm))
                tt(gw, ga, bc(sm[:, 0:TT], 4))
                tt(ex[:, TT:NS, :], ex[:, TT:NS, :], bc(sm[:, TT:NS], 4))
                tt(wts.rearrange("p t (g e) -> p (t g) e", g=NG), ex[:, TT:NS, :],
                   bc(gw.rearrange("p t g -> p (t g)"), 4))
                gax = bc(ga.rearrange("p t g -> p (t g)"), 4)
                for f, lo in ((f1, 0.0), (f2, 1.0)):
                    fv = f.rearrange("p t (g e) -> p (t g) e", g=NG)
                    run(v.tensor_scalar(fv, rank[:, TT:NS, :], lo, None, ALU.is_equal))
                    tt(fv, fv, gax)
                tt(selb[:, :, :], f1, f2, ALU.add, s=d_sel)
                for i, f in enumerate((f1, f2)):
                    tt(tq, wts, f)
                    run(v.tensor_reduce(c_w[:, i, :], tq, AX.X, ALU.add))
                dve.wait_ge(d_pos, 1)
                run(v.scalar_tensor_tensor(dest, bank(3, NE * TT).rearrange("p (t e) -> p t e", t=TT), float(NE),
                                           cc("expert").unsqueeze(1).broadcast_to([P, TT, NE]), ALU.mult, ALU.add))
                for i, f in enumerate((f1, f2)):
                    tt(tq, dest, f)
                    run(v.tensor_reduce(d_f[:, i, :], tq, AX.X, ALU.add))
                run(v.tensor_copy(d_i[:, :, :], d_f[:, :, :]), d_ids)
                run(v.tensor_reduce(cnt[:, 0:1], bank(3)[:, NE * TT:NE * TT + NE], AX.X, ALU.max))
                for i in range(1, ROUNDS):
                    run(v.tensor_scalar(cnt[:, i:i + 1], cnt[:, 0:1], float(SLOTS * i), None, ALU.is_gt))
                run(v.tensor_reduce(cnt[:, 6:7], cnt[:, 1:ROUNDS], AX.X, ALU.add))
                run(v.tensor_scalar(n_rounds[:, :], cnt[:, 6:7], 1.0, None, ALU.add), d_n)
                for t in range(TT):
                    n = rows_of(t)
                    if t >= 2:
                        dve.wait_ge(d_u2w[t % 2], 16 * (t // 2))
                    ins = v.scalar_tensor_tensor(u2b[0:n, t % 2, :], x2t[0:n, t, :], rstd[0:n, t:t + 1],
                                                 g_row[0:n, 0, :], ALU.mult, ALU.mult)
                    ins.then_inc(d_u2, 1)

        q_id = sem("q_id")
        q_g = [sem(f"q_g{i}") for i in range(2)]
        q_tr = sem("q_tr")
        q_ue = sem("q_ue")
        q_gu = sem("q_gu")
        q_sig = sem("q_sig")
        q_h1 = sem("q_h1")
        q_h = sem("q_h")
        q_ht = sem("q_ht")
        q_hte = sem("q_hte")
        q_dn = sem("q_dn")
        q_yo = sem("q_yo")
        q_yd = [sem(f"q_yd{i}") for i in range(2)]
        q_ix = sem("q_ix")
        q_yg = [sem(f"q_yg{i}") for i in range(5)]
        q_cb = sem("q_cb")
        q_dv = sem("q_dv")

        rounds = nc.values_load(n_rounds[0:1, 0:1], min_val=1, max_val=ROUNDS)
        with nc.Fori(0, rounds) as r:
            def at_least(eng, s, per, n):
                assert n > 0
                eng.wait_ge(s, r * per + n)

            with nc.Block() as block:
                @block.sync
                def _(sp):
                    sp.dma_start(ids[:, :], id_rows[bass.ds(r * P, P), :]).then_inc(q_id, 16)
                    for e in range(NWE, NE):
                        at_least(sp, q_dn, NE, e - NWE + 1)
                        load_expert(sp, e)
                    at_least(sp, q_dn, NE, NE)
                    sp.nop(nofuse=True)
                    with sp.If(r + 1 < rounds):
                        for e in range(NWE):
                            load_expert(sp, e)

                @block.gpsimd
                def _(pool):
                    def then(s, per, n):
                        at_least(pool, s, per, n)
                        pool.nop(nofuse=True)

                    then(q_id, 16, 16)
                    for e in range(NE):
                        if e >= 2:
                            then(q_tr, NE, e - 1)
                        pool.indirect_dma_start(ug[:, e % 2, :], None, u2_dram,
                                                bass.IndirectOffsetOnAxis(ap=ids[:, e:e + 1], axis=0))\
                            .then_inc(q_g[e % 2], 16)
                    then(q_ix, 1, 1)
                    for i in range(2):
                        then(q_yd[i], 8 * 16, 8 * 16)
                    for j in range(2 * TT):
                        t, i = j // 2, j % 2
                        n = rows_of(t)
                        if j >= 5:
                            then(q_cb, 2 * TT, j - 4)
                        pool.indirect_dma_start(yg[0:n, j % 5, :], None, y_dram,
                                                bass.IndirectOffsetOnAxis(ap=d_i[0:n, i, t:t + 1], axis=0))\
                            .then_inc(q_yg[j % 5], 16)

                @block.tensor
                def _(pe):
                    mm = nc.tensor.matmul
                    for i in range(NE + 1):
                        if i < NE:
                            e = i
                            at_least(pe, q_g[e % 2], 8 * 16, 16 * (e // 2 + 1))
                            if e:
                                at_least(pe, q_ue, NE, e)
                            for k in range(KD):
                                last = nc.tensor.transpose(psum[:, P * k:P * (k + 1)], ug[:, e % 2, P * k:P * (k + 1)], ident)
                            last.then_inc(q_tr, 1)
                            at_least(pe, q_ue, NE, e + 1)
                            at_least(pe, s_we[e % NWE], 4 * 32, 32 * (e // NWE + 1))
                            if e >= 2:
                                at_least(pe, q_h, NE, e - 1)
                            for k in range(KD):
                                last = mm(bank(2 + e % 2), ue[:, e % 2, k, :], w_gu[:, e % NWE, k, :], start=(k == 0),
                                          stop=(k == KD - 1))
                            last.then_inc(q_gu, 1)
                        if i:
                            e = i - 1
                            at_least(pe, q_h, NE, e + 1)
                            if e:
                                at_least(pe, q_hte, NE, e)
                            for f in range(2):
                                last = nc.tensor.transpose(bank(4)[:, P * f:P * f + P], hh[:, P * f:P * f + P], ident)
                            last.then_inc(q_ht, 1)
                            at_least(pe, q_hte, NE, e + 1)
                            if e:
                                at_least(pe, q_yo, NE, e)
                            for f in range(2):
                                for q in range(2):
                                    last = mm(bank(6 + q), hht[:, f, :], w_dn[:, e % NWE, f, 512 * q:512 * q + 512],
                                              start=(f == 0), stop=(f == 1))
                            last.then_inc(q_dn, 1)

                @block.scalar
                def _(act):
                    a = nc.scalar.activation
                    for i in range(NE + 1):
                        if i < NE:
                            e = i
                            at_least(act, q_tr, NE, e + 1)
                            a(ue[:, e % 2].rearrange("p k t -> p (k t)"), psum[:, 0:1024], ACT.Copy).then_inc(q_ue, 1)
                        if i:
                            e = i - 1
                            at_least(act, q_ht, NE, e + 1)
                            a(hht.rearrange("p f t -> p (f t)"), bank(4, 256), ACT.Copy).then_inc(q_hte, 1)
                        if i < NE:
                            e = i
                            at_least(act, q_gu, NE, e + 1)
                            if e:
                                at_least(act, q_h, NE, e)
                            a(sig, bank(2 + e % 2, FF), ACT.Sigmoid).then_inc(q_sig, 1)
                        if i:
                            e = i - 1
                            at_least(act, q_yo, NE, e + 1)
                            act.dma_start(y_view[:, e, :], yo[:, e % 2, :]).then_inc(q_yd[e % 2], 16)

                @block.vector
                def _(dve):
                    v = nc.vector

                    def tt(out, x, y, op, s):
                        v.tensor_tensor(out, x, y, op).then_inc(s, 1)

                    v.tensor_scalar(in_r[:, :, :], d_f[:, :, :], 0.0, None, ALU.is_ge).then_inc(q_dv, 1)
                    at_least(dve, q_dv, 6, 1)
                    v.tensor_tensor(cw_r[:, :, :], c_w[:, :, :], in_r[:, :, :], ALU.mult).then_inc(q_dv, 1)
                    at_least(dve, q_dv, 6, 2)
                    v.tensor_scalar(in_r[:, :, :], d_f[:, :, :], float(ROWS), None, ALU.is_lt).then_inc(q_dv, 1)
                    at_least(dve, q_dv, 6, 3)
                    v.tensor_tensor(cw_r[:, :, :], cw_r[:, :, :], in_r[:, :, :], ALU.mult).then_inc(q_dv, 1)
                    at_least(dve, q_dv, 6, 4)
                    v.tensor_scalar(dcl[:, :, :], d_f[:, :, :], 0.0, float(ROWS - 1), ALU.max, ALU.min)\
                        .then_inc(q_dv, 1)
                    at_least(dve, q_dv, 6, 5)
                    v.tensor_copy(d_i[:, :, :], dcl[:, :, :]).then_inc(q_ix, 1)
                    v.tensor_scalar(d_f[:, :, :], d_f[:, :, :], -float(ROWS), None, ALU.add).then_inc(q_dv, 1)
                    at_least(dve, q_dv, 6, 6)
                    for i in range(NE + 1):
                        if i < NE:
                            e = i
                            at_least(dve, q_sig, NE, e + 1)
                            if e:
                                at_least(dve, q_ht, NE, e)
                            b = bank(2 + e % 2)
                            tt(hh, b[:, 0:FF], sig, ALU.mult, q_h1)
                            at_least(dve, q_h1, NE, e + 1)
                            tt(hh, b[:, FF:2 * FF], hh, ALU.mult, q_h)
                        if i:
                            e = i - 1
                            at_least(dve, q_dn, NE, e + 1)
                            if e >= 2:
                                at_least(dve, q_yd[e % 2], 8 * 16, 16 * (e // 2))
                            v.tensor_copy(yo[:, e % 2, :], psum[:, 3072:4096]).then_inc(q_yo, 1)
                    for j in range(2 * TT):
                        t, i = j // 2, j % 2
                        n = rows_of(t)
                        at_least(dve, q_yg[j % 5], 32, 16 * (j // 5 + 1))
                        v.scalar_tensor_tensor(x2t[0:n, t, :], yg[0:n, j % 5, :], cw_r[0:n, i, t:t + 1], x2t[0:n, t, :],
                                               ALU.mult, ALU.add).then_inc(q_cb, 1)
                        if j < 2 * TT - 1:
                            at_least(dve, q_cb, 2 * TT, j + 1)

        z_ss = sem("z_ss")
        z_rt = sem("z_rt")
        z_rc = sem("z_rc")
        z_y = sem("z_y")
        z_out = sem("z_out")
        fs = E(nc.sbuf_tensor("fs", [P, 2 * TT], F32))
        with nc.Block() as block:
            @block.scalar
            def _(act):
                for t in range(TT):
                    n = rows_of(t)
                    nc.scalar.activation(ug[0:n, 0, :], x2t[0:n, t, :], ACT.Square, accum_out=fs[0:n, t:t + 1])\
                        .then_inc(z_ss, 1)
                    act.wait_ge(z_ss, t + 1)
                    nc.scalar.activation(fs[0:n, TT + t:TT + t + 1], fs[0:n, t:t + 1], ACT.Sqrt, scale=1.0 / D,
                                         bias=eps2[0:n, :]).then_inc(z_rt, 1)

            @block.vector
            def _(dve):
                v = nc.vector
                for t in range(TT):
                    n = rows_of(t)
                    dve.wait_ge(z_rt, t + 1)
                    v.reciprocal(fs[0:n, TT + t:TT + t + 1], fs[0:n, TT + t:TT + t + 1]).then_inc(z_rc, 1)
                    dve.wait_ge(z_rc, t + 1)
                    v.scalar_tensor_tensor(x2t[0:n, t, :], x2t[0:n, t, :], fs[0:n, TT + t:TT + t + 1], g_row[0:n, 1, :],
                                           ALU.mult, ALU.mult).then_inc(z_y, 1)

            @block.sync
            def _(sp):
                for t in range(TT):
                    n = rows_of(t)
                    sp.wait_ge(z_y, t + 1)
                    sp.dma_start(O["y"][t * P:t * P + n, :], x2t[0:n, t, :]).then_inc(z_out, 16)
                sp.wait_ge(z_out, 16 * TT)


def host_inputs(x):
    c = np.ascontiguousarray
    out = {}
    xs = np.concatenate([x["meta_tokens"], x["x_prompt"][0], x["x_sample"][:, 0]], 0)
    out["x"] = c(xs.T.reshape(KD, P, T).transpose(1, 0, 2))
    out["con"] = constants()
    vec = np.concatenate([x[n][0].reshape(-1, P) for n in ("norm1_g", "shift_mu", "decay_w0", "aaa_a0", "k_k", "k_a", "r_k", "lnx_w", "lnx_b", "norm2_g")], 0)
    out["vec"] = c(vec.T)
    out["sh0"] = c(x["state_shift"][0].reshape(8, 14, P).transpose(2, 1, 0))
    out["up_wa"] = c(np.concatenate([x["decay_up"][0], x["aaa_up"][0]], 0))
    out["up_g"] = c(x["gate_up"][0])
    def tiles(w):
        return c(w.reshape(w.shape[0] // P, P, w.shape[1] // P, P).transpose(2, 1, 0, 3))
    out["w_in"] = tiles(x["w_in"][0])
    out["w_bb"] = tiles(x["w_branch_b"][0])
    out["w_ba"] = tiles(x["w_branch_a"][0])
    out["w_out"] = tiles(x["w_out"][0])
    out["wkv0"] = c(x["state_wkv"][0].reshape(8, 4, 2, 64, 64).transpose(2, 4, 1, 0, 3).reshape(P, 4, 8, 64))
    out["rets0"] = c(x["state_ret"][0].transpose(2, 1, 0, 3))
    w = np.concatenate([x["expert_w_gate"][0], x["expert_w_up"][0]], 2)
    out["w_gu"] = c(w.reshape(16, KD, P, 512).transpose(0, 2, 1, 3).reshape(16, P, 4096))
    out["w_dn"] = c(x["expert_w_down"][0].reshape(16, 2, P, D).transpose(0, 2, 1, 3).reshape(16, P, 2048))
    out["w_r"] = c(np.concatenate([x["router_group_w"][0], x["router_expert_w"][0]], 1).reshape(KD, P, 20).transpose(1, 0, 2))
    out["b_r"] = c(np.broadcast_to(np.concatenate([x["router_group_b"][0], x["router_expert_b"][0]]), (P, 20)))
    out["g2row"] = c(np.broadcast_to(x["norm2_g"][0], (P, D)))
    out["gfrow"] = c(np.broadcast_to(x["final_norm_g"], (P, D)))
    return out

def host_outputs(o):
    r = {}
    r["wkvp"] = o["wkvp"].reshape(2, 64, 4, 64).transpose(2, 0, 3, 1).reshape(1, 1, 8, 64, 64)
    r["wkvs"] = o["wkvs"].reshape(2, 64, 4, 8, 64).transpose(3, 2, 0, 4, 1).reshape(1, 8, 8, 64, 64)
    sh = o["shift"].transpose(2, 1, 0).reshape(9, 14 * P)
    r["shiftp"], r["shifts"] = sh[0].reshape(1, 1, -1), sh[1:].reshape(1, 8, -1)
    r["retp"] = o["retp"].transpose(1, 0, 2)[None, None]
    r["rets"] = o["rets"].transpose(2, 1, 0, 3)[None]
    return r


OUTS = {"y": (T, D), "wkvp": (P, NP, 64), "shift": (P, SHIFT_TILES, 9), "retp": (P, RH, P),
        "wkvs": (P, NP, NB, 64), "rets": (P, RH, NB, P)}


def kernel(**inputs):
    import concourse.bacc as bacc
    from concourse.bass_utils import run_bass_kernel_spmd

    nc = bacc.Bacc("TRN2", target_bir_lowering=False, num_devices=1)
    arrays = host_inputs({n: np.asarray(a) for n, a in inputs.items()})
    ins = {n: nc.dram_tensor(f"in_{n}", a.shape, F32, kind="ExternalInput").ap() for n, a in arrays.items()}
    outs = {n: nc.dram_tensor(f"out_{n}", s, F32, kind="ExternalOutput").ap() for n, s in OUTS.items()}
    hybrid_step(nc, ins, outs)
    r = run_bass_kernel_spmd(nc, [{f"in_{n}": a for n, a in arrays.items()}], core_ids=[0]).results[0]
    o = host_outputs({n: r[f"out_{n}"] for n in OUTS})
    y = r["out_y"]
    return (y[None, META:TP], y[TP:T, None], o["wkvp"], o["shiftp"], o["retp"], o["wkvs"], o["shifts"], o["rets"])
```

```python
import math
from contextlib import ExitStack

import numpy as np
import concourse.bass as bass
from concourse import mybir

F32 = mybir.dt.float32
I32 = mybir.dt.int32
BF16 = mybir.dt.bfloat16
ALU = mybir.AluOpType
ACT = mybir.ActivationFunctionType
AX = mybir.AxisListType

P = 128
D = 1024
KD = D // P
META, SEQ, NB = 16, 512, 8
TP = META + SEQ
T = TP + NB
HT = T // 2
PAST = 4096
NP = 4
RH = 4
C = 64
CHUNKS = [(c * C, min(C, TP - c * C)) for c in range((TP + C - 1) // C)]
LEVELS = [1, 2, 4, 8, 16, 32]
DECAY = math.exp(-0.5)
EPS = 1e-6
LNX_EPS = 64e-5
NE, NG, EPG, FF = 16, 4, 4, 256
SLOTS = P
TT = (T + P - 1) // P
LASTT = T - (TT - 1) * P
ROUNDS = (T + SLOTS - 1) // SLOTS
ROWS = NE * SLOTS
SHIFT_TILES = 14
RET0, GA0, GB0 = 14, 30, 38

VEC = {}
_n = 0
for _name, _w in [("norm1_g", KD), ("mu", SHIFT_TILES), ("w0", NP), ("a0", NP), ("kk", NP), ("ka", NP),
                  ("rk", NP), ("lnw", NP), ("lnb", NP), ("norm2_g", KD)]:
    VEC[_name] = _n
    _n += _w
NVEC = _n

CON = {}
_n = 0
for _name, _w in [("ident", P), ("bones", P), ("ones", P), ("tri", P), ("reset", TP), ("lev", len(LEVELS) * C),
                  ("lev0t", C), ("eye", C), ("ai", 2 * C), ("tie", 16), ("expert", NE),
                  ("valid", TT),
                  ("perm", P), ("smask", NB), ("cos", T), ("sin", T), ("dec", RH * TP), ("dend", TT * RH)]:
    CON[_name] = (_n, _w)
    _n += _w
NCON = _n
NKEEP = CON["perm"][0]


def constants():
    t = np.zeros((P, NCON), np.float32)

    def put(name, a):
        o, w = CON[name]
        a = np.asarray(a, np.float32).reshape(a.shape[0], -1)
        t[:a.shape[0], o:o + w] = a

    p = np.arange(P)
    put("ident", np.eye(P))
    put("bones", (p[:, None] // 64 == p[None] // 64))
    put("ones", np.ones((P, P)))
    perm = np.zeros((P, P))
    for i in range(P // 2):
        perm[2 * i + 1, 2 * i] = -1
        perm[2 * i, 2 * i + 1] = 1
    put("perm", perm)
    put("tri", p[:, None] < p[None])
    pos = np.concatenate([np.arange(TP), np.full(NB, PAST)]).astype(np.float32)
    inv = np.float32(10000.0) ** (-np.arange(64, dtype=np.float32) / np.float32(64))
    ang = (pos[None] * inv[p // 2][:, None]).astype(np.float32)
    put("cos", np.cos(ang))
    put("sin", np.sin(ang))
    lg = np.log(1.0 - 2.0 ** (-5.0 - np.arange(RH)))
    diff = np.arange(TP)[None] - p[:, None]
    put("dec", np.stack([np.where(diff >= 0, np.exp(np.maximum(diff, 0) * g), 0) for g in lg], 1))
    tok = np.arange(TT)[None, :] * P + p[:, None]
    put("dend", np.stack([np.where(tok < TP, np.exp(np.maximum(TP - 1 - tok, 0) * g), 0) for g in lg], 2))
    put("reset", np.broadcast_to(np.arange(TP) % C != 0, (P, TP)))
    row, col = p % 64, np.arange(C)

    def half(b, r, c):
        return (r // (2 * b) == c // (2 * b)) & (r // b % 2 == 1) & (c // b % 2 == 0)

    put("lev", np.stack([half(b, row[:, None], col[None]) for b in LEVELS], 1))
    put("lev0t", half(1, col[None], row[:, None]))
    put("eye", row[:, None] == col[None])
    strict, incl = row[:, None] < col[None], row[:, None] <= col[None]
    put("ai", np.stack([strict, incl], 1))
    put("smask", (p[:, None] - META == np.arange(NB)[None]))
    put("tie", np.broadcast_to((np.arange(4)[None] < np.arange(4)[:, None]).reshape(-1), (P, 16)))
    put("valid", tok < T)
    put("expert", np.broadcast_to(np.arange(NE), (P, NE)))
    return t


GAMMA = [float(1.0 - 2.0 ** (-5.0 - h)) for h in range(RH)]

RB = []
for _h in range(RH):
    for _r in range(2):
        _js = [j for j in range(TT) if j * P < (_r + 1) * (TP // 2)]
        for _j in _js:
            _i0 = max(_r * (TP // 2), _j * P)
            RB.append((_h, _r, _j, _i0, (_r + 1) * (TP // 2), _j == _js[0], _j == _js[-1]))


PARTS = {"j_proj": 4, "j_bb": 2}


def order():
    s = [("j_norm", 0, 0), ("j_norm", 0, 1)]

    def proj(m):
        return [("j_proj", m, 0), ("j_proj", m, 1)]

    for j in range(12):
        s += proj(RET0 + j)
        if 1 <= j <= 8:
            s += [("j_rope", j - 1, 0), ("j_rope", j - 1, 1)]
    s += [("j_vt", t) for t in range(TT)] + [("j_kt", t) for t in range(TT)]
    for h in range(RH):
        s += [("rs_v", h), ("j_proj", RET0 + 12 + h, 0), ("rs_a", h), ("j_proj", RET0 + 12 + h, 1), ("rs_b", h)]
    s += [("j_ros", h) for h in range(RH)] + [("j_rst", h) for h in range(RH)]
    for n in range(len(RB)):
        s.append(("j_score", n))
        if n:
            s.append(("att", n - 1))
    s += [("att", len(RB) - 1)] + [("osq", h) for h in range(RH)] + [("phase2",)]
    for n, m in enumerate([12, 13, 4, 5, 6, 7, 0, 1, 2, 3, 8, 9, 10, 11]):
        s += proj(m)
        if n < RH:
            s += [("j_orms", n, 0), ("j_orms", n, 1)]
        if n == 1:
            s += [("lora_in",)]
        if 3 <= n <= 6:
            s += [("j_lora", k, n - 3, hf) for k in ("w", "a") for hf in range(2)]
        if 5 <= n <= 8:
            s += [("kk_in", n - 5)]
        if 6 <= n <= 9:
            s += [("j_kkn", n - 6, 0), ("j_kkn", n - 6, 1)]
        if 7 <= n <= 10:
            s += [("j_lora", "g", n - 7, hf) for hf in range(2)]
        if 8 <= n <= 11:
            s += [("bon_in", n - 8)]
    fill = []

    def parts(st, n):
        return [("pre", st, i) for i in range(n - 1)] + [st]

    for m in range(8):
        for st in proj(GB0 + m):
            fill += parts(st, PARTS["j_proj"])
        for hf in range(2):
            fill += parts(("j_bb", m, hf), PARTS["j_bb"])
    for m in range(8):
        for st in proj(GA0 + m):
            fill += parts(st, PARTS["j_proj"])
    small = []
    budget = [0]

    def take(n=1):
        out = []
        for _ in range(n):
            if fill:
                out.append(fill.pop(0))
            if small and budget[0] and (not fill or fill[0][0] == "pre" and fill[0][2] == 0):
                out.append(small.pop(0))
                budget[0] -= 1
        return out

    def whole():
        out = []
        while fill and not (fill[0][0] == "pre" and fill[0][2] == 0):
            out += take()
        return out

    for p in range(NP):
        s += [("j_bon", p, 0), ("j_bon", p, 1)]
    for p in range(NP):
        small += [("sm_in", p), ("j_sk", p), ("j_sv", p), ("sm_y", p), ("j_sy", p)]
    s += [("wk_prep", 0)] + take(8)
    for c, (_, w) in enumerate(CHUNKS):
        budget[0] = 4 if c else 0
        if c == 6:
            small += [("j_mean", p, 0) for p in range(NP)]
        if c == 7:
            small += [("j_var", p, 0) for p in range(NP)]
        s += [("wk_a", c)] + take(3)
        if c + 1 < len(CHUNKS):
            s += [("wk_prep", c + 1)]
        for b in LEVELS[1:]:
            if b < w:
                s += [("wk_x", c, b)] + take(1) + [("wk_t", c, b)]
                if b == 2:
                    s += [("wk_k", c)]
                s += take(1)
        s += [("wk_r", c)] + take(1) + [("wk_sa", c)] + take(1) + [("wk_s", c)]
        s += take(1)
    s += whole()
    budget[0] = len(small)
    s += small
    small[:] = []
    ba = [("j_ba", m, 0) for m in range(8)]
    for p in range(NP):
        s += [("j_mean", p, 1)] + take(PARTS["j_proj"])
    s += fill
    fill[:] = []
    s += ba[0:4] + [("j_var", p, 1) for p in range(NP)] + ba[4:]
    s += [("j_ba", m, 1) for m in range(8)]
    s += [("j_out", m, 0) for m in range(8)] + [("j_out", m, 1) for m in range(8)]
    return s


STEPS = order()
JOBS = {s: n for n, s in enumerate([s for s in STEPS if s[0].startswith("j_")])}
KINDS = {"j_proj": "in", "j_bb": "bb", "j_ba": "ba", "j_out": "out"}
WTILES = []
for _s in STEPS:
    if _s[0] in ("j_proj", "j_bb") and _s[2] == 0:
        WTILES.append((_s[0], _s[1], (0, 1)))
    elif _s[0] in ("j_ba", "j_out"):
        WTILES.append((_s[0], _s[1], (_s[2],)))
WIDX = {(k, m, h): n for n, (k, m, hs) in enumerate(WTILES) for h in hs}
NW = 3


def bank_of(step):
    return JOBS[step] % 2


def hybrid_step(nc, I, O):
    with ExitStack() as ctx:
        E = ctx.enter_context
        sem_names = set()

        def sem(name):
            assert name not in sem_names
            sem_names.add(name)
            return E(nc.semaphore(name))

        NARENA = 52300
        arena = E(nc.sbuf_tensor("arena", [P, NARENA], F32))
        top = [0]

        def at(n, *dims, start=None):
            if start is None:
                start = top[0]
                top[0] += n
            assert start + n <= NARENA, (start, n)
            a = arena[:, start:start + n]
            if len(dims) == 2:
                return a.rearrange("p (a b) -> p a b", a=dims[0])
            if len(dims) == 3:
                return a.rearrange("p (a b c) -> p a b c", a=dims[0], b=dims[1])
            if len(dims) == 4:
                return a.rearrange("p (a b c d) -> p a b c d", a=dims[0], b=dims[1], c=dims[2])
            return a

        con = at(NKEEP)
        vec = at(NVEC)
        up_wa = at(512)
        up_g = at(512)
        u = at(KD * T, KD, T)
        u_end = top[0]
        wt = at(NW * 1024, NW, 8, P)
        ret_o = at(RH * T, RH, T)
        tmp = at(4 * T, 4, T)
        base = top[0]
        con1 = at(NCON - NKEEP)
        ret = at(16 * T, 16, T)
        v_tok = at(TT * 512, TT, RH, P)
        k_tok = at(TT * 512, TT, RH, P)
        k_smp = at(512, RH, P)
        sc = at(3 * HT, 3, HT)
        vb = at(1024, NB, P)
        s_new = at(RH * 1024, RH, NB, P)
        o_smp = at(512, RH, P)
        o_diag = at(1024, NB, P)
        ret_st = at(512, RH, P)
        top1 = top[0]
        top[0] = base
        r_f = at(NP * T, NP, T)
        k_f = at(NP * T, NP, T)
        v_f = at(NP * T, NP, T)
        wad = at(T)
        gd = at(T)
        ly = at(NP * T, NP, T)
        b_f = at(NP * T, NP, T)
        kk_f = at(NP * T, NP, T)
        g_f = at(NP * T, NP, T)
        bon = at(NP * T, NP, T)
        dif = bon[:, 3, :]
        raw0 = top[0]
        raw = at(2 * (T + 1), 2, T + 1)
        top[0] = raw0
        ep = at(2 * NP * (C + 1), 2, NP, C + 1)
        en = at(NP * C, NP, C)
        ar = at(2 * NP * 2 * C, 2, NP, 2, C)
        bk = at(2 * 2 * NP * C, 2, 2, NP, C)
        bkp = at(2 * NP * C, 2, NP, C)
        tp = at(2 * NP * C, 2, NP, C)
        ab = at(NP * 2 * C, NP, 2, C)
        kq = at(NP * 2 * C, NP, 2, C)
        tok = at(3 * NP * C, 3, NP, C)
        xl = at(NP * C, NP, C)
        rr = at(NP * C, NP, C)
        sa = at(NP * C, NP, C)
        st = at(2 * NP * C, 2, NP, C)
        stp = at(NP * C, NP, C)
        chunk_end = top[0]
        ws = at(2048, NP, NB, 64)
        t1 = at(512, NB, 64)
        t2 = at(512, NB, 64)
        wsmp = at(NP * NB, NP, NB)
        merged = at(KD * T, KD, T)
        sga = at(KD * T, KD, T)
        sh = at(SHIFT_TILES * 9, SHIFT_TILES, 9)
        eps = at(1)
        lnx_eps = at(1)
        shs = at(SHIFT_TILES * NB, SHIFT_TILES, NB)
        shd = at(SHIFT_TILES * NB, SHIFT_TILES, NB)

        def cc(name, *dims, rows=P):
            o, w = CON[name]
            a = con[0:rows, o:o + w] if o < NKEEP else con1[0:rows, o - NKEEP:o - NKEEP + w]
            if len(dims) == 2:
                return a.rearrange("p (a b) -> p a b", a=dims[0])
            if len(dims) == 3:
                return a.rearrange("p (a b c) -> p a b c", a=dims[0], b=dims[1])
            return a

        def vv(name, i):
            o = VEC[name] + i
            return vec[:, o:o + 1]

        ident, bones, ones, perm = cc("ident"), cc("bones"), cc("ones"), cc("perm")

        psum = E(nc.psum_tensor("psum", [P, 4096], F32))

        def bank(b, n=512, rows=P):
            return psum[0:rows, 512 * b:512 * b + n]

        s_load = sem("s_load")
        s_load2 = sem("s_load2")
        s_x = [sem(f"s_xin{i}") for i in range(KD // 2)]
        s_w = [sem(f"s_w{i}") for i in range(NW)]
        s_job = sem("s_job")
        s_free = [sem(f"s_free{i}") for i in range(2)]
        s_act = sem("s_act")
        s_dve = sem("s_dve")
        s_pool = sem("s_pool")
        s_sq = sem("s_sq")
        s_rms = sem("s_rms")
        s_u = sem("s_u")
        s_raw = sem("s_raw")
        s_shift = sem("s_shift")
        s_sig = sem("s_sig")
        s_kq = sem("s_kq")
        s_vb = sem("s_vb")
        s_rsp = sem("s_rsp")
        s_sn = sem("s_sn")
        s_roq = sem("s_roq")
        s_od = sem("s_od")
        s_osq = sem("s_osq")
        s_on = sem("s_on")
        s_ys = sem("s_ys")
        s_ph = sem("s_ph")
        s_smr = sem("s_smr")
        s_ws = sem("s_ws")
        s_vsr = sem("s_vsr")
        s_att = sem("s_att")
        s_atf = [sem(f"s_atf{i}") for i in range(2)]
        s_lin = sem("s_lin")
        s_kkt = sem("s_kkt")
        s_kks = sem("s_kks")
        s_kkd = sem("s_kkd")
        s_bont = sem("s_bont")
        s_e = sem("s_e")
        s_ab = sem("s_ab")
        s_abp = sem("s_abp")
        s_pab = sem("s_pab")
        s_tri = sem("s_tri")
        s_toks = sem("s_toks")
        s_px = sem("s_px")
        s_xl = sem("s_xl")
        s_pt = sem("s_pt")
        s_tt = sem("s_tt")
        s_pr = sem("s_pr")
        s_rr = sem("s_rr")
        s_psa = sem("s_psa")
        s_sa = sem("s_sa")
        s_ps = sem("s_ps")
        s_st = sem("s_st")
        s_y = sem("s_y")
        s_gb = sem("s_gb")
        s_m1 = sem("s_m1")
        s_sw = sem("s_sw")
        s_sld = sem("s_sld")
        s_smt = sem("s_smt")
        s_smp = sem("s_smp")
        s_var = sem("s_var")
        s_vsd = sem("s_vsd")
        s_ya = sem("s_ya")
        s_mg = sem("s_mg")
        s_xr = sem("s_xr")
        s_x2 = sem("s_x2")
        s_out = sem("s_out")
        s_rets = sem("s_rets")
        s_rst = sem("s_rst")

        def job(step):
            return JOBS[step]

        def job_done(eng, step):
            eng.wait_ge(s_job, JOBS[step] + 1)

        def job_read(eng, step):
            n = JOBS[step]
            eng.wait_ge(s_free[n % 2], n // 2 + 1)

        def job_ps(step, n=HT, rows=P):
            return bank(JOBS[step] % 2, n, rows)

        def cols(hf):
            return slice(hf * HT, (hf + 1) * HT)

        NCH = len(CHUNKS)
        NLEV = [sum(1 for b in LEVELS[1:] if b < w) for _, w in CHUNKS]
        LEV0 = [sum(NLEV[:c]) for c in range(NCH)]

        def wk(c, s):
            t0, w = CHUNKS[c]
            return t0, w, slice(64 * s, 64 * s + 64), slice(64 * s, 64 * s + w)

        def bc(a, n):
            return a.unsqueeze(len(a.shape)).broadcast_to(list(a.shape) + [n])

        def pairs(a):
            return a.unsqueeze(1).broadcast_to([a.shape[0], NP] + list(a.shape[1:]))

        mixer = nc.Block()
        block = mixer.__enter__()

        @block.sync
        def _(sp):
            for k in range(0, KD, 2):
                sp.dma_start(u[:, k:k + 2, :], I["x"][:, k:k + 2, :]).then_inc(s_x[k // 2], 16)
            sp.dma_start(con, I["con"][:, 0:NKEEP]).then_inc(s_load, 16)
            sp.dma_start(vec, I["vec"]).then_inc(s_load, 16)

            def tables():
                for dst, src in ((con1, I["con"][:, NKEEP:NCON]), (shs, I["sh0"]), (up_wa, I["up_wa"]),
                                 (up_g, I["up_g"])):
                    sp.dma_start(dst, src).then_inc(s_load2, 16)


            def weights(i):
                kind, m, _ = WTILES[i]
                if i >= NW:
                    k0, m0, h0 = WTILES[i - NW]
                    job_done(sp, (k0, m0, h0[-1]))
                nk = KD if kind in ("j_proj", "j_out") else NP
                sp.dma_start(wt[:, i % NW, 0:nk, :], I["w_" + KINDS[kind]][m]).then_inc(s_w[i % NW], 16)

            for i in range(len(WTILES)):
                if i == 1:
                    tables()
                if i == NW:
                    sp.dma_start(s_new, I["rets0"]).then_inc(s_rets, 16)
                if i == 16 + NW:
                    sp.wait_ge(s_sn, RH)
                    sp.wait_ge(s_roq, RH)
                    sp.dma_start(O["rets"], s_new).then_inc(s_out, 16)
                    for h in range(RH):
                        job_read(sp, ("j_rst", h))
                    sp.dma_start(O["retp"], ret_st).then_inc(s_out, 16)
                if i == 16 + 8:
                    sp.wait_ge(s_ph, 1)
                    sp.dma_start(ws, I["wkv0"]).then_inc(s_sld, 16)
                if i == WIDX[("j_ba", NW, 0)]:
                    for q in range(2):
                        job_done(sp, ("j_proj", GA0 + 7, q))
                    sp.dma_start(u, I["x"]).then_inc(s_xr, 16)
                    sp.wait_ge(s_st, NCH + 1)
                    sp.dma_start(O["wkvp"], st[:, NCH % 2]).then_inc(s_out, 16)
                    sp.wait_ge(s_raw, SHIFT_TILES)
                    sp.dma_start(O["shift"], sh).then_inc(s_out, 16)
                    sp.wait_ge(s_ws, NP)
                    sp.dma_start(O["wkvs"], ws).then_inc(s_out, 16)
                weights(i)
            sp.wait_ge(s_out, 16 * 5)

        @block.tensor
        def _(pe):
            mm = nc.tensor.matmul

            def open_job(step):
                n = JOBS[step]
                if n >= 2:
                    pe.wait_ge(s_free[n % 2], n // 2)
                return job_ps(step)

            def products(step, nk, rhs, part=None):
                kind, m, hf = step
                np_ = PARTS.get(kind)
                ps = job_ps(step) if part else open_job(step)
                i = WIDX[step]
                if hf == WTILES[i][2][0] and not part:
                    pe.wait_ge(s_w[i % NW], 16 * (i // NW + 1))
                for k in range(nk) if part is None else range(part * nk // np_, (part + 1) * nk // np_):
                    if step == ("j_proj", RET0, 0):
                        pe.wait_ge(s_u, k + 1)
                    if step == ("j_proj", RET0, 1) and k == 0:
                        pe.wait_ge(s_u, 2 * KD)
                    last = mm(ps, wt[:, i % NW, k, :], rhs[:, k, cols(hf)], start=(k == 0), stop=(k == nk - 1))
                if part is None or part == np_ - 1:
                    last.then_inc(s_job, 1)

            pe.wait_ge(s_load, 32)
            halved = [s_[1] for s_ in STEPS if s_[0] == "pre"]
            for step in STEPS:
                kind = step[0]
                if kind == "j_norm":
                    ps = open_job(step)
                    for k in range(KD):
                        if step[2] == 0:
                            pe.wait_ge(s_sq, k + 1)
                        last = mm(ps, ones, merged[:, k, cols(step[2])], start=(k == 0), stop=(k == KD - 1))
                    last.then_inc(s_job, 1)
                elif kind == "j_proj":
                    products(step, KD, u, PARTS[kind] - 1 if step in halved else None)
                elif kind == "pre":
                    if step[1] == ("j_bb", 0, 0):
                        pe.wait_ge(s_on, RH)
                    _, whole_step, part = step
                    products(whole_step, *((KD, u) if whole_step[0] == "j_proj" else (NP, ret_o)), part)
                elif kind == "j_rope":
                    _, j, hf = step
                    if j == 0:
                        pe.wait_ge(s_load2, 64)
                    job_read(pe, ("j_proj", RET0 + j, hf))
                    ps = open_job(step)
                    mm(ps, perm, ret[:, j, cols(hf)], start=True, stop=True).then_inc(s_job, 1)
                elif kind in ("j_vt", "j_kt"):
                    t = step[1]
                    n = LASTT if t == TT - 1 else P
                    open_job(step)
                    ps = bank(bank_of(step), 512, n)
                    if kind == "j_vt":
                        job_read(pe, ("j_proj", RET0 + 11, 0))
                        job_read(pe, ("j_proj", RET0 + 11, 1))
                    else:
                        pe.wait_ge(s_kq, 16)
                    for h in range(RH):
                        src = ret[:, (8 if kind == "j_vt" else 4) + h, t * P:t * P + n]
                        last = nc.tensor.transpose(ps[:, h * P:(h + 1) * P], src, ident)
                    last.then_inc(s_job, 1)
                elif kind == "rs_a":
                    h = step[1]
                    pe.wait_ge(s_vb, h + 1)
                    if h:
                        pe.wait_ge(s_sn, h)
                    job_read(pe, ("j_kt", TT - 1))
                    for q in range(2):
                        last = mm(bank(4 + q), k_smp[0:LASTT, h, :], vb[0:LASTT, 4 * q:4 * q + 4, :],
                                  start=True, stop=True)
                    last.then_inc(s_rsp, 1)
                elif kind == "rs_b":
                    h = step[1]
                    pe.wait_ge(s_sn, h + 1)
                    if h:
                        pe.wait_ge(s_od, h)
                    for q in range(2):
                        last = mm(bank(6 + q, 512, NB), ret[:, h, TP:T], s_new[:, h, 4 * q:4 * q + 4, :],
                                  start=True, stop=True)
                    last.then_inc(s_roq, 1)
                elif kind == "j_ros":
                    h = step[1]
                    open_job(step)
                    pe.wait_ge(s_od, h + 1)
                    mm(job_ps(step, NB), o_smp[0:NB, h, :], ident[0:NB, 0:NB], start=True,
                       stop=True).then_inc(s_job, 1)
                elif kind == "j_score":
                    h, r, j, i0, i1, first, last_ = RB[step[1]]
                    n = min(P, TP - j * P)
                    open_job(step)
                    mm(job_ps(step, i1 - i0, n), ret[:, 4 + h, j * P:j * P + n], ret[:, h, i0:i1],
                       start=True, stop=True).then_inc(s_job, 1)
                elif kind == "att":
                    b = step[1]
                    h, r, j, i0, i1, first, last_ = RB[b]
                    n = min(P, TP - j * P)
                    g = 2 * h + r
                    if first and g >= 2:
                        pe.wait_ge(s_atf[g % 2], g // 2)
                    job_read(pe, ("j_score", b))
                    o0 = i0 - r * (TP // 2)
                    x = mm(bank(2 + g % 2)[:, o0:TP // 2], v_tok[0:n, j, h, :], sc[0:n, b % 3, 0:i1 - i0],
                           start=first, stop=last_)
                    x.then_inc(s_att, 1)
                elif kind == "j_rst":
                    h = step[1]
                    open_job(step)
                    for j in range(TT):
                        n = LASTT if j == TT - 1 else P
                        last = mm(job_ps(step, P), k_tok[0:n, j, h, :], v_tok[0:n, j, h, :], start=(j == 0),
                                  stop=(j == TT - 1))
                    last.then_inc(s_job, 1)
                elif kind == "j_orms":
                    ps = open_job(step)
                    pe.wait_ge(s_osq, step[1] + 1)
                    mm(ps, ones, tmp[:, step[1], cols(step[2])], start=True, stop=True).then_inc(s_job, 1)
                elif kind == "j_lora":
                    _, k, p, hf = step
                    ps = open_job(step)
                    pe.wait_ge(s_lin, 2)
                    rows = {"w": slice(0, 64), "a": slice(64, P), "g": slice(0, P)}[k]
                    w, x = (up_g, gd) if k == "g" else (up_wa, wad)
                    mm(ps, w[rows, p * P:(p + 1) * P], x[rows, cols(hf)], start=True, stop=True)\
                        .then_inc(s_job, 1)
                elif kind in ("j_kkn", "j_bon"):
                    _, p, hf = step
                    ps = open_job(step)
                    pe.wait_ge(s_kkt if kind == "j_kkn" else s_bont, p + 1)
                    mm(ps, bones, tmp[:, p, cols(hf)],
                       start=True, stop=True).then_inc(s_job, 1)
                elif kind == "j_bb":
                    products(step, NP, ret_o, PARTS[kind] - 1)
                elif kind == "wk_a":
                    c = step[1]
                    t0, w, _, _ = wk(c, 0)
                    q = c % 2
                    pe.wait_ge(s_ab, c + 1)
                    if c:
                        pe.wait_ge(s_tri, 3 * c)
                        pe.wait_ge(s_tt, LEV0[c])
                        pe.wait_ge(s_rr, c)
                        pe.wait_ge(s_sa, c)
                        pe.wait_ge(s_st, c + 1)
                        pe.wait_ge(s_y, c)
                        pe.wait_ge(s_toks, 3 * c)
                    for s in range(2):
                        _, _, full, part = wk(c, s)
                        for p in range(NP):
                            rhs = ar[full, q, p, :, 0:w]
                            o = psum[part, 1024 + 128 * p:1024 + 128 * p + 128]\
                                .rearrange("p (a b) -> p a b", a=2)[:, :, 0:w]
                            mm(o, bk[full, q, 0, p, 0:w], rhs, start=True, stop=True)
                            o = psum[part, 1536 + 128 * p:1536 + 128 * p + 128]\
                                .rearrange("p (a b) -> p a b", a=2)[:, :, 0:w]
                            mm(o, bk[full, q, 1, p, 0:w], rhs, start=True, stop=True)
                            last = mm(psum[part, 2048 + 64 * p:2048 + 64 * p + w], ar[full, q, p, 0, 0:w],
                                      bk[full, q, 0, p, 0:w], start=True, stop=True)
                    last.then_inc(s_pab, 1)
                    for i in range(2):
                        b = 7 - i
                        if i == 1:
                            pe.wait_ge(s_abp, c + 1)
                        for p in range(NP):
                            src = v_f[:, p, t0:t0 + w] if i == 0 else bkp[:, 0, p, 0:w]
                            last = nc.tensor.transpose(bank(b, 512, w)[:, p * P:(p + 1) * P], src, ident)
                        last.then_inc(s_px, 1)
                elif kind == "wk_k":
                    c = step[1]
                    _, w, _, _ = wk(c, 0)
                    pe.wait_ge(s_toks, 3 * c + 1)
                    for p in range(NP):
                        last = nc.tensor.transpose(bank(7, 512, w)[:, p * P:(p + 1) * P], bkp[:, 1, p, 0:w], ident)
                    last.then_inc(s_px, 1)
                elif kind == "wk_x":
                    _, c, b = step
                    l = LEVELS.index(b)
                    if b == 2:
                        pe.wait_ge(s_tri, 3 * c + 2)
                    else:
                        pe.wait_ge(s_tt, LEV0[c] + l - 1)
                    for s in range(2):
                        _, w, full, part = wk(c, s)
                        for p in range(NP):
                            last = mm(psum[part, 2048 + 64 * p:2048 + 64 * p + w], ab[part, p, 0, 0:w],
                                      tp[part, 0, p, 0:w], start=True, stop=True)
                    last.then_inc(s_pt, 1)
                elif kind == "wk_t":
                    _, c, b = step
                    l = LEVELS.index(b)
                    pe.wait_ge(s_xl, LEV0[c] + l)
                    for s in range(2):
                        _, w, full, part = wk(c, s)
                        for p in range(NP):
                            if 2 * b < w:
                                mm(psum[part, 2560 + 64 * p:2560 + 64 * p + w], tp[part, 1, p, 0:w],
                                   xl[part, p, 0:w], start=True, stop=True)
                            last = mm(psum[part, 2816 + 64 * p:2816 + 64 * p + w], xl[part, p, 0:w],
                                      tp[part, 1, p, 0:w], start=True, stop=True)
                    last.then_inc(s_pr, 1)
                elif kind == "wk_r":
                    c = step[1]
                    q = c % 2
                    pe.wait_ge(s_st, c + 1)
                    pe.wait_ge(s_toks, 3 * c + 3)
                    pe.wait_ge(s_tri, 3 * c + 3)
                    for s in range(2):
                        _, w, full, part = wk(c, s)
                        for p in range(NP):
                            o = psum[part, 3072 + 64 * p:3072 + 64 * p + 64]
                            mm(o, ar[full, q, p, 0, 0:w], st[full, q, p, :], start=True, stop=False)
                            last = mm(o, kq[part, p, 0, 0:w], tok[part, 0, p, :], start=False, stop=True)
                    last.then_inc(s_psa, 1)
                elif kind == "wk_sa":
                    c = step[1]
                    pe.wait_ge(s_tt, LEV0[c] + NLEV[c])
                    pe.wait_ge(s_rr, c + 1)
                    for s in range(2):
                        _, w, full, part = wk(c, s)
                        for p in range(NP):
                            last = mm(psum[part, 3328 + 64 * p:3328 + 64 * p + 64], tp[part, 1, p, 0:w],
                                      rr[part, p, :], start=True, stop=True)
                    last.then_inc(s_psa, 1)
                elif kind == "wk_s":
                    c = step[1]
                    q = c % 2
                    pe.wait_ge(s_sa, c + 1)
                    for s in range(2):
                        _, w, full, part = wk(c, s)
                        for p in range(NP):
                            o = psum[full, 3584 + 64 * p:3584 + 64 * p + 64]
                            mm(o, tok[part, 1, p, :], sa[part, p, :], start=True, stop=False)
                            last = mm(o, tok[part, 2, p, :], tok[part, 0, p, :], start=False, stop=True)
                    last.then_inc(s_ps, 1)
                    for s in range(2):
                        _, w, full, part = wk(c, s)
                        for p in range(NP):
                            o = psum[full, 3072 + 64 * p:3072 + 64 * p + w]
                            mm(o, st[full, q, p, :], ar[full, q, p, 1, 0:w], start=True, stop=False)
                            mm(o, sa[part, p, :], ab[part, p, 1, 0:w], start=False, stop=False)
                            last = mm(o, tok[part, 0, p, :], kq[part, p, 1, 0:w], start=False, stop=True)
                    last.then_inc(s_ps, 1)
                elif kind in ("j_sk", "j_sv", "j_sy"):
                    p = step[1]
                    open_job(step)
                    pe.wait_ge(s_smt, 3 * p + {"j_sk": 1, "j_sv": 2, "j_sy": 3}[kind])
                    mm(job_ps(step, 512), bones, (t2 if kind == "j_sv" else t1), start=True, stop=True)\
                        .then_inc(s_job, 1)
                elif kind in ("j_mean", "j_var"):
                    _, p, hf = step
                    ps = open_job(step)
                    if kind == "j_mean":
                        pe.wait_ge(s_y, 1 + (HT - 1) // C if hf == 0 else NCH)
                        if hf:
                            pe.wait_ge(s_ys, NP)
                    else:
                        pe.wait_ge(s_vsd, NP * hf + p + 1)
                    mm(ps, bones, (ly if kind == "j_mean" else tmp)[:, p, cols(hf)], start=True,
                       stop=True).then_inc(s_job, 1)
                elif kind == "j_ba":
                    if step[1] == 0:
                        pe.wait_ge(s_ya, NP * (step[2] + 1))
                    products(step, NP, ly)
                elif kind == "j_out":
                    if step[1] == 0:
                        pe.wait_ge(s_mg, KD * (step[2] + 1))
                    products(step, KD, merged)

        SHIFT_ORDER = [s_[1] for s_ in STEPS if s_[0] == "j_proj" and s_[1] < SHIFT_TILES and s_[2] == 0]

        def shifted(m):
            return [r_f, k_f, v_f][m // 4][:, m % 4, :] if m < 12 else (wad, gd)[m - 12]

        @block.scalar
        def _(act):
            own = [0]

            def run(ins, s=None):
                if s is None:
                    own[0] += 1
                    ins.then_inc(s_act, 1)
                    act.wait_ge(s_act, own[0])
                else:
                    ins.then_inc(s, 1)

            def f(out, in_, fn=ACT.Copy, s=None, **kw):
                run(nc.scalar.activation(out, in_, fn, **kw), s)

            act.wait_ge(s_load, 32)
            for step in STEPS:
                kind = step[0]
                free = s_free[JOBS[step] % 2] if step in JOBS else None
                if kind == "j_norm":
                    job_done(act, step)
                    f(tmp[:, 0, cols(step[2])], job_ps(step), ACT.Sqrt, scale=1.0 / D, bias=eps, s=free)
                elif kind == "j_proj":
                    _, m, hf = step
                    job_done(act, step)
                    if m < SHIFT_TILES:
                        i = SHIFT_ORDER.index(m)
                        if i == 0:
                            act.wait_ge(s_ph, 1)
                        if i >= 2:
                            act.wait_ge(s_shift, i - 1)
                        f(raw[:, i % 2, 1 + hf * HT:1 + (hf + 1) * HT], job_ps(step), s=free)
                        if hf:
                            job_read(act, ("j_proj", m, 0))
                            job_read(act, step)
                            f(sh[:, m, :], raw[:, i % 2, TP:TP + 9], s=s_raw)
                    elif m < RET0 + 12:
                        f(ret[:, m - RET0, cols(hf)], job_ps(step), s=free)
                    elif m < GA0:
                        f(ret[:, m - RET0, cols(hf)], job_ps(step), ACT.Sigmoid, s=s_sig)
                    elif m < GB0:
                        f(sga[:, m - GA0, cols(hf)], job_ps(step), ACT.Sigmoid, s=free)
                    else:
                        f(merged[:, m - GB0, cols(hf)], job_ps(step), ACT.Sigmoid, s=free)
                elif kind == "j_vt":
                    t = step[1]
                    n = LASTT if t == TT - 1 else P
                    job_done(act, step)
                    f(v_tok[0:n, t, :, :], bank(bank_of(step), 512, n).rearrange("p (h v) -> p h v", h=RH), s=free)
                elif kind == "j_ros":
                    job_done(act, step)
                    f(ret_o[:, step[1], TP:T], job_ps(step, NB), s=free)
                elif kind == "att":
                    b = step[1]
                    h, r, j, i0, i1, first, last_ = RB[b]
                    if last_:
                        g = 2 * h + r
                        act.wait_ge(s_att, b + 1)
                        f(ret_o[:, h, r * (TP // 2):(r + 1) * (TP // 2)], bank(2 + g % 2, TP // 2), s=s_atf[g % 2])
                elif kind == "j_rst":
                    job_done(act, step)
                    f(ret_st[:, step[1], :], job_ps(step, P), s=free)
                elif kind == "j_orms":
                    _, h, hf = step
                    job_done(act, step)
                    f(tmp[:, h, cols(hf)], job_ps(step), ACT.Sqrt, scale=1.0 / P, bias=eps, s=free)
                elif kind == "lora_in":
                    act.wait_ge(s_load2, 64)
                    act.wait_ge(s_shift, 2)
                    f(wad[0:64, :], wad[0:64, :], ACT.Tanh, s=s_lin)
                    f(gd, gd, ACT.Sigmoid, s=s_lin)
                elif kind == "j_lora":
                    _, k, p, hf = step
                    job_done(act, step)
                    if k == "g":
                        f(g_f[:, p, cols(hf)], job_ps(step), s=free)
                    else:
                        f((ly if k == "w" else b_f)[:, p, cols(hf)], job_ps(step), ACT.Sigmoid,
                          bias=vv("w0" if k == "w" else "a0", p), s=free)
                elif kind == "j_kkn":
                    job_done(act, step)
                    f(tmp[:, step[1], cols(step[2])], job_ps(step), ACT.Sqrt, s=free)
                elif kind == "wk_prep":
                    c = step[1]
                    t0, w, _, _ = wk(c, 0)
                    if c == 0:
                        act.wait_ge(s_bont, NP)
                        act.wait_ge(s_st, 1)
                    else:
                        act.wait_ge(s_ab, c)
                    if c >= 2:
                        act.wait_ge(s_st, c)
                    f(ep[:, c % 2, :, 1:w + 1], ly[:, :, t0:t0 + w], ACT.Exp, scale=-DECAY, s=s_e)
                    f(en[:, :, 0:w], ly[:, :, t0:t0 + w], ACT.Exp, scale=DECAY, s=s_e)
                elif kind in ("wk_a", "wk_k"):
                    c = step[1]
                    if c and kind == "wk_a":
                        act.wait_ge(s_ps, 2 * c)
                    for i in (0, 1) if kind == "wk_a" else (2,):
                        act.wait_ge(s_px, 3 * c + i + 1)
                        for s in range(2):
                            _, w, full, part = wk(c, s)
                            src = bank(6 if i == 1 else 7, 512, w)\
                                .rearrange("t (p s k) -> t p s k", p=NP, s=2)[:, :, s, :]
                            nc.scalar.activation(tok[part, i, :, :], src, ACT.Copy).then_inc(s_toks if s else s_act, 1)
                            if s == 0:
                                own[0] += 1
                        act.wait_ge(s_act, own[0])
                elif kind == "wk_r":
                    c = step[1]
                    act.wait_ge(s_psa, 2 * c + 1)
                    f(rr, bank(6, 256).rearrange("t (p k) -> t p k", p=NP), s=s_rr)
                elif kind == "wk_sa":
                    c = step[1]
                    act.wait_ge(s_psa, 2 * c + 2)
                    f(sa, psum[:, 3328:3584].rearrange("t (p k) -> t p k", p=NP), s=s_sa)
                elif kind == "wk_s":
                    c = step[1]
                    t0, w, _, _ = wk(c, 0)
                    act.wait_ge(s_ps, 2 * c + 2)
                    f(ly[:, :, t0:t0 + w], bank(6, 256).rearrange("t (p k) -> t p k", p=NP)[:, :, 0:w], s=s_y)
                elif step == ("sm_in", 0):
                    f(wsmp, ly[:, :, TP:T], ACT.Exp, scale=-DECAY, s=s_sw)
                elif kind == "j_var":
                    _, p, hf = step
                    job_done(act, step)
                    f(tmp[:, p, cols(hf)], job_ps(step), ACT.Sqrt, scale=1.0 / 64, bias=lnx_eps, s=free)

        @block.vector
        def _(dve):
            v = nc.vector
            own = [0]
            counts = {}

            def run(ins, s=None):
                s = s_dve if s is None else s
                counts[s.name] = counts.get(s.name, 0) + 1
                ins.then_inc(s, 1)
                if s.name in alone:
                    dve.wait_ge(s, counts[s.name])

            alone = {x.name for x in (s_dve, s_sq, s_u, s_shift, s_kq, s_vb, s_sn, s_od, s_osq, s_ph, s_kkt,
                                      s_bont, s_ab, s_abp, s_tri, s_tt, s_st, s_smt, s_ws, s_on, s_xl, s_ys, s_vsd, s_ya,
                                      s_mg, s_x2)}

            def tt(out, a, b, op=ALU.mult, s=None):
                run(v.tensor_tensor(out, a, b, op), s)

            def stt(out, a, sc_, b, op0, op1, s=None):
                run(v.scalar_tensor_tensor(out, a, sc_, b, op0, op1), s)

            def ts(out, a, s1, s2, op0, op1=None, s=None):
                run(v.tensor_scalar(out, a, s1, s2, op0, op1) if op1 is not None
                    else v.tensor_scalar(out, a, s1, None, op0), s)

            def decayed(c):
                _, w, _, _ = wk(c, 0)
                q = c % 2
                for i in range(2):
                    tt(bkp[:, i, :, 0:w], bk[:, q, i, :, 0:w], bc(ep[:, q, :, w], w), s=s_abp if i else None)

            dve.wait_ge(s_load, 32)
            run(v.memset(eps, EPS))
            run(v.memset(lnx_eps, LNX_EPS))
            for k in range(KD):
                dve.wait_ge(s_x[k // 2], 16)
                tt(merged[:, k, :], u[:, k, :], u[:, k, :], s=s_sq)
            nsig = 0
            for step in STEPS:
                kind = step[0]
                free = s_free[JOBS[step] % 2] if step in JOBS else None
                if kind == "j_norm":
                    hf = step[2]
                    job_read(dve, step)
                    run(v.reciprocal(tmp[:, 1, cols(hf)], tmp[:, 0, cols(hf)]))
                    for k in range(KD):
                        x = u[:, k, cols(hf)]
                        stt(x, x, vv("norm1_g", k), tmp[:, 1, cols(hf)], ALU.mult, ALU.mult, s=s_u)
                elif kind == "j_proj":
                    _, m, hf = step
                    if m < SHIFT_TILES and hf:
                        i = SHIFT_ORDER.index(m)
                        x = raw[:, i % 2, :]
                        o = shifted(m)
                        dve.wait_ge(s_raw, i + 1)
                        tt(dif[:, 0:TP], x[:, 0:TP], x[:, 1:TP + 1], ALU.subtract)
                        tt(shd[:, m, :], shs[:, m, :], sh[:, m, 1:9], ALU.subtract)
                        stt(o[:, TP:T], shd[:, m, :], vv("mu", m), sh[:, m, 1:9], ALU.mult, ALU.add)
                        stt(o[:, 0:TP], dif[:, 0:TP], vv("mu", m), x[:, 1:TP + 1], ALU.mult, ALU.add, s=s_shift)
                    elif RET0 + 12 <= m < GA0:
                        nsig += 1
                        dve.wait_ge(s_sig, nsig)
                        tt(ret[:, m - RET0, cols(hf)], job_ps(step), ret[:, m - RET0, cols(hf)], s=free)
                elif kind == "j_rope":
                    _, j, hf = step
                    a = 1.0 if j < RH else P ** -0.5
                    dve.wait_ge(s_load2, 64)
                    x = ret[:, j, cols(hf)]
                    job_done(dve, step)
                    stt(tmp[:, 2, 0:HT], job_ps(step), a, cc("sin")[:, cols(hf)], ALU.mult, ALU.mult, s=free)
                    stt(tmp[:, 3, 0:HT], x, a, cc("cos")[:, cols(hf)], ALU.mult, ALU.mult)
                    job_read(dve, step)
                    tt(x, tmp[:, 2, 0:HT], tmp[:, 3, 0:HT], ALU.add, s=s_kq)
                elif kind == "j_kt":
                    t = step[1]
                    n = LASTT if t == TT - 1 else P
                    ps = bank(bank_of(step), 512, n).rearrange("p (h v) -> p h v", h=RH)
                    job_done(dve, step)
                    if t == TT - 1:
                        run(v.tensor_copy(k_smp[0:n], ps))
                    tt(k_tok[0:n, t, :, :], ps, bc(cc("dend", TT, RH, rows=n)[:, t, :], P), s=free)
                elif kind == "rs_v":
                    h = step[1]
                    if h == 0:
                        job_read(dve, ("j_vt", TT - 1))
                        dve.wait_ge(s_rets, 16)
                    else:
                        dve.wait_ge(s_rsp, h)
                    tt(vb[0:LASTT], v_tok[0:LASTT, TT - 1, h, :].unsqueeze(1).broadcast_to([LASTT, NB, P]),
                       bc(cc("smask", rows=LASTT), P), s=s_vb)
                elif kind == "rs_a":
                    h = step[1]
                    dve.wait_ge(s_rsp, h + 1)
                    stt(s_new[:, h].rearrange("p b v -> p (b v)"), s_new[:, h].rearrange("p b v -> p (b v)"),
                        GAMMA[h], psum[:, 2048:3072], ALU.mult, ALU.add, s=s_sn)
                elif kind == "rs_b":
                    h = step[1]
                    dve.wait_ge(s_roq, h + 1)
                    tt(o_diag[0:NB], psum[0:NB, 3072:4096].rearrange("p (b v) -> p b v", b=NB),
                       bc(ident[0:NB, 0:NB], P))
                    run(v.tensor_reduce(o_smp[0:NB, h, :], o_diag[0:NB].rearrange("p b v -> p v b"), AX.X, ALU.add),
                        s_od)
                elif kind == "j_score":
                    n_ = step[1]
                    h, r, j, i0, i1, first, last_ = RB[n_]
                    n = min(P, TP - j * P)
                    job_done(dve, step)
                    if n_ >= 3:
                        dve.wait_ge(s_att, n_ - 2)
                    d = cc("dec", RH, TP, rows=n)[:, h, i0 - j * P:i1 - j * P]
                    tt(sc[0:n, n_ % 3, 0:i1 - i0], job_ps(step, i1 - i0, n), d, s=free)
                elif kind == "osq":
                    h = step[1]
                    job_read(dve, ("j_ros", h))
                    for g in range(2):
                        dve.wait_ge(s_atf[g], h + 1)
                    tt(tmp[:, h, :], ret_o[:, h, :], ret_o[:, h, :], s=s_osq)
                    for q in range(2):
                        job_read(dve, ("j_proj", RET0 + 12 + h, q))
                    tt(ret_o[:, h, :], ret_o[:, h, :], ret[:, 12 + h, :])
                elif kind == "phase2":
                    dve.wait_ge(s_out, 32)
                    dve.wait_ge(s_att, len(RB))
                    run(v.memset(raw[:, :, 0:1], 0.0), s_ph)
                elif kind == "j_orms" and step[2]:
                    h = step[1]
                    job_read(dve, ("j_orms", h, 0))
                    job_read(dve, step)
                    run(v.reciprocal(tmp[:, h, :], tmp[:, h, :]))
                    tt(ret_o[:, h, :], ret_o[:, h, :], tmp[:, h, :], s=s_on)
                elif kind == "kk_in":
                    p = step[1]
                    for hf in range(2):
                        job_read(dve, ("j_lora", "w", p, hf))
                    run(v.tensor_tensor_scan(ly[:, p, 0:TP], cc("reset"), ly[:, p, 0:TP], 0.0, ALU.mult, ALU.add))
                    ts(kk_f[:, p, :], k_f[:, p, :], vv("kk", p), None, ALU.mult)
                    tt(tmp[:, p, :], kk_f[:, p, :], kk_f[:, p, :], s=s_kkt)
                elif kind == "j_kkn" and step[2]:
                    p = step[1]
                    for hf in range(2):
                        job_read(dve, ("j_kkn", p, hf))
                    ts(tmp[:, p, :], tmp[:, p, :], 1e-12, None, ALU.max)
                    run(v.reciprocal(tmp[:, p, :], tmp[:, p, :]))
                    tt(kk_f[:, p, :], kk_f[:, p, :], tmp[:, p, :])
                elif kind == "bon_in":
                    p = step[1]
                    for hf in range(2):
                        job_read(dve, ("j_lora", "a", p, hf))
                    ts(tmp[:, p, :], b_f[:, p, :], -1.0, vv("ka", p), ALU.add, ALU.mult)
                    stt(k_f[:, p, :], tmp[:, p, :], 1.0, k_f[:, p, :], ALU.add, ALU.mult)
                    tt(b_f[:, p, :], kk_f[:, p, :], b_f[:, p, :])
                    stt(tmp[:, p, :], r_f[:, p, :], vv("rk", p), k_f[:, p, :], ALU.mult, ALU.mult, s=s_bont)
                elif kind == "j_bon":
                    _, p, hf = step
                    job_done(dve, step)
                    tt(bon[:, p, cols(hf)], job_ps(step), v_f[:, p, cols(hf)], s=free)
                elif kind == "wk_prep":
                    c = step[1]
                    q = c % 2
                    t0, w, _, _ = wk(c, 0)
                    if c == 0:
                        run(v.memset(ep[:, :, :, 0:1], 1.0))
                        run(v.memset(st[:, 0], 0.0), s_st)
                    dve.wait_ge(s_e, 2 * c + 2)
                    if c >= 2:
                        dve.wait_ge(s_ps, 2 * c - 2)
                    x = slice(t0, t0 + w)
                    tt(bk[:, q, 0, :, 0:w], b_f[:, :, x], en[:, :, 0:w])
                    tt(bk[:, q, 1, :, 0:w], k_f[:, :, x], en[:, :, 0:w])
                    stt(ar[:, q, :, 0, 0:w], kk_f[:, :, x], -1.0, ep[:, q, :, 0:w], ALU.mult, ALU.mult)
                    tt(ar[:, q, :, 1, 0:w], r_f[:, :, x], ep[:, q, :, 1:w + 1], s=s_ab)
                    if c == 0:
                        decayed(0)
                elif kind == "wk_k":
                    if step[1] + 1 < NCH:
                        dve.wait_ge(s_px, 3 * step[1] + 3)
                        decayed(step[1] + 1)
                elif kind == "wk_a":
                    c = step[1]
                    t0, w, _, _ = wk(c, 0)
                    dve.wait_ge(s_pab, c + 1)
                    if c:
                        dve.wait_ge(s_ps, 2 * c)
                    b2 = bank(2).rearrange("t (p a k) -> t p a k", p=NP, a=2)
                    ai = pairs(cc("ai", 2, C)[:, :, 0:w])
                    tt(tp[:, 1, :, 0:w], b2[:, :, 0, 0:w], pairs(cc("lev0t")[:, 0:w]))
                    tt(tp[:, 0, :, 0:w], bank(4, 256).rearrange("t (p k) -> t p k", p=NP)[:, :, 0:w],
                       pairs(cc("lev", 6, C)[:, 0, 0:w]))
                    for i in range(2):
                        tt(tp[:, i, :, 0:w], tp[:, i, :, 0:w], pairs(cc("eye")[:, 0:w]), ALU.add, s=s_tri if i else None)
                    tt(ab[:, :, :, 0:w], b2[:, :, :, 0:w], ai, s=s_tri)
                elif kind == "wk_x":
                    _, c, b = step
                    l = LEVELS.index(b)
                    _, w, _, _ = wk(c, 0)
                    dve.wait_ge(s_pt, LEV0[c] + l)
                    tt(xl[:, :, 0:w], bank(4, 256).rearrange("t (p k) -> t p k", p=NP)[:, :, 0:w],
                       pairs(cc("lev", 6, C)[:, l, 0:w]), s=s_xl)
                    if b == 2:
                        tt(kq[:, :, :, 0:w], bank(3).rearrange("t (p a k) -> t p a k", p=NP, a=2)[:, :, :, 0:w],
                           pairs(cc("ai", 2, C)[:, :, 0:w]), s=s_tri)
                elif kind == "wk_t":
                    _, c, b = step
                    l = LEVELS.index(b)
                    _, w, _, _ = wk(c, 0)
                    dve.wait_ge(s_pr, LEV0[c] + l)
                    f0 = 0 if 2 * b < w else 1
                    ps = bank(5).rearrange("t (a p k) -> t a p k", a=2, p=NP)
                    tt(tp[:, f0:2, :, 0:w], ps[:, f0:2, :, 0:w], tp[:, f0:2, :, 0:w], ALU.add, s=s_tt)
                elif kind == "wk_s":
                    c = step[1]
                    q = c % 2
                    _, w, _, _ = wk(c, 0)
                    tt(stp, st[:, q], bc(ep[:, q, :, w], C))
                    dve.wait_ge(s_ps, 2 * c + 1)
                    tt(st[:, 1 - q], bank(7, 256).rearrange("t (p k) -> t p k", p=NP), stp, ALU.add, s=s_st)
                elif kind == "j_bb":
                    _, m, hf = step
                    job_read(dve, ("j_proj", GB0 + m, hf))
                    job_done(dve, step)
                    tt(merged[:, m, cols(hf)], job_ps(step), merged[:, m, cols(hf)], s=free)
                elif kind in ("sm_in", "j_sk", "j_sv", "sm_y", "j_sy"):
                    p = step[1]

                    def tok_bc(a):
                        return bc(a[:, p, TP:T], 64)

                    w_, a1, a2 = ws[:, p], t1, t2
                    eye = cc("eye").unsqueeze(1).broadcast_to([P, NB, 64])
                    if kind == "sm_in":
                        if p == 0:
                            dve.wait_ge(s_sld, 16)
                            dve.wait_ge(s_sw, 1)
                        tt(a1, w_, tok_bc(kk_f), s=s_smt)
                        tt(a2, eye, tok_bc(v_f), s=s_smt)
                        tt(w_, w_, bc(wsmp[:, p, :], 64))
                    elif kind == "sm_y":
                        tt(a1, w_, tok_bc(r_f), s=s_smt)
                    else:
                        ps = job_ps(step, 512).rearrange("k (b v) -> k b v", b=NB)
                        job_done(dve, step)
                        if kind == "j_sk":
                            tt(a1, ps, tok_bc(b_f), s=free)
                            job_read(dve, step)
                            tt(w_, w_, a1, ALU.subtract)
                        elif kind == "j_sv":
                            tt(a1, ps, tok_bc(k_f), s=free)
                            job_read(dve, step)
                            tt(w_, w_, a1, ALU.add, s=s_ws)
                        else:
                            tt(a2, ps, eye, s=free)
                            job_read(dve, step)
                            run(v.tensor_reduce(ly[:, p, TP:T], a2, AX.X, ALU.add), s_ys)
                elif kind == "j_mean":
                    _, p, hf = step
                    job_done(dve, step)
                    x = ly[:, p, cols(hf)]
                    stt(x, job_ps(step), -1.0 / 64, x, ALU.mult, ALU.add, s=free)
                    job_read(dve, step)
                    tt(tmp[:, p, cols(hf)], x, x, s=s_vsd)
                elif kind == "j_var":
                    _, p, hf = step
                    job_read(dve, step)
                    x, y = tmp[:, p, cols(hf)], ly[:, p, cols(hf)]
                    run(v.reciprocal(x, x))
                    stt(y, y, vv("lnw", p), x, ALU.mult, ALU.mult)
                    stt(y, y, vv("lnb", p), bon[:, p, cols(hf)], ALU.add, ALU.add)
                    tt(y, y, g_f[:, p, cols(hf)], s=s_ya)
                elif kind == "j_ba":
                    _, m, hf = step
                    job_done(dve, step)
                    if hf == 0:
                        for q in range(2):
                            job_read(dve, ("j_proj", GA0 + m, q))
                            job_read(dve, ("j_bb", m, q))
                    tt(sga[:, m, cols(hf)], job_ps(step), sga[:, m, cols(hf)], s=free)
                    job_read(dve, step)
                    tt(merged[:, m, cols(hf)], merged[:, m, cols(hf)], sga[:, m, cols(hf)], ALU.add, s=s_mg)
                elif kind == "j_out":
                    _, m, hf = step
                    dve.wait_ge(s_xr, 16)
                    job_done(dve, step)
                    tt(u[:, m, cols(hf)], job_ps(step), u[:, m, cols(hf)], ALU.add, s=free)


        mixer.__exit__(None, None, None)

        top[0] = u_end
        NWE = 4
        we = at(NWE * 6144, NWE, 6144)
        w_gu = we[:, :, 0:4096].rearrange("p s (k f) -> p s k f", k=KD)
        w_dn = we[:, :, 4096:6144].rearrange("p s (f d) -> p s f d", f=2)
        x2t = at(TT * D, TT, D)
        ug0 = top[0]
        ug = at(2 * D, 2, D)
        ue = at(2 * D, 2, KD, P)
        sig = at(FF)
        hh = at(FF)
        hht = at(2 * P, 2, P)
        yo = at(2 * D, 2, D)
        yg = at(5 * D, 5, D, start=ug0)
        g_row = at(2 * D, 2, D)
        top[0] = ug0
        wr = at(KD * 20, KD, 20)
        logt = at(T)
        bias = at(20)
        lg = at(TT * 20, TT, 20)
        NS = TT * (1 + NG)
        ll = at(NS * 4, NS, 4)
        gt = at(NS * 16, NS, 4, 4)
        eq = at(NS * 16, NS, 4, 4)
        rank = at(NS * 4, NS, 4)
        mx = at(NS)
        ex = at(NS * 4, NS, 4)
        sel = at(NS * 4, NS, 4)
        sm = at(NS)
        ga = at(TT * 4, TT, 4)
        gw = at(TT * 4, TT, 4)
        f1 = at(TT * NE, TT, NE)
        f2 = at(TT * NE, TT, NE)
        wts = at(TT * NE, TT, NE)
        dest = at(TT * NE, TT, NE)
        tq = at(TT * NE, TT, NE)
        ssq = at(TT)
        rstd = at(TT)
        cnt = at(8)
        zero = E(nc.sbuf_tensor("zero", [P, ROUNDS * NE], I32))
        u2b = at(2 * D, 2, D)
        junk = yo[:, 0, :]
        assert top[0] <= ug0 + 4 * D + 3 * FF, top[0] - ug0
        oneb = E(nc.sbuf_tensor("oneb", [P, P], BF16))
        trib = E(nc.sbuf_tensor("trib", [P, P], BF16))
        selb = E(nc.sbuf_tensor("selb", [P, TT, NE], BF16))
        token = E(nc.sbuf_tensor("token", [P, TT], I32))
        d_i = E(nc.sbuf_tensor("d_i", [P, 2, TT], I32))
        c_w = E(nc.sbuf_tensor("c_w", [P, 2, TT], F32))
        d_f = E(nc.sbuf_tensor("d_f", [P, 2, TT], F32))
        in_r = E(nc.sbuf_tensor("in_r", [P, 2, TT], F32))
        cw_r = E(nc.sbuf_tensor("cw_r", [P, 2, TT], F32))
        dcl = E(nc.sbuf_tensor("dcl", [P, 2, TT], F32))
        n_rounds = E(nc.sbuf_tensor("n_rounds", [P, 1], I32))
        ids = E(nc.sbuf_tensor("ids", [P, NE], I32))
        eps2 = E(nc.sbuf_tensor("eps2", [P, 1], F32))

        u2_dram = nc.dram_tensor("u2_rows", [T, D], F32, kind="Internal").ap()
        id_dram = nc.dram_tensor("id_list", [ROUNDS * ROWS, 1], I32, kind="Internal").ap()
        y_dram = nc.dram_tensor("y_rows", [ROWS, D], F32, kind="Internal").ap()
        id_rows = id_dram.rearrange("(r e) o -> r (e o)", e=NE)
        y_view = y_dram.rearrange("(p e) d -> p e d", e=NE)

        d_ld = sem("d_ld")
        s_we = [sem(f"s_we{i}") for i in range(NWE)]
        d_wr = sem("d_wr")
        d_lt = sem("d_lt")
        d_ltc = sem("d_ltc")
        d_lg = sem("d_lg")
        d_x = sem("d_x")
        d_xc = sem("d_xc")
        d_act = sem("d_act")
        d_dve = sem("d_dve")
        d_ss = sem("d_ss")
        d_rt = sem("d_rt")
        d_ll = sem("d_ll")
        d_ex = sem("d_ex")
        d_u2 = sem("d_u2")
        d_u2w = [sem(f"d_u2w{i}") for i in range(2)]
        d_sel = sem("d_sel")
        d_pos = sem("d_pos")
        d_ids = sem("d_ids")
        d_z = sem("d_z")
        d_zw = sem("d_zw")
        d_sc = sem("d_sc")
        d_tok = sem("d_tok")
        d_n = sem("d_n")

        def rows_of(t):
            return LASTT if t == TT - 1 else P

        def load_expert(eng, e):
            eng.dma_start(we[:, e % NWE, 0:4096], I["w_gu"][e]).then_inc(s_we[e % NWE], 16)
            eng.dma_start(we[:, e % NWE, 4096:6144], I["w_dn"][e]).then_inc(s_we[e % NWE], 16)

        with nc.Block() as block:
            @block.sync
            def _(sp):
                for dst, src in ((wr, I["w_r"]), (bias, I["b_r"]), (g_row[:, 0, :], I["g2row"]),
                                 (g_row[:, 1, :], I["gfrow"])):
                    sp.dma_start(dst, src).then_inc(d_ld, 16)
                sp.wait_ge(d_z, 1)
                sp.dma_start(id_dram.rearrange("(p c) o -> p (c o)", p=P), zero[:, :]).then_inc(d_zw, 16)
                for e in range(NWE):
                    load_expert(sp, e)
                for t in range(TT):
                    sp.wait_ge(d_u2, t + 1)
                    sp.dma_start(u2_dram[t * P:t * P + rows_of(t), :], u2b[0:rows_of(t), t % 2, :])\
                        .then_inc(d_u2w[t % 2], 16)
                sp.wait_ge(d_u2w[0], 16 * 3)
                sp.wait_ge(d_u2w[1], 16 * 2)

            @block.gpsimd
            def _(pool):
                nc.gpsimd.memset(zero[:, :], 0).then_inc(d_z, 1)
                nc.gpsimd.iota(token[:, :], [[P, TT]], base=0, channel_multiplier=1).then_inc(d_tok, 1)
                pool.wait_ge(d_tok, 1)
                pool.wait_ge(d_zw, 16)
                pool.wait_ge(d_ids, 1)
                for i in range(2):
                    for t in range(TT):
                        n = rows_of(t)
                        pool.indirect_dma_start(id_dram, bass.IndirectOffsetOnAxis(ap=d_i[0:n, i, t:t + 1], axis=0),
                                                token[0:n, t:t + 1], None).then_inc(d_sc, 16)
                pool.wait_ge(d_sc, 16 * 2 * TT)

            @block.tensor
            def _(pe):
                pe.wait_ge(d_wr, 1)
                for hf in range(2):
                    for k in range(KD):
                        last = nc.tensor.matmul(bank(hf, HT, 20), wr[:, k, :], u[:, k, cols(hf)], start=(k == 0),
                                                stop=(k == KD - 1))
                last.then_inc(d_lt, 1)
                for t in range(TT):
                    n = rows_of(t)
                    if t >= 2:
                        pe.wait_ge(d_xc, t - 1)
                    for k in range(KD):
                        last = nc.tensor.transpose(psum[0:n, 2048 + 1024 * (t % 2) + P * k:2048 + 1024 * (t % 2) + P * (k + 1)],
                                                   u[:, k, t * P:t * P + n], ident)
                    last.then_inc(d_x, 1)
                    if t == 1:
                        pe.wait_ge(d_ltc, 1)
                        for q in range(TT):
                            m = rows_of(q)
                            last = nc.tensor.transpose(bank(2, 512, m)[:, 20 * q:20 * q + 20],
                                                       logt[0:20, q * P:q * P + m], ident[0:20, 0:20])
                        last.then_inc(d_lg, 1)
                pe.wait_ge(d_sel, 1)
                for t in range(TT + 1):
                    o = bank(3)[:, NE * t:NE * t + NE]
                    for q in range(min(t, TT - 1) + 1 if t < TT else TT):
                        last = nc.tensor.matmul(o, trib[:, :] if q == t else oneb[:, :], selb[:, q, :], start=(q == 0),
                                                stop=(q == min(t, TT - 1)))
                last.then_inc(d_pos, 1)

            @block.scalar
            def _(act):
                a = nc.scalar.activation
                act.wait_ge(d_lt, 1)
                a(logt[0:20, :].rearrange("p (a c) -> p a c", a=2),
                  psum[0:20, 0:1024].rearrange("p (a c) -> p a c", a=2)[:, :, 0:HT], ACT.Copy).then_inc(d_ltc, 1)
                for t in range(TT):
                    n = rows_of(t)
                    act.wait_ge(d_x, t + 1)
                    a(x2t[0:n, t, :], psum[0:n, 2048 + 1024 * (t % 2):3072 + 1024 * (t % 2)], ACT.Copy).then_inc(d_xc, 1)
                    act.wait_ge(d_xc, t + 1)
                    if t:
                        act.wait_ge(d_act, t)
                    else:
                        act.wait_ge(d_dve, 2)
                    a(junk[0:n], x2t[0:n, t, :], ACT.Square, accum_out=ssq[0:n, t:t + 1]).then_inc(d_act, 1)
                act.wait_ge(d_act, TT)
                a(rstd, ssq, ACT.Sqrt, scale=1.0 / D, bias=eps2[:, :]).then_inc(d_rt, 1)
                act.wait_ge(d_ll, 1)
                a(ex, ll, ACT.Exp).then_inc(d_ex, 1)

            @block.vector
            def _(dve):
                v = nc.vector
                own = [0]

                def run(ins, s=None):
                    if s is None:
                        own[0] += 1
                        ins.then_inc(d_dve, 1)
                        dve.wait_ge(d_dve, own[0])
                    else:
                        ins.then_inc(s, 1)
                        dve.wait_ge(s, 1)

                def tt(out, x, y, op=ALU.mult, s=None):
                    run(v.tensor_tensor(out, x, y, op), s)

                run(v.memset(eps2[:, :], EPS))
                run(v.memset(ssq, 1.0))
                run(v.memset(lg, 0.0))
                run(v.tensor_copy(trib[:, :], cc("tri")))
                run(v.tensor_copy(oneb[:, :], ones))
                dve.wait_ge(d_ld, 64)
                o2 = VEC["norm2_g"]
                tt(wr, wr, bc(vec[:, o2:o2 + KD], 20), s=d_wr)
                dve.wait_ge(d_rt, 1)
                run(v.reciprocal(rstd, rstd))
                dve.wait_ge(d_lg, 1)
                for t in range(TT):
                    n = rows_of(t)
                    run(v.scalar_tensor_tensor(lg[0:n, t, :], bank(2, 512, n)[:, 20 * t:20 * t + 20], rstd[0:n, t:t + 1],
                                               bias[0:n], ALU.mult, ALU.add))
                run(v.tensor_copy(ll[:, 0:TT, :], lg[:, :, 0:4]))
                run(v.tensor_copy(ll[:, TT:NS, :].rearrange("p (t g) e -> p t (g e)", t=TT), lg[:, :, 4:20]))
                me = bc(ll, 4)
                other = ll.unsqueeze(2).broadcast_to([P, NS, 4, 4])
                tt(gt, other, me, ALU.is_gt)
                tt(eq, other, me, ALU.is_equal)
                tt(eq, eq, cc("tie", 4, 4).unsqueeze(1).broadcast_to([P, NS, 4, 4]))
                tt(gt, gt, eq, ALU.add)
                run(v.tensor_reduce(rank, gt, AX.X, ALU.add))
                run(v.tensor_reduce(mx, ll, AX.X, ALU.max))
                tt(ll, ll, bc(mx, 4), ALU.subtract, s=d_ll)
                dve.wait_ge(d_ex, 1)
                run(v.tensor_reduce(sm[:, 0:TT], ex[:, 0:TT, :], AX.X, ALU.add))
                run(v.tensor_scalar(ga, rank[:, 0:TT, :], 0.5, None, ALU.is_lt))
                tt(ga, ga, bc(cc("valid"), 4))
                run(v.tensor_scalar(sel[:, TT:NS, :], rank[:, TT:NS, :], 1.5, None, ALU.is_lt))
                tt(ex[:, TT:NS, :], ex[:, TT:NS, :], sel[:, TT:NS, :])
                run(v.tensor_reduce(sm[:, TT:NS], ex[:, TT:NS, :], AX.X, ALU.add))
                run(v.reciprocal(sm, sm))
                tt(gw, ga, bc(sm[:, 0:TT], 4))
                tt(ex[:, TT:NS, :], ex[:, TT:NS, :], bc(sm[:, TT:NS], 4))
                tt(wts.rearrange("p t (g e) -> p (t g) e", g=NG), ex[:, TT:NS, :],
                   bc(gw.rearrange("p t g -> p (t g)"), 4))
                gax = bc(ga.rearrange("p t g -> p (t g)"), 4)
                for f, lo in ((f1, 0.0), (f2, 1.0)):
                    fv = f.rearrange("p t (g e) -> p (t g) e", g=NG)
                    run(v.tensor_scalar(fv, rank[:, TT:NS, :], lo, None, ALU.is_equal))
                    tt(fv, fv, gax)
                tt(selb[:, :, :], f1, f2, ALU.add, s=d_sel)
                for i, f in enumerate((f1, f2)):
                    tt(tq, wts, f)
                    run(v.tensor_reduce(c_w[:, i, :], tq, AX.X, ALU.add))
                dve.wait_ge(d_pos, 1)
                run(v.scalar_tensor_tensor(dest, bank(3, NE * TT).rearrange("p (t e) -> p t e", t=TT), float(NE),
                                           cc("expert").unsqueeze(1).broadcast_to([P, TT, NE]), ALU.mult, ALU.add))
                for i, f in enumerate((f1, f2)):
                    tt(tq, dest, f)
                    run(v.tensor_reduce(d_f[:, i, :], tq, AX.X, ALU.add))
                run(v.tensor_copy(d_i[:, :, :], d_f[:, :, :]), d_ids)
                run(v.tensor_reduce(cnt[:, 0:1], bank(3)[:, NE * TT:NE * TT + NE], AX.X, ALU.max))
                for i in range(1, ROUNDS):
                    run(v.tensor_scalar(cnt[:, i:i + 1], cnt[:, 0:1], float(SLOTS * i), None, ALU.is_gt))
                run(v.tensor_reduce(cnt[:, 6:7], cnt[:, 1:ROUNDS], AX.X, ALU.add))
                run(v.tensor_scalar(n_rounds[:, :], cnt[:, 6:7], 1.0, None, ALU.add), d_n)
                for t in range(TT):
                    n = rows_of(t)
                    if t >= 2:
                        dve.wait_ge(d_u2w[t % 2], 16 * (t // 2))
                    ins = v.scalar_tensor_tensor(u2b[0:n, t % 2, :], x2t[0:n, t, :], rstd[0:n, t:t + 1],
                                                 g_row[0:n, 0, :], ALU.mult, ALU.mult)
                    ins.then_inc(d_u2, 1)

        q_id = sem("q_id")
        q_g = [sem(f"q_g{i}") for i in range(2)]
        q_tr = sem("q_tr")
        q_ue = sem("q_ue")
        q_gu = sem("q_gu")
        q_sig = sem("q_sig")
        q_h1 = sem("q_h1")
        q_h = sem("q_h")
        q_ht = sem("q_ht")
        q_hte = sem("q_hte")
        q_dn = sem("q_dn")
        q_yo = sem("q_yo")
        q_yd = [sem(f"q_yd{i}") for i in range(2)]
        q_ix = sem("q_ix")
        q_yg = [sem(f"q_yg{i}") for i in range(5)]
        q_cb = sem("q_cb")
        q_dv = sem("q_dv")

        rounds = nc.values_load(n_rounds[0:1, 0:1], min_val=1, max_val=ROUNDS)
        with nc.Fori(0, rounds) as r:
            def at_least(eng, s, per, n):
                assert n > 0
                eng.wait_ge(s, r * per + n)

            with nc.Block() as block:
                @block.sync
                def _(sp):
                    sp.dma_start(ids[:, :], id_rows[bass.ds(r * P, P), :]).then_inc(q_id, 16)
                    for e in range(NWE, NE):
                        at_least(sp, q_dn, NE, e - NWE + 1)
                        load_expert(sp, e)
                    at_least(sp, q_dn, NE, NE)
                    sp.nop(nofuse=True)
                    with sp.If(r + 1 < rounds):
                        for e in range(NWE):
                            load_expert(sp, e)

                @block.gpsimd
                def _(pool):
                    def then(s, per, n):
                        at_least(pool, s, per, n)
                        pool.nop(nofuse=True)

                    then(q_id, 16, 16)
                    for e in range(NE):
                        if e >= 2:
                            then(q_tr, NE, e - 1)
                        pool.indirect_dma_start(ug[:, e % 2, :], None, u2_dram,
                                                bass.IndirectOffsetOnAxis(ap=ids[:, e:e + 1], axis=0))\
                            .then_inc(q_g[e % 2], 16)
                    then(q_ix, 1, 1)
                    for i in range(2):
                        then(q_yd[i], 8 * 16, 8 * 16)
                    for j in range(2 * TT):
                        t, i = j // 2, j % 2
                        n = rows_of(t)
                        if j >= 5:
                            then(q_cb, 2 * TT, j - 4)
                        pool.indirect_dma_start(yg[0:n, j % 5, :], None, y_dram,
                                                bass.IndirectOffsetOnAxis(ap=d_i[0:n, i, t:t + 1], axis=0))\
                            .then_inc(q_yg[j % 5], 16)

                @block.tensor
                def _(pe):
                    mm = nc.tensor.matmul

                    def to_channels(e):
                        at_least(pe, q_g[e % 2], 8 * 16, 16 * (e // 2 + 1))
                        if e:
                            at_least(pe, q_ue, NE, e)
                        for k in range(KD):
                            last = nc.tensor.transpose(psum[:, P * k:P * (k + 1)], ug[:, e % 2, P * k:P * (k + 1)], ident)
                        last.then_inc(q_tr, 1)

                    to_channels(0)
                    for i in range(NE + 1):
                        if i < NE:
                            at_least(pe, q_ue, NE, i + 1)
                            at_least(pe, s_we[i % NWE], 4 * 32, 32 * (i // NWE + 1))
                            if i >= 2:
                                at_least(pe, q_h, NE, i - 1)
                            for k in range(KD):
                                last = mm(bank(2 + i % 2), ue[:, i % 2, k, :], w_gu[:, i % NWE, k, :], start=(k == 0),
                                          stop=(k == KD - 1))
                            last.then_inc(q_gu, 1)
                        if i:
                            e = i - 1
                            at_least(pe, q_h, NE, e + 1)
                            if e:
                                at_least(pe, q_hte, NE, e)
                            for f in range(2):
                                last = nc.tensor.transpose(bank(4)[:, P * f:P * f + P], hh[:, P * f:P * f + P], ident)
                            last.then_inc(q_ht, 1)
                        if i + 1 < NE:
                            to_channels(i + 1)
                        if i:
                            e = i - 1
                            at_least(pe, q_hte, NE, e + 1)
                            if e:
                                at_least(pe, q_yo, NE, e)
                            for f in range(2):
                                for q in range(2):
                                    last = mm(bank(6 + q), hht[:, f, :], w_dn[:, e % NWE, f, 512 * q:512 * q + 512],
                                              start=(f == 0), stop=(f == 1))
                            last.then_inc(q_dn, 1)

                @block.scalar
                def _(act):
                    a = nc.scalar.activation
                    def rows_in(e):
                        at_least(act, q_tr, NE, e + 1)
                        a(ue[:, e % 2].rearrange("p k t -> p (k t)"), psum[:, 0:1024], ACT.Copy).then_inc(q_ue, 1)

                    rows_in(0)
                    for i in range(NE + 1):
                        if i < NE:
                            at_least(act, q_gu, NE, i + 1)
                            if i:
                                at_least(act, q_h, NE, i)
                            a(sig, bank(2 + i % 2, FF), ACT.Sigmoid).then_inc(q_sig, 1)
                        if i:
                            at_least(act, q_ht, NE, i)
                            a(hht.rearrange("p f t -> p (f t)"), bank(4, 256), ACT.Copy).then_inc(q_hte, 1)
                        if i + 1 < NE:
                            rows_in(i + 1)
                        if i:
                            e = i - 1
                            at_least(act, q_yo, NE, e + 1)
                            act.dma_start(y_view[:, e, :], yo[:, e % 2, :]).then_inc(q_yd[e % 2], 16)

                @block.vector
                def _(dve):
                    v = nc.vector

                    def tt(out, x, y, op, s):
                        v.tensor_tensor(out, x, y, op).then_inc(s, 1)

                    v.tensor_scalar(in_r[:, :, :], d_f[:, :, :], 0.0, None, ALU.is_ge).then_inc(q_dv, 1)
                    at_least(dve, q_dv, 6, 1)
                    v.tensor_tensor(cw_r[:, :, :], c_w[:, :, :], in_r[:, :, :], ALU.mult).then_inc(q_dv, 1)
                    at_least(dve, q_dv, 6, 2)
                    v.tensor_scalar(in_r[:, :, :], d_f[:, :, :], float(ROWS), None, ALU.is_lt).then_inc(q_dv, 1)
                    at_least(dve, q_dv, 6, 3)
                    v.tensor_tensor(cw_r[:, :, :], cw_r[:, :, :], in_r[:, :, :], ALU.mult).then_inc(q_dv, 1)
                    at_least(dve, q_dv, 6, 4)
                    v.tensor_scalar(dcl[:, :, :], d_f[:, :, :], 0.0, float(ROWS - 1), ALU.max, ALU.min)\
                        .then_inc(q_dv, 1)
                    at_least(dve, q_dv, 6, 5)
                    v.tensor_copy(d_i[:, :, :], dcl[:, :, :]).then_inc(q_ix, 1)
                    v.tensor_scalar(d_f[:, :, :], d_f[:, :, :], -float(ROWS), None, ALU.add).then_inc(q_dv, 1)
                    at_least(dve, q_dv, 6, 6)
                    for i in range(NE + 1):
                        if i < NE:
                            e = i
                            at_least(dve, q_sig, NE, e + 1)
                            if e:
                                at_least(dve, q_ht, NE, e)
                            b = bank(2 + e % 2)
                            tt(hh, b[:, 0:FF], sig, ALU.mult, q_h1)
                            at_least(dve, q_h1, NE, e + 1)
                            tt(hh, b[:, FF:2 * FF], hh, ALU.mult, q_h)
                        if i:
                            e = i - 1
                            at_least(dve, q_dn, NE, e + 1)
                            if e >= 2:
                                at_least(dve, q_yd[e % 2], 8 * 16, 16 * (e // 2))
                            v.tensor_copy(yo[:, e % 2, :], psum[:, 3072:4096]).then_inc(q_yo, 1)
                    for j in range(2 * TT):
                        t, i = j // 2, j % 2
                        n = rows_of(t)
                        at_least(dve, q_yg[j % 5], 32, 16 * (j // 5 + 1))
                        v.scalar_tensor_tensor(x2t[0:n, t, :], yg[0:n, j % 5, :], cw_r[0:n, i, t:t + 1], x2t[0:n, t, :],
                                               ALU.mult, ALU.add).then_inc(q_cb, 1)
                        if j < 2 * TT - 1:
                            at_least(dve, q_cb, 2 * TT, j + 1)

        z_ss = sem("z_ss")
        z_rt = sem("z_rt")
        z_rc = sem("z_rc")
        z_y = sem("z_y")
        z_out = sem("z_out")
        fs = E(nc.sbuf_tensor("fs", [P, 2 * TT], F32))
        with nc.Block() as block:
            @block.scalar
            def _(act):
                for t in range(TT):
                    n = rows_of(t)
                    nc.scalar.activation(ug[0:n, 0, :], x2t[0:n, t, :], ACT.Square, accum_out=fs[0:n, t:t + 1])\
                        .then_inc(z_ss, 1)
                    act.wait_ge(z_ss, t + 1)
                    nc.scalar.activation(fs[0:n, TT + t:TT + t + 1], fs[0:n, t:t + 1], ACT.Sqrt, scale=1.0 / D,
                                         bias=eps2[0:n, :]).then_inc(z_rt, 1)

            @block.vector
            def _(dve):
                v = nc.vector
                for t in range(TT):
                    n = rows_of(t)
                    dve.wait_ge(z_rt, t + 1)
                    v.reciprocal(fs[0:n, TT + t:TT + t + 1], fs[0:n, TT + t:TT + t + 1]).then_inc(z_rc, 1)
                    dve.wait_ge(z_rc, t + 1)
                    v.scalar_tensor_tensor(x2t[0:n, t, :], x2t[0:n, t, :], fs[0:n, TT + t:TT + t + 1], g_row[0:n, 1, :],
                                           ALU.mult, ALU.mult).then_inc(z_y, 1)

            @block.sync
            def _(sp):
                for t in range(TT):
                    n = rows_of(t)
                    sp.wait_ge(z_y, t + 1)
                    sp.dma_start(O["y"][t * P:t * P + n, :], x2t[0:n, t, :]).then_inc(z_out, 16)
                sp.wait_ge(z_out, 16 * TT)


def host_inputs(x):
    c = np.ascontiguousarray
    out = {}
    xs = np.concatenate([x["meta_tokens"], x["x_prompt"][0], x["x_sample"][:, 0]], 0)
    out["x"] = c(xs.T.reshape(KD, P, T).transpose(1, 0, 2))
    out["con"] = constants()
    vec = np.concatenate([x[n][0].reshape(-1, P) for n in ("norm1_g", "shift_mu", "decay_w0", "aaa_a0", "k_k", "k_a", "r_k", "lnx_w", "lnx_b", "norm2_g")], 0)
    out["vec"] = c(vec.T)
    out["sh0"] = c(x["state_shift"][0].reshape(8, 14, P).transpose(2, 1, 0))
    out["up_wa"] = c(np.concatenate([x["decay_up"][0], x["aaa_up"][0]], 0))
    out["up_g"] = c(x["gate_up"][0])
    def tiles(w):
        return c(w.reshape(w.shape[0] // P, P, w.shape[1] // P, P).transpose(2, 1, 0, 3))
    out["w_in"] = tiles(x["w_in"][0])
    out["w_bb"] = tiles(x["w_branch_b"][0])
    out["w_ba"] = tiles(x["w_branch_a"][0])
    out["w_out"] = tiles(x["w_out"][0])
    out["wkv0"] = c(x["state_wkv"][0].reshape(8, 4, 2, 64, 64).transpose(2, 4, 1, 0, 3).reshape(P, 4, 8, 64))
    out["rets0"] = c(x["state_ret"][0].transpose(2, 1, 0, 3))
    w = np.concatenate([x["expert_w_gate"][0], x["expert_w_up"][0]], 2)
    out["w_gu"] = c(w.reshape(16, KD, P, 512).transpose(0, 2, 1, 3).reshape(16, P, 4096))
    out["w_dn"] = c(x["expert_w_down"][0].reshape(16, 2, P, D).transpose(0, 2, 1, 3).reshape(16, P, 2048))
    out["w_r"] = c(np.concatenate([x["router_group_w"][0], x["router_expert_w"][0]], 1).reshape(KD, P, 20).transpose(1, 0, 2))
    out["b_r"] = c(np.broadcast_to(np.concatenate([x["router_group_b"][0], x["router_expert_b"][0]]), (P, 20)))
    out["g2row"] = c(np.broadcast_to(x["norm2_g"][0], (P, D)))
    out["gfrow"] = c(np.broadcast_to(x["final_norm_g"], (P, D)))
    return out

def host_outputs(o):
    r = {}
    r["wkvp"] = o["wkvp"].reshape(2, 64, 4, 64).transpose(2, 0, 3, 1).reshape(1, 1, 8, 64, 64)
    r["wkvs"] = o["wkvs"].reshape(2, 64, 4, 8, 64).transpose(3, 2, 0, 4, 1).reshape(1, 8, 8, 64, 64)
    sh = o["shift"].transpose(2, 1, 0).reshape(9, 14 * P)
    r["shiftp"], r["shifts"] = sh[0].reshape(1, 1, -1), sh[1:].reshape(1, 8, -1)
    r["retp"] = o["retp"].transpose(1, 0, 2)[None, None]
    r["rets"] = o["rets"].transpose(2, 1, 0, 3)[None]
    return r


OUTS = {"y": (T, D), "wkvp": (P, NP, 64), "shift": (P, SHIFT_TILES, 9), "retp": (P, RH, P),
        "wkvs": (P, NP, NB, 64), "rets": (P, RH, NB, P)}


def kernel(**inputs):
    import concourse.bacc as bacc
    from concourse.bass_utils import run_bass_kernel_spmd

    nc = bacc.Bacc("TRN2", target_bir_lowering=False, num_devices=1)
    arrays = host_inputs({n: np.asarray(a) for n, a in inputs.items()})
    ins = {n: nc.dram_tensor(f"in_{n}", a.shape, F32, kind="ExternalInput").ap() for n, a in arrays.items()}
    outs = {n: nc.dram_tensor(f"out_{n}", s, F32, kind="ExternalOutput").ap() for n, s in OUTS.items()}
    hybrid_step(nc, ins, outs)
    r = run_bass_kernel_spmd(nc, [{f"in_{n}": a for n, a in arrays.items()}], core_ids=[0]).results[0]
    o = host_outputs({n: r[f"out_{n}"] for n in OUTS})
    y = r["out_y"]
    return (y[None, META:TP], y[TP:T, None], o["wkvp"], o["shiftp"], o["retp"], o["wkvs"], o["shifts"], o["rets"])
```

```python
import math
from contextlib import ExitStack

import numpy as np
import concourse.bass as bass
from concourse import mybir

F32 = mybir.dt.float32
I32 = mybir.dt.int32
BF16 = mybir.dt.bfloat16
ALU = mybir.AluOpType
ACT = mybir.ActivationFunctionType
AX = mybir.AxisListType

P = 128
D = 1024
KD = D // P
META, SEQ, NB = 16, 512, 8
TP = META + SEQ
T = TP + NB
HT = T // 2
PAST = 4096
NP = 4
RH = 4
C = 64
CHUNKS = [(c * C, min(C, TP - c * C)) for c in range((TP + C - 1) // C)]
LEVELS = [1, 2, 4, 8, 16, 32]
DECAY = math.exp(-0.5)
EPS = 1e-6
LNX_EPS = 64e-5
NE, NG, EPG, FF = 16, 4, 4, 256
SLOTS = P
TT = (T + P - 1) // P
LASTT = T - (TT - 1) * P
ROUNDS = (T + SLOTS - 1) // SLOTS
ROWS = NE * SLOTS
SHIFT_TILES = 14
RET0, GA0, GB0 = 14, 30, 38

VEC = {}
_n = 0
for _name, _w in [("norm1_g", KD), ("mu", SHIFT_TILES), ("w0", NP), ("a0", NP), ("kk", NP), ("ka", NP),
                  ("rk", NP), ("lnw", NP), ("lnb", NP), ("norm2_g", KD)]:
    VEC[_name] = _n
    _n += _w
NVEC = _n

CON = {}
_n = 0
for _name, _w in [("ident", P), ("bones", P), ("ones", P), ("tri", P), ("reset", TP), ("lev", len(LEVELS) * C),
                  ("lev0t", C), ("eye", C), ("ai", 2 * C), ("tie", 16), ("expert", NE),
                  ("valid", TT), ("slot", SLOTS), ("more", ROUNDS - 1), ("part", 1), ("tile", TT),
                  ("perm", P), ("smask", NB), ("cos", T), ("sin", T), ("dec", RH * TP), ("dend", TT * RH)]:
    CON[_name] = (_n, _w)
    _n += _w
NCON = _n
NKEEP = CON["perm"][0]
NFIRST = CON["ones"][0] + P


def constants():
    t = np.zeros((P, NCON), np.float32)

    def put(name, a):
        o, w = CON[name]
        a = np.asarray(a, np.float32).reshape(a.shape[0], -1)
        t[:a.shape[0], o:o + w] = a

    p = np.arange(P)
    put("ident", np.eye(P))
    put("bones", (p[:, None] // 64 == p[None] // 64))
    put("ones", np.ones((P, P)))
    perm = np.zeros((P, P))
    for i in range(P // 2):
        perm[2 * i + 1, 2 * i] = -1
        perm[2 * i, 2 * i + 1] = 1
    put("perm", perm)
    put("tri", p[:, None] < p[None])
    pos = np.concatenate([np.arange(TP), np.full(NB, PAST)]).astype(np.float32)
    inv = np.float32(10000.0) ** (-np.arange(64, dtype=np.float32) / np.float32(64))
    ang = (pos[None] * inv[p // 2][:, None]).astype(np.float32)
    put("cos", np.cos(ang))
    put("sin", np.sin(ang))
    lg = np.log(1.0 - 2.0 ** (-5.0 - np.arange(RH)))
    diff = np.arange(TP)[None] - p[:, None]
    put("dec", np.stack([np.where(diff >= 0, np.exp(np.maximum(diff, 0) * g), 0) for g in lg], 1))
    tok = np.arange(TT)[None, :] * P + p[:, None]
    put("dend", np.stack([np.where(tok < TP, np.exp(np.maximum(TP - 1 - tok, 0) * g), 0) for g in lg], 2))
    put("reset", np.broadcast_to(np.arange(TP) % C != 0, (P, TP)))
    row, col = p % 64, np.arange(C)

    def half(b, r, c):
        return (r // (2 * b) == c // (2 * b)) & (r // b % 2 == 1) & (c // b % 2 == 0)

    put("lev", np.stack([half(b, row[:, None], col[None]) for b in LEVELS], 1))
    put("lev0t", half(1, col[None], row[:, None]))
    put("eye", row[:, None] == col[None])
    strict, incl = row[:, None] < col[None], row[:, None] <= col[None]
    put("ai", np.stack([strict, incl], 1))
    put("smask", (p[:, None] - META == np.arange(NB)[None]))
    put("tie", np.broadcast_to((np.arange(4)[None] < np.arange(4)[:, None]).reshape(-1), (P, 16)))
    put("valid", tok < T)
    put("slot", np.broadcast_to(np.arange(SLOTS), (P, SLOTS)))
    put("part", p[:, None])
    put("more", np.broadcast_to(np.arange(1, ROUNDS) * SLOTS, (P, ROUNDS - 1)))
    put("tile", np.broadcast_to(np.arange(TT) * P, (P, TT)))
    put("expert", np.broadcast_to(np.arange(NE), (P, NE)))
    return t


GAMMA = [float(1.0 - 2.0 ** (-5.0 - h)) for h in range(RH)]

RB = []
for _h in range(RH):
    for _r in range(2):
        _js = [j for j in range(TT) if j * P < (_r + 1) * (TP // 2)]
        for _j in _js:
            _i0 = max(_r * (TP // 2), _j * P)
            RB.append((_h, _r, _j, _i0, (_r + 1) * (TP // 2), _j == _js[0], _j == _js[-1]))


PARTS = {"j_proj": 4, "j_bb": 2}


def order():
    def proj(m):
        return [("j_proj", m, 0), ("j_proj", m, 1)]

    s = [("sq", 0), ("j_norm", 0, 0), ("sq", 1), ("j_proj", RET0, 0), ("j_norm", 0, 1), ("j_proj", RET0 + 1, 0),
         ("j_proj", RET0, 1), ("j_proj", RET0 + 1, 1)]
    for j in range(12):
        if j > 1:
            s += proj(RET0 + j)
        if 1 <= j <= 8:
            s += [("j_rope", j - 1, 0), ("j_rope", j - 1, 1)]
    s += [("j_vt", t) for t in range(TT)] + [("j_kt", t) for t in range(TT)]
    for h in range(RH):
        s += [("rs_v", h), ("j_proj", RET0 + 12 + h, 0), ("rs_a", h), ("j_proj", RET0 + 12 + h, 1), ("rs_b", h)]
    s += [("j_ros", h) for h in range(RH)] + [("j_rst", h) for h in range(RH)]
    for n in range(len(RB)):
        s.append(("j_score", n))
        if n:
            s.append(("att", n - 1))
    s += [("att", len(RB) - 1)] + [("osq", h) for h in range(RH)] + [("phase2",)]
    for n, m in enumerate([12, 13, 4, 5, 6, 7, 0, 1, 2, 3, 8, 9, 10, 11]):
        s += proj(m)
        if n < RH:
            s += [("j_orms", n, 0), ("j_orms", n, 1)]
        if n == 1:
            s += [("lora_in",)]
        if 3 <= n <= 6:
            s += [("j_lora", k, n - 3, hf) for k in ("w", "a") for hf in range(2)]
        if 5 <= n <= 8:
            s += [("kk_in", n - 5)]
        if 6 <= n <= 9:
            s += [("j_kkn", n - 6, 0), ("j_kkn", n - 6, 1)]
        if 7 <= n <= 10:
            s += [("j_lora", "g", n - 7, hf) for hf in range(2)]
        if 8 <= n <= 11:
            s += [("bon_in", n - 8)]
    fill = []

    def parts(st, n):
        return [("pre", st, i) for i in range(n - 1)] + [st]

    for m in range(8):
        for st in proj(GB0 + m):
            fill += parts(st, PARTS["j_proj"])
        for hf in range(2):
            fill += parts(("j_bb", m, hf), PARTS["j_bb"])
    for m in range(8):
        for st in proj(GA0 + m):
            fill += parts(st, PARTS["j_proj"])
    small = []
    budget = [0]

    def take(n=1):
        out = []
        for _ in range(n):
            if fill:
                out.append(fill.pop(0))
            if small and budget[0] and (not fill or fill[0][0] == "pre" and fill[0][2] == 0):
                out.append(small.pop(0))
                budget[0] -= 1
        return out

    def whole():
        out = []
        while fill and not (fill[0][0] == "pre" and fill[0][2] == 0):
            out += take()
        return out

    for p in range(NP):
        s += [("j_bon", p, 0), ("j_bon", p, 1)]
    for p in range(NP):
        small += [("sm_in", p), ("j_sk", p), ("j_sv", p), ("sm_y", p), ("j_sy", p)]
    s += [("wk_prep", 0)] + take(8)
    for c, (_, w) in enumerate(CHUNKS):
        budget[0] = [0, 3, 3, 3, 3, 4, 4, 4, 4][c]
        if c == 6:
            small += [(k, p, 0) for k in ("j_mean", "j_var") for p in range(NP)]
        s += [("wk_a", c)] + take(3)
        if c + 1 < len(CHUNKS):
            s += [("wk_prep", c + 1)]
        for b in LEVELS[1:]:
            if b < w:
                s += [("wk_x", c, b)] + take(1) + [("wk_t", c, b)]
                if b == 2:
                    s += [("wk_k", c)]
                s += take(1)
        s += [("wk_r", c)] + take(1) + [("wk_sa", c)] + take(1) + [("wk_s", c)]
        s += take(1)
    s += whole()
    budget[0] = len(small)
    s += small
    small[:] = []
    ba = [("j_ba", m, 0) for m in range(8)]
    for p in range(NP):
        s += [("j_mean", p, 1)] + take(PARTS["j_proj"])
    s += [("j_var", 0, 1)] + fill
    fill[:] = []
    for p in range(1, NP):
        s += [ba.pop(0), ("j_var", p, 1)]
    s += ba
    s += [("j_ba", m, 1) for m in range(8)] + [("rt_in",)]
    for m in range(8):
        s += [("j_out", m, 0)] + ([("tok", 0, m - 1)] if m else [])
    s += [("j_out", 0, 1), ("tok", 0, 7), ("x2", 0)]
    for m in range(1, 8):
        s += [("j_out", m, 1)]
        if m >= 3:
            s += [("tok", 1, k) for k in (range(3) if m == 3 else [m - 1])]
    s += [("tok", 1, 7), ("tok4",), ("route",)]
    return s


STEPS = order()
JOBS = {s: n for n, s in enumerate([s for s in STEPS if s[0].startswith("j_")])}
KINDS = {"j_proj": "in", "j_bb": "bb"}
WTILES = []
for _s in STEPS:
    if _s[0] in ("j_proj", "j_bb") and _s[2] == 0:
        WTILES.append((_s[0], _s[1], (0, 1)))
WIDX = {(k, m, h): n for n, (k, m, hs) in enumerate(WTILES) for h in hs}
NW = 3


def bank_of(step):
    return JOBS[step] % 2


def hybrid_step(nc, I, O):
    with ExitStack() as ctx:
        E = ctx.enter_context
        sem_names = set()

        def sem(name):
            assert name not in sem_names
            sem_names.add(name)
            return E(nc.semaphore(name))

        NARENA = 52020
        arena = E(nc.sbuf_tensor("arena", [P, NARENA], F32))
        top = [0]

        def at(n, *dims, start=None):
            if start is None:
                start = top[0]
                top[0] += n
            assert start + n <= NARENA, (start, n)
            a = arena[:, start:start + n]
            if len(dims) == 2:
                return a.rearrange("p (a b) -> p a b", a=dims[0])
            if len(dims) == 3:
                return a.rearrange("p (a b c) -> p a b c", a=dims[0], b=dims[1])
            if len(dims) == 4:
                return a.rearrange("p (a b c d) -> p a b c d", a=dims[0], b=dims[1], c=dims[2])
            return a

        con = at(NKEEP)
        vec = at(NVEC)
        up_wa = at(512)
        up_g = at(512)
        u = at(KD * T, KD, T)
        u_end = top[0]
        wt = at(NW * 1024, NW, 8, P)
        ret_o = at(RH * T, RH, T)
        tmp = at(4 * T, 4, T)
        base = top[0]
        con1 = at(NCON - NKEEP)
        ret = at(16 * T, 16, T)
        v_tok = at(TT * 512, TT, RH, P)
        k_tok = at(TT * 512, TT, RH, P)
        k_smp = at(512, RH, P)
        sc = at(3 * HT, 3, HT)
        vb = at(1024, NB, P)
        s_new = at(RH * 1024, RH, NB, P)
        o_smp = at(512, RH, P)
        o_diag = at(1024, NB, P)
        ret_st = at(512, RH, P)
        top1 = top[0]
        top[0] = base
        r_f = at(NP * T, NP, T)
        k_f = at(NP * T, NP, T)
        v_f = at(NP * T, NP, T)
        wad = at(T)
        gd = at(T)
        b_f = at(NP * T, NP, T)
        kk_f = at(NP * T, NP, T)
        w_out = at(KD * KD * P, KD, KD, P, start=base)
        ly = at(NP * T, NP, T)
        g_f = at(NP * T, NP, T)
        bon = at(NP * T, NP, T)
        dif = bon[:, 3, :]
        raw0 = top[0]
        raw = at(2 * (T + 1), 2, T + 1)
        top[0] = raw0
        ep = at(2 * NP * (C + 1), 2, NP, C + 1)
        en = at(NP * C, NP, C)
        ar = at(2 * NP * 2 * C, 2, NP, 2, C)
        bk = at(2 * 2 * NP * C, 2, 2, NP, C)
        bkp = at(2 * NP * C, 2, NP, C)
        tp = at(2 * NP * C, 2, NP, C)
        ab = at(NP * 2 * C, NP, 2, C)
        kq = at(NP * 2 * C, NP, 2, C)
        tok = at(3 * NP * C, 3, NP, C)
        xl = at(NP * C, NP, C)
        rr = at(NP * C, NP, C)
        sa = at(NP * C, NP, C)
        st = at(2 * NP * C, 2, NP, C)
        stp = at(NP * C, NP, C)
        w_ba = at(KD * NP * P, KD, NP, P, start=raw0)
        ws = at(2048, NP, NB, 64)
        t1 = at(512, NB, 64)
        t2 = at(512, NB, 64)
        wsmp = at(NP * NB, NP, NB)
        mg0 = top[0]
        merged = at(KD * T, KD, T)
        sga = at(KD * T, KD, T)
        sh = at(SHIFT_TILES * 9, SHIFT_TILES, 9)
        eps = at(1)
        lnx_eps = at(1)
        dummy = at(1)
        shs = at(SHIFT_TILES * NB, SHIFT_TILES, NB)
        shd = at(SHIFT_TILES * NB, SHIFT_TILES, NB)

        def cc(name, *dims, rows=P):
            o, w = CON[name]
            a = con[0:rows, o:o + w] if o < NKEEP else con1[0:rows, o - NKEEP:o - NKEEP + w]
            if len(dims) == 2:
                return a.rearrange("p (a b) -> p a b", a=dims[0])
            if len(dims) == 3:
                return a.rearrange("p (a b c) -> p a b c", a=dims[0], b=dims[1])
            return a

        def vv(name, i):
            o = VEC[name] + i
            return vec[:, o:o + 1]

        ident, bones, ones, perm = cc("ident"), cc("bones"), cc("ones"), cc("perm")

        psum = E(nc.psum_tensor("psum", [P, 4096], F32))

        def bank(b, n=512, rows=P):
            return psum[0:rows, 512 * b:512 * b + n]

        s_load = sem("s_load")
        s_load2 = sem("s_load2")
        s_x = [[sem(f"s_xin{hf}_{i}") for i in range(KD // 2)] for hf in range(2)]
        s_w = [sem(f"s_w{i}") for i in range(NW)]
        s_job = sem("s_job")
        s_free = [sem(f"s_free{i}") for i in range(2)]
        s_act = sem("s_act")
        s_dve = sem("s_dve")
        s_sq = sem("s_sq")
        s_sqa = sem("s_sqa")
        s_eps = sem("s_eps")
        s_dum = sem("s_dum")
        s_u = sem("s_u")
        s_raw = sem("s_raw")
        s_shift = sem("s_shift")
        s_sig = sem("s_sig")
        s_kq = sem("s_kq")
        s_vb = sem("s_vb")
        s_rsp = sem("s_rsp")
        s_sn = sem("s_sn")
        s_roq = sem("s_roq")
        s_od = sem("s_od")
        s_osq = sem("s_osq")
        s_on = sem("s_on")
        s_ys = sem("s_ys")
        s_ph = sem("s_ph")
        s_ws = sem("s_ws")
        s_att = sem("s_att")
        s_atf = [sem(f"s_atf{i}") for i in range(2)]
        s_lin = sem("s_lin")
        s_kkt = sem("s_kkt")
        s_bont = sem("s_bont")
        s_e = sem("s_e")
        s_ab = sem("s_ab")
        s_abp = sem("s_abp")
        s_pab = sem("s_pab")
        s_tri = sem("s_tri")
        s_toks = sem("s_toks")
        s_px = sem("s_px")
        s_xl = sem("s_xl")
        s_pt = sem("s_pt")
        s_tt = sem("s_tt")
        s_pr = sem("s_pr")
        s_rr = sem("s_rr")
        s_psa = sem("s_psa")
        s_sa = sem("s_sa")
        s_ps = sem("s_ps")
        s_st = sem("s_st")
        s_y = sem("s_y")
        s_sw = sem("s_sw")
        s_sld = sem("s_sld")
        s_smt = sem("s_smt")
        s_vsd = sem("s_vsd")
        s_ya = sem("s_ya")
        s_mg = sem("s_mg")
        s_xr = sem("s_xr")
        s_out = sem("s_out")
        s_rets = sem("s_rets")

        def job(step):
            return JOBS[step]

        def job_done(eng, step):
            eng.wait_ge(s_job, JOBS[step] + 1)

        def job_read(eng, step):
            n = JOBS[step]
            eng.wait_ge(s_free[n % 2], n // 2 + 1)

        def job_ps(step, n=HT, rows=P):
            return bank(JOBS[step] % 2, n, rows)

        def cols(hf):
            return slice(hf * HT, (hf + 1) * HT)

        NCH = len(CHUNKS)
        NLEV = [sum(1 for b in LEVELS[1:] if b < w) for _, w in CHUNKS]
        LEV0 = [sum(NLEV[:c]) for c in range(NCH)]

        def wk(c, s):
            t0, w = CHUNKS[c]
            return t0, w, slice(64 * s, 64 * s + 64), slice(64 * s, 64 * s + w)

        def bc(a, n):
            return a.unsqueeze(len(a.shape)).broadcast_to(list(a.shape) + [n])

        def pairs(a):
            return a.unsqueeze(1).broadcast_to([a.shape[0], NP] + list(a.shape[1:]))

        NWE = 4
        a0, a1 = base + KD * KD * P, base + KD * KD * P + 6144
        we = [at(6144, start=x) for x in (a0, a1, base, mg0)]
        assert a0 + 6144 * 2 <= raw0 + 4096
        w_gu = [x[:, 0:4096].rearrange("p (k f) -> p k f", k=KD) for x in we]
        w_dn = [x[:, 4096:6144].rearrange("p (f d) -> p f d", f=2) for x in we]
        x2t = at(TT * D, TT, D, start=raw0 + 4096)
        top[0] = a1 + 6144
        sig = at(FF)
        hh = at(FF)
        hht = at(2 * P, 2, P)
        assert top[0] <= raw0 + 4096
        yo = at(2 * D, 2, D, start=base + 6144)
        assert base + 6144 + 2 * D <= a0
        junk = at(D, start=mg0 + 6144)
        assert mg0 + 6144 + D <= mg0 + 2 * KD * T
        top[0] = mg0 + 6144 + D
        NS = TT * (1 + NG)
        rank = at(NS * 4, NS, 4)
        ex = at(NS * 4, NS, 4)
        exs = at((NS - TT) * 4, NS - TT, 4)
        sel = at((NS - TT) * 4, NS - TT, 4)
        sm = at(NS)
        ga = at(TT * 4, TT, 4)
        gw = at(TT * 4, TT, 4)
        ff = at(2 * TT * NE, 2, TT, NE)
        wts = at(TT * NE, TT, NE)
        tq = at(2 * TT * NE, 2, TT, NE)
        ei = at(2 * TT, 2, TT)
        assert top[0] <= mg0 + 2 * KD * T
        top[0] = u_end
        g_row = at(D)
        ug0 = top[0]
        ug = at(2 * D, 2, D)
        ue = at(2 * D, 2, KD, P)
        NYG = 4
        yg = at(NYG * D, NYG, D, start=ug0)
        top[0] = ug0
        wr = at(KD * 20, KD, 20)
        logt = at(T)
        bias = at(20)
        lg = at(TT * 20, TT, 20)
        ll = at(NS * 4, NS, 4)
        gt = at(NS * 16, NS, 4, 4)
        eq = at(NS * 16, NS, 4, 4)
        mx = at(NS)
        ssq = at(TT)
        rstd = at(TT)
        cnt = at(8)
        u2b = at(2 * D, 2, D)
        assert top[0] <= base, top[0] - base
        oneb = E(nc.sbuf_tensor("oneb", [P, P], BF16))
        trib = E(nc.sbuf_tensor("trib", [P, P], BF16))
        selb = E(nc.sbuf_tensor("selb", [P, TT, NE], BF16))
        toke = E(nc.sbuf_tensor("toke", [P, 2, 2, TT, NE], BF16))
        onehot = E(nc.sbuf_tensor("onehot", [P, 2 * TT, SLOTS], BF16))
        d_i = E(nc.sbuf_tensor("d_i", [P, 2, TT], I32))
        c_w = E(nc.sbuf_tensor("c_w", [P, 2, TT], F32))
        place = E(nc.sbuf_tensor("place", [P, 2, TT], F32))
        d_f = E(nc.sbuf_tensor("d_f", [P, 2, TT], F32))
        in_r = E(nc.sbuf_tensor("in_r", [P, 2, TT], F32))
        cw_r = E(nc.sbuf_tensor("cw_r", [P, 2, TT], F32))
        dcl = E(nc.sbuf_tensor("dcl", [P, 2, TT], F32))
        n_rounds = E(nc.sbuf_tensor("n_rounds", [P, 1], I32))
        ids = E(nc.sbuf_tensor("ids", [P, NE], I32))
        eps2 = E(nc.sbuf_tensor("eps2", [P, 1], F32))
        fs = E(nc.sbuf_tensor("fs", [P, 2 * TT], F32))

        u2_dram = nc.dram_tensor("u2_rows", [T, D], F32, kind="Internal").ap()
        y_dram = nc.dram_tensor("y_rows", [ROWS, D], F32, kind="Internal").ap()
        y_view = y_dram.rearrange("(p e) d -> p e d", e=NE)

        s_ba = sem("s_ba")
        s_wo = [sem(f"s_wo{i}") for i in range(2)]
        s_we = [sem(f"s_we{i}") for i in range(NWE)]
        d_ld = sem("d_ld")
        d_wr = sem("d_wr")
        d_lt = sem("d_lt")
        d_ltc = sem("d_ltc")
        d_lg = sem("d_lg")
        d_x = sem("d_x")
        d_xc = sem("d_xc")
        d_ss = sem("d_ss")
        d_rt = sem("d_rt")
        d_rc = sem("d_rc")
        d_ll = sem("d_ll")
        d_ex = sem("d_ex")
        d_u2 = sem("d_u2")
        d_u2w = [sem(f"d_u2w{i}") for i in range(2)]
        d_sel = sem("d_sel")
        d_pos = sem("d_pos")
        d_n = sem("d_n")

        def rows_of(t):
            return LASTT if t == TT - 1 else P

        def u2_rows(t):
            return (yo if t // 2 == 1 else u2b)[0:rows_of(t), t % 2, :]

        def load_expert(eng, e):
            eng.dma_start(we[e % NWE][:, 0:4096], I["w_gu"][e]).then_inc(s_we[e % NWE], 16)
            eng.dma_start(we[e % NWE][:, 4096:6144], I["w_dn"][e]).then_inc(s_we[e % NWE], 16)

        def route(dve, v, run, tt):
            dve.wait_ge(d_rt, 2)
            run(v.reciprocal(rstd[:, 2:TT], rstd[:, 2:TT]), d_rc)
            dve.wait_ge(d_lg, 1)
            for t in range(TT):
                n = rows_of(t)
                run(v.scalar_tensor_tensor(lg[0:n, t, :], bank(6, 512, n)[:, 20 * t:20 * t + 20], rstd[0:n, t:t + 1],
                                           bias[0:n], ALU.mult, ALU.add))
            run(v.tensor_copy(ll[:, 0:TT, :], lg[:, :, 0:4]))
            run(v.tensor_copy(ll[:, TT:NS, :].rearrange("p (t g) e -> p t (g e)", t=TT), lg[:, :, 4:20]))
            run(v.tensor_reduce(mx, ll, AX.X, ALU.max))
            me = bc(ll, 4)
            other = ll.unsqueeze(2).broadcast_to([P, NS, 4, 4])
            tt(gt, other, me, ALU.is_gt)
            tt(eq, other, me, ALU.is_equal)
            tt(ll, ll, bc(mx, 4), ALU.subtract, s=d_ll)
            tt(eq, eq, cc("tie", 4, 4).unsqueeze(1).broadcast_to([P, NS, 4, 4]))
            tt(gt, gt, eq, ALU.add)
            run(v.tensor_reduce(rank, gt, AX.X, ALU.add))
            run(v.tensor_scalar(ga, rank[:, 0:TT, :], 0.5, None, ALU.is_lt))
            tt(ga, ga, bc(cc("valid"), 4))
            gax = bc(ga.rearrange("p t g -> p (t g)"), 4)
            for i in range(2):
                fv = ff[:, i].rearrange("p t (g e) -> p (t g) e", g=NG)
                run(v.scalar_tensor_tensor(fv, rank[:, TT:NS, :], float(i), gax, ALU.is_equal, ALU.mult))
            tt(selb[:, :, :], ff[:, 0], ff[:, 1], ALU.add, s=d_sel)
            run(v.tensor_scalar(toke[:, 0], ff, cc("part"), None, ALU.mult))
            tt(toke[:, 1], ff, bc(cc("tile"), NE).unsqueeze(1).broadcast_to([P, 2, TT, NE]))
            dve.wait_ge(d_pos, 1)
            tt(tq, ff, bank(7, NE * TT).rearrange("p (t e) -> p t e", t=TT).unsqueeze(1).broadcast_to([P, 2, TT, NE]))
            run(v.tensor_reduce(place[:, :, :], tq, AX.X, ALU.add))
            run(v.tensor_reduce(cnt[:, 0:1], bank(7)[:, NE * TT:NE * TT + NE], AX.X, ALU.max))
            tt(cnt[:, 1:ROUNDS], cnt[:, 0:1].broadcast_to([P, ROUNDS - 1]), cc("more"), ALU.is_gt)
            run(v.tensor_reduce(cnt[:, 6:7], cnt[:, 1:ROUNDS], AX.X, ALU.add))
            run(v.tensor_scalar(n_rounds[:, :], cnt[:, 6:7], 1.0, None, ALU.add), d_n)

        mixer = nc.Block()
        block = mixer.__enter__()

        @block.sync
        def _(sp):
            def half_of_x(hf):
                for k in range(0, KD, 2):
                    sp.dma_start(u[:, k:k + 2, cols(hf)], I["x"][:, k:k + 2, cols(hf)]).then_inc(s_x[hf][k // 2], 16)

            half_of_x(0)
            sp.dma_start(con[:, 0:NFIRST], I["con"][:, 0:NFIRST]).then_inc(s_load, 16)
            sp.dma_start(vec, I["vec"]).then_inc(s_load, 16)

            def tables():
                for dst, src in ((con[:, NFIRST:NKEEP], I["con"][:, NFIRST:NKEEP]), (con1, I["con"][:, NKEEP:NCON]), (shs, I["sh0"]), (up_wa, I["up_wa"]),
                                 (up_g, I["up_g"])):
                    sp.dma_start(dst, src).then_inc(s_load2, 16)


            def weights(i):
                kind, m, _ = WTILES[i]
                if i >= NW:
                    k0, m0, h0 = WTILES[i - NW]
                    job_done(sp, (k0, m0, h0[-1]))
                nk = KD if kind == "j_proj" else NP
                sp.dma_start(wt[:, i % NW, 0:nk, :], I["w_" + KINDS[kind]][m]).then_inc(s_w[i % NW], 16)

            for i in range(len(WTILES)):
                if i == 1:
                    half_of_x(1)
                if i == 2:
                    tables()
                if i == NW:
                    sp.dma_start(s_new, I["rets0"]).then_inc(s_rets, 16)
                if i == 16 + NW:
                    sp.wait_ge(s_sn, RH)
                    sp.wait_ge(s_roq, RH)
                    sp.dma_start(O["rets"], s_new).then_inc(s_out, 16)
                    for h in range(RH):
                        job_read(sp, ("j_rst", h))
                    sp.dma_start(O["retp"], ret_st).then_inc(s_out, 16)
                if i == 16 + 8:
                    sp.wait_ge(s_ph, 1)
                    sp.dma_start(ws, I["wkv0"]).then_inc(s_sld, 16)
                weights(i)
            sp.wait_ge(s_st, NCH + 1)
            sp.wait_ge(s_ps, 2 * NCH)
            sp.dma_start(w_ba, I["w_ba"].rearrange("m p k c -> p m k c")).then_inc(s_ba, 16)
            sp.dma_start(O["wkvp"], st[:, NCH % 2]).then_inc(s_out, 16)
            sp.wait_ge(s_raw, SHIFT_TILES)
            sp.dma_start(O["shift"], sh).then_inc(s_out, 16)
            sp.wait_ge(s_ws, NP)
            sp.dma_start(O["wkvs"], ws).then_inc(s_out, 16)
            sp.wait_ge(s_ys, NP)
            for i in range(2):
                m = slice(4 * i, 4 * i + 4)
                sp.dma_start(w_out[:, m], I["w_out"][m].rearrange("m p k c -> p m k c")).then_inc(s_wo[i], 16)
                if i == 0:
                    for q in range(2):
                        job_done(sp, ("j_proj", GA0 + 7, q))
                    sp.dma_start(u, I["x"]).then_inc(s_xr, 16)
                    for dst, src in ((wr, I["w_r"]), (bias, I["b_r"])):
                        sp.dma_start(dst, src).then_inc(d_ld, 16)
            sp.wait_ge(s_out, 16 * 5)
            for hf in range(2):
                job_read(sp, ("j_ba", 7, hf))
            sp.dma_start(g_row, I["gfrow"]).then_inc(d_ld, 16)
            for e in range(2):
                load_expert(sp, e)

        @block.tensor
        def _(pe):
            mm = nc.tensor.matmul

            def open_job(step):
                n = JOBS[step]
                if n >= 2:
                    pe.wait_ge(s_free[n % 2], n // 2)
                return job_ps(step)

            def products(step, nk, rhs, part=None):
                kind, m, hf = step
                np_ = PARTS.get(kind)
                ps = job_ps(step) if part else open_job(step)
                i = WIDX[step]
                if hf == WTILES[i][2][0] and not part:
                    pe.wait_ge(s_w[i % NW], 16 * (i // NW + 1))
                for k in range(nk) if part is None else range(part * nk // np_, (part + 1) * nk // np_):
                    if step == ("j_proj", RET0, 0):
                        pe.wait_ge(s_u, k + 1)
                    if step == ("j_proj", RET0, 1):
                        pe.wait_ge(s_u, KD + k + 1)
                    last = mm(ps, wt[:, i % NW, k, :], rhs[:, k, cols(hf)], start=(k == 0), stop=(k == nk - 1))
                if part is None or part == np_ - 1:
                    last.then_inc(s_job, 1)

            pe.wait_ge(s_load, 32)
            halved = [s_[1] for s_ in STEPS if s_[0] == "pre"]
            for step in STEPS:
                kind = step[0]
                if kind == "j_norm":
                    ps = open_job(step)
                    for k in range(KD):
                        pe.wait_ge(s_sq if k % 2 == 0 else s_sqa, KD // 2 * step[2] + k // 2 + 1)
                        last = mm(ps, ones, merged[:, k, cols(step[2])], start=(k == 0), stop=(k == KD - 1))
                    last.then_inc(s_job, 1)
                elif kind == "j_proj":
                    products(step, KD, u, PARTS[kind] - 1 if step in halved else None)
                elif kind == "pre":
                    if step[1] == ("j_bb", 0, 0):
                        pe.wait_ge(s_on, RH)
                    _, whole_step, part = step
                    products(whole_step, *((KD, u) if whole_step[0] == "j_proj" else (NP, ret_o)), part)
                elif kind == "j_rope":
                    _, j, hf = step
                    if j == 0:
                        pe.wait_ge(s_load2, 80)
                    job_read(pe, ("j_proj", RET0 + j, hf))
                    ps = open_job(step)
                    mm(ps, perm, ret[:, j, cols(hf)], start=True, stop=True).then_inc(s_job, 1)
                elif kind in ("j_vt", "j_kt"):
                    t = step[1]
                    n = LASTT if t == TT - 1 else P
                    open_job(step)
                    ps = bank(bank_of(step), 512, n)
                    if kind == "j_vt":
                        job_read(pe, ("j_proj", RET0 + 11, 0))
                        job_read(pe, ("j_proj", RET0 + 11, 1))
                    else:
                        pe.wait_ge(s_kq, 16)
                    for h in range(RH):
                        src = ret[:, (8 if kind == "j_vt" else 4) + h, t * P:t * P + n]
                        last = nc.tensor.transpose(ps[:, h * P:(h + 1) * P], src, ident)
                    last.then_inc(s_job, 1)
                elif kind == "rs_a":
                    h = step[1]
                    pe.wait_ge(s_vb, h + 1)
                    if h:
                        pe.wait_ge(s_sn, h)
                    job_read(pe, ("j_kt", TT - 1))
                    for q in range(2):
                        last = mm(bank(4 + q), k_smp[0:LASTT, h, :], vb[0:LASTT, 4 * q:4 * q + 4, :],
                                  start=True, stop=True)
                    last.then_inc(s_rsp, 1)
                elif kind == "rs_b":
                    h = step[1]
                    pe.wait_ge(s_sn, h + 1)
                    if h:
                        pe.wait_ge(s_od, h)
                    for q in range(2):
                        last = mm(bank(6 + q, 512, NB), ret[:, h, TP:T], s_new[:, h, 4 * q:4 * q + 4, :],
                                  start=True, stop=True)
                    last.then_inc(s_roq, 1)
                elif kind == "j_ros":
                    h = step[1]
                    open_job(step)
                    pe.wait_ge(s_od, h + 1)
                    mm(job_ps(step, NB), o_smp[0:NB, h, :], ident[0:NB, 0:NB], start=True,
                       stop=True).then_inc(s_job, 1)
                elif kind == "j_score":
                    h, r, j, i0, i1, first, last_ = RB[step[1]]
                    n = min(P, TP - j * P)
                    open_job(step)
                    mm(job_ps(step, i1 - i0, n), ret[:, 4 + h, j * P:j * P + n], ret[:, h, i0:i1],
                       start=True, stop=True).then_inc(s_job, 1)
                elif kind == "att":
                    b = step[1]
                    h, r, j, i0, i1, first, last_ = RB[b]
                    n = min(P, TP - j * P)
                    g = 2 * h + r
                    if first and g >= 2:
                        pe.wait_ge(s_atf[g % 2], g // 2)
                    job_read(pe, ("j_score", b))
                    o0 = i0 - r * (TP // 2)
                    x = mm(bank(2 + g % 2)[:, o0:TP // 2], v_tok[0:n, j, h, :], sc[0:n, b % 3, 0:i1 - i0],
                           start=first, stop=last_)
                    x.then_inc(s_att, 1)
                elif kind == "j_rst":
                    h = step[1]
                    open_job(step)
                    for j in range(TT):
                        n = LASTT if j == TT - 1 else P
                        last = mm(job_ps(step, P), k_tok[0:n, j, h, :], v_tok[0:n, j, h, :], start=(j == 0),
                                  stop=(j == TT - 1))
                    last.then_inc(s_job, 1)
                elif kind == "j_orms":
                    ps = open_job(step)
                    pe.wait_ge(s_osq, step[1] + 1)
                    mm(ps, ones, tmp[:, step[1], cols(step[2])], start=True, stop=True).then_inc(s_job, 1)
                elif kind == "j_lora":
                    _, k, p, hf = step
                    ps = open_job(step)
                    pe.wait_ge(s_lin, 2)
                    rows = {"w": slice(0, 64), "a": slice(64, P), "g": slice(0, P)}[k]
                    w, x = (up_g, gd) if k == "g" else (up_wa, wad)
                    mm(ps, w[rows, p * P:(p + 1) * P], x[rows, cols(hf)], start=True, stop=True)\
                        .then_inc(s_job, 1)
                elif kind in ("j_kkn", "j_bon"):
                    _, p, hf = step
                    ps = open_job(step)
                    pe.wait_ge(s_kkt if kind == "j_kkn" else s_bont, p + 1)
                    mm(ps, bones, tmp[:, p, cols(hf)],
                       start=True, stop=True).then_inc(s_job, 1)
                elif kind == "j_bb":
                    products(step, NP, ret_o, PARTS[kind] - 1)
                elif kind == "wk_a":
                    c = step[1]
                    t0, w, _, _ = wk(c, 0)
                    q = c % 2
                    pe.wait_ge(s_ab, c + 1)
                    if c:
                        pe.wait_ge(s_tri, 3 * c)
                        pe.wait_ge(s_tt, LEV0[c])
                        pe.wait_ge(s_rr, c)
                        pe.wait_ge(s_sa, c)
                        pe.wait_ge(s_st, c + 1)
                        pe.wait_ge(s_y, c)
                        pe.wait_ge(s_toks, 3 * c)
                    for s in range(2):
                        _, _, full, part = wk(c, s)
                        for p in range(NP):
                            rhs = ar[full, q, p, :, 0:w]
                            o = psum[part, 1024 + 128 * p:1024 + 128 * p + 128]\
                                .rearrange("p (a b) -> p a b", a=2)[:, :, 0:w]
                            mm(o, bk[full, q, 0, p, 0:w], rhs, start=True, stop=True)
                            o = psum[part, 1536 + 128 * p:1536 + 128 * p + 128]\
                                .rearrange("p (a b) -> p a b", a=2)[:, :, 0:w]
                            mm(o, bk[full, q, 1, p, 0:w], rhs, start=True, stop=True)
                            last = mm(psum[part, 2048 + 64 * p:2048 + 64 * p + w], ar[full, q, p, 0, 0:w],
                                      bk[full, q, 0, p, 0:w], start=True, stop=True)
                    last.then_inc(s_pab, 1)
                    for i in range(2):
                        b = 7 - i
                        if i == 1:
                            pe.wait_ge(s_abp, c + 1)
                        for p in range(NP):
                            src = v_f[:, p, t0:t0 + w] if i == 0 else bkp[:, 0, p, 0:w]
                            last = nc.tensor.transpose(bank(b, 512, w)[:, p * P:(p + 1) * P], src, ident)
                        last.then_inc(s_px, 1)
                elif kind == "wk_k":
                    c = step[1]
                    _, w, _, _ = wk(c, 0)
                    pe.wait_ge(s_toks, 3 * c + 1)
                    for p in range(NP):
                        last = nc.tensor.transpose(bank(7, 512, w)[:, p * P:(p + 1) * P], bkp[:, 1, p, 0:w], ident)
                    last.then_inc(s_px, 1)
                elif kind == "wk_x":
                    _, c, b = step
                    l = LEVELS.index(b)
                    if b == 2:
                        pe.wait_ge(s_tri, 3 * c + 2)
                    else:
                        pe.wait_ge(s_tt, LEV0[c] + l - 1)
                    for s in range(2):
                        _, w, full, part = wk(c, s)
                        for p in range(NP):
                            last = mm(psum[part, 2048 + 64 * p:2048 + 64 * p + w], ab[part, p, 0, 0:w],
                                      tp[part, 0, p, 0:w], start=True, stop=True)
                    last.then_inc(s_pt, 1)
                elif kind == "wk_t":
                    _, c, b = step
                    l = LEVELS.index(b)
                    pe.wait_ge(s_xl, LEV0[c] + l)
                    for s in range(2):
                        _, w, full, part = wk(c, s)
                        for p in range(NP):
                            if 2 * b < w:
                                mm(psum[part, 2560 + 64 * p:2560 + 64 * p + w], tp[part, 1, p, 0:w],
                                   xl[part, p, 0:w], start=True, stop=True)
                            last = mm(psum[part, 2816 + 64 * p:2816 + 64 * p + w], xl[part, p, 0:w],
                                      tp[part, 1, p, 0:w], start=True, stop=True)
                    last.then_inc(s_pr, 1)
                elif kind == "wk_r":
                    c = step[1]
                    q = c % 2
                    pe.wait_ge(s_st, c + 1)
                    pe.wait_ge(s_toks, 3 * c + 3)
                    pe.wait_ge(s_tri, 3 * c + 3)
                    for s in range(2):
                        _, w, full, part = wk(c, s)
                        for p in range(NP):
                            o = psum[part, 3072 + 64 * p:3072 + 64 * p + 64]
                            mm(o, ar[full, q, p, 0, 0:w], st[full, q, p, :], start=True, stop=False)
                            last = mm(o, kq[part, p, 0, 0:w], tok[part, 0, p, :], start=False, stop=True)
                    last.then_inc(s_psa, 1)
                elif kind == "wk_sa":
                    c = step[1]
                    pe.wait_ge(s_tt, LEV0[c] + NLEV[c])
                    pe.wait_ge(s_rr, c + 1)
                    for s in range(2):
                        _, w, full, part = wk(c, s)
                        for p in range(NP):
                            last = mm(psum[part, 3328 + 64 * p:3328 + 64 * p + 64], tp[part, 1, p, 0:w],
                                      rr[part, p, :], start=True, stop=True)
                    last.then_inc(s_psa, 1)
                elif kind == "wk_s":
                    c = step[1]
                    q = c % 2
                    pe.wait_ge(s_sa, c + 1)
                    for s in range(2):
                        _, w, full, part = wk(c, s)
                        for p in range(NP):
                            o = psum[full, 3584 + 64 * p:3584 + 64 * p + 64]
                            mm(o, tok[part, 1, p, :], sa[part, p, :], start=True, stop=False)
                            last = mm(o, tok[part, 2, p, :], tok[part, 0, p, :], start=False, stop=True)
                    last.then_inc(s_ps, 1)
                    for s in range(2):
                        _, w, full, part = wk(c, s)
                        for p in range(NP):
                            o = psum[full, 3072 + 64 * p:3072 + 64 * p + w]
                            mm(o, st[full, q, p, :], ar[full, q, p, 1, 0:w], start=True, stop=False)
                            mm(o, sa[part, p, :], ab[part, p, 1, 0:w], start=False, stop=False)
                            last = mm(o, tok[part, 0, p, :], kq[part, p, 1, 0:w], start=False, stop=True)
                    last.then_inc(s_ps, 1)
                elif kind in ("j_sk", "j_sv", "j_sy"):
                    p = step[1]
                    open_job(step)
                    pe.wait_ge(s_smt, 3 * p + {"j_sk": 1, "j_sv": 2, "j_sy": 3}[kind])
                    mm(job_ps(step, 512), bones, (t2 if kind == "j_sv" else t1), start=True, stop=True)\
                        .then_inc(s_job, 1)
                elif kind in ("j_mean", "j_var"):
                    _, p, hf = step
                    ps = open_job(step)
                    if kind == "j_mean":
                        pe.wait_ge(s_y, 1 + (HT - 1) // C if hf == 0 else NCH)
                        if hf:
                            pe.wait_ge(s_ys, NP)
                    else:
                        pe.wait_ge(s_vsd, NP * hf + p + 1)
                    mm(ps, bones, (ly if kind == "j_mean" else tmp)[:, p, cols(hf)], start=True,
                       stop=True).then_inc(s_job, 1)
                elif kind in ("j_ba", "j_out"):
                    _, m, hf = step
                    w, nk, x = (w_ba, NP, ly) if kind == "j_ba" else (w_out, KD, merged)
                    ps = open_job(step)
                    if kind == "j_ba":
                        pe.wait_ge(s_ba, 16)
                        pe.wait_ge(s_ya, NP * (hf + 1))
                    else:
                        pe.wait_ge(s_wo[m // 4], 16)
                        pe.wait_ge(s_mg, KD * (hf + 1))
                    for k in range(nk):
                        last = mm(ps, w[:, m, k, :], x[:, k, cols(hf)], start=(k == 0), stop=(k == nk - 1))
                    last.then_inc(s_job, 1)
                elif kind == "tok":
                    _, g, k = step
                    if k == 0 and g == 0:
                        pe.wait_ge(d_wr, 1)
                    if k == 0 and g:
                        pe.wait_ge(d_xc, 2)
                    job_read(pe, ("j_out", k, g))
                    for q in range(2):
                        o = 1024 * (q + 1) + P * k
                        t = 2 * g + q
                        last = nc.tensor.transpose(psum[:, o:o + P], u[:, k, t * P:t * P + P], ident)
                    if k == KD - 1:
                        last.then_inc(d_x, 1)
                    last = mm(bank(6 + g, HT, 20), wr[:, k, :], u[:, k, cols(g)], start=(k == 0), stop=(k == KD - 1))
                    if k == KD - 1:
                        last.then_inc(d_lt, 1)
                elif kind == "tok4":
                    for q in range(2):
                        job_read(pe, ("j_out", 6 + q, 1))
                    for k in range(KD):
                        last = nc.tensor.transpose(psum[0:LASTT, P * k:P * k + P], u[:, k, (TT - 1) * P:T], ident)
                    last.then_inc(d_x, 1)
                elif kind == "route":
                    pe.wait_ge(d_ltc, 2)
                    for t in range(TT):
                        n = rows_of(t)
                        last = nc.tensor.transpose(bank(6, 512, n)[:, 20 * t:20 * t + 20], logt[0:20, t * P:t * P + n],
                                                   ident[0:20, 0:20])
                    last.then_inc(d_lg, 1)
                    pe.wait_ge(d_sel, 1)
                    for t in range(TT + 1):
                        o = bank(7)[:, NE * t:NE * t + NE]
                        for q in range(min(t, TT - 1) + 1 if t < TT else TT):
                            last = mm(o, trib[:, :] if q == t else oneb[:, :], selb[:, q, :], start=(q == 0),
                                      stop=(q == min(t, TT - 1)))
                    last.then_inc(d_pos, 1)

        SHIFT_ORDER = [s_[1] for s_ in STEPS if s_[0] == "j_proj" and s_[1] < SHIFT_TILES and s_[2] == 0]

        def shifted(m):
            return [r_f, k_f, v_f][m // 4][:, m % 4, :] if m < 12 else (wad, gd)[m - 12]

        @block.scalar
        def _(act):
            own = [0]

            def run(ins, s=None):
                if s is None:
                    own[0] += 1
                    ins.then_inc(s_act, 1)
                    act.wait_ge(s_act, own[0])
                else:
                    ins.then_inc(s, 1)

            def f(out, in_, fn=ACT.Copy, s=None, **kw):
                run(nc.scalar.activation(out, in_, fn, **kw), s)

            act.wait_ge(s_eps, 1)
            f(dummy, eps, ACT.Sqrt, s=s_dum)
            for step in STEPS:
                kind = step[0]
                free = s_free[JOBS[step] % 2] if step in JOBS else None
                if kind == "sq":
                    for k in range(1, KD, 2):
                        act.wait_ge(s_x[step[1]][k // 2], 16)
                        f(merged[:, k, cols(step[1])], u[:, k, cols(step[1])], ACT.Square, s=s_sqa)
                if kind == "j_norm":
                    if step[2] == 0:
                        act.wait_ge(s_load, 32)
                    job_done(act, step)
                    f(tmp[:, 0, cols(step[2])], job_ps(step), ACT.Sqrt, scale=1.0 / D, bias=eps, s=free)
                elif kind == "j_proj":
                    _, m, hf = step
                    job_done(act, step)
                    if m < SHIFT_TILES:
                        i = SHIFT_ORDER.index(m)
                        if i == 0:
                            act.wait_ge(s_ph, 1)
                        if i >= 2:
                            act.wait_ge(s_shift, i - 1)
                        f(raw[:, i % 2, 1 + hf * HT:1 + (hf + 1) * HT], job_ps(step), s=free)
                        if hf:
                            job_read(act, ("j_proj", m, 0))
                            job_read(act, step)
                            f(sh[:, m, :], raw[:, i % 2, TP:TP + 9], s=s_raw)
                    elif m < RET0 + 12:
                        f(ret[:, m - RET0, cols(hf)], job_ps(step), s=free)
                    elif m < GA0:
                        f(ret[:, m - RET0, cols(hf)], job_ps(step), ACT.Sigmoid, s=s_sig)
                    elif m < GB0:
                        f(sga[:, m - GA0, cols(hf)], job_ps(step), ACT.Sigmoid, s=free)
                    else:
                        f(merged[:, m - GB0, cols(hf)], job_ps(step), ACT.Sigmoid, s=free)
                elif kind == "j_vt":
                    t = step[1]
                    n = LASTT if t == TT - 1 else P
                    job_done(act, step)
                    f(v_tok[0:n, t, :, :], bank(bank_of(step), 512, n).rearrange("p (h v) -> p h v", h=RH), s=free)
                elif kind == "j_ros":
                    job_done(act, step)
                    f(ret_o[:, step[1], TP:T], job_ps(step, NB), s=free)
                elif kind == "att":
                    b = step[1]
                    h, r, j, i0, i1, first, last_ = RB[b]
                    if last_:
                        g = 2 * h + r
                        act.wait_ge(s_att, b + 1)
                        f(ret_o[:, h, r * (TP // 2):(r + 1) * (TP // 2)], bank(2 + g % 2, TP // 2), s=s_atf[g % 2])
                elif kind == "j_rst":
                    job_done(act, step)
                    f(ret_st[:, step[1], :], job_ps(step, P), s=free)
                elif kind == "j_orms":
                    _, h, hf = step
                    job_done(act, step)
                    f(tmp[:, h, cols(hf)], job_ps(step), ACT.Sqrt, scale=1.0 / P, bias=eps, s=free)
                elif kind == "lora_in":
                    act.wait_ge(s_load2, 80)
                    act.wait_ge(s_shift, 2)
                    f(wad[0:64, :], wad[0:64, :], ACT.Tanh, s=s_lin)
                    f(gd, gd, ACT.Sigmoid, s=s_lin)
                elif kind == "j_lora":
                    _, k, p, hf = step
                    job_done(act, step)
                    if k == "g":
                        f(g_f[:, p, cols(hf)], job_ps(step), s=free)
                    else:
                        f((ly if k == "w" else b_f)[:, p, cols(hf)], job_ps(step), ACT.Sigmoid,
                          bias=vv("w0" if k == "w" else "a0", p), s=free)
                elif kind == "j_kkn":
                    job_done(act, step)
                    f(tmp[:, step[1], cols(step[2])], job_ps(step), ACT.Sqrt, s=free)
                elif kind == "wk_prep":
                    c = step[1]
                    t0, w, _, _ = wk(c, 0)
                    if c == 0:
                        act.wait_ge(s_bont, NP)
                        act.wait_ge(s_st, 1)
                    else:
                        act.wait_ge(s_ab, c)
                    if c >= 2:
                        act.wait_ge(s_st, c)
                    f(ep[:, c % 2, :, 1:w + 1], ly[:, :, t0:t0 + w], ACT.Exp, scale=-DECAY, s=s_e)
                    f(en[:, :, 0:w], ly[:, :, t0:t0 + w], ACT.Exp, scale=DECAY, s=s_e)
                elif kind in ("wk_a", "wk_k"):
                    c = step[1]
                    if c and kind == "wk_a":
                        act.wait_ge(s_ps, 2 * c)
                    for i in (0, 1) if kind == "wk_a" else (2,):
                        act.wait_ge(s_px, 3 * c + i + 1)
                        for s in range(2):
                            _, w, full, part = wk(c, s)
                            src = bank(6 if i == 1 else 7, 512, w)\
                                .rearrange("t (p s k) -> t p s k", p=NP, s=2)[:, :, s, :]
                            nc.scalar.activation(tok[part, i, :, :], src, ACT.Copy).then_inc(s_toks if s else s_act, 1)
                            if s == 0:
                                own[0] += 1
                        act.wait_ge(s_act, own[0])
                elif kind == "wk_r":
                    c = step[1]
                    act.wait_ge(s_psa, 2 * c + 1)
                    f(rr, bank(6, 256).rearrange("t (p k) -> t p k", p=NP), s=s_rr)
                elif kind == "wk_sa":
                    c = step[1]
                    act.wait_ge(s_psa, 2 * c + 2)
                    f(sa, psum[:, 3328:3584].rearrange("t (p k) -> t p k", p=NP), s=s_sa)
                elif kind == "wk_s":
                    c = step[1]
                    t0, w, _, _ = wk(c, 0)
                    act.wait_ge(s_ps, 2 * c + 2)
                    f(ly[:, :, t0:t0 + w], bank(6, 256).rearrange("t (p k) -> t p k", p=NP)[:, :, 0:w], s=s_y)
                elif step == ("sm_in", 0):
                    f(wsmp, ly[:, :, TP:T], ACT.Exp, scale=-DECAY, s=s_sw)
                elif kind == "j_var":
                    _, p, hf = step
                    job_done(act, step)
                    f(tmp[:, p, cols(hf)], job_ps(step), ACT.Sqrt, scale=1.0 / 64, bias=lnx_eps, s=free)
                elif kind == "x2":
                    act.wait_ge(s_out, 16 * 5)
                    act.wait_ge(d_x, 1)
                    for t in range(2):
                        f(x2t[:, t, :], psum[:, 1024 * (t + 1):1024 * (t + 2)], s=d_xc)
                    act.wait_ge(d_lt, 1)
                    act.wait_ge(d_ld, 48)
                    f(logt[0:20, cols(0)], bank(6, HT, 20), s=d_ltc)
                    act.wait_ge(d_xc, 2)
                    for t in range(2):
                        f(junk, x2t[:, t, :], ACT.Square, accum_out=ssq[:, t:t + 1], s=d_ss)
                        act.wait_ge(d_ss, t + 1)
                    f(rstd[:, 0:2], ssq[:, 0:2], ACT.Sqrt, scale=1.0 / D, bias=eps2[:, :], s=d_rt)
                    act.wait_ge(d_rc, 1)
                    for t in range(2):
                        f(u2_rows(t), x2t[:, t, :], ACT.Copy, scale=rstd[:, t:t + 1], s=d_u2)
                elif kind == "route":
                    act.wait_ge(d_lt, 2)
                    f(logt[0:20, cols(1)], bank(7, HT, 20), s=d_ltc)
                    src = [psum[:, 1024:2048], psum[:, 2048:3072], psum[0:LASTT, 0:1024]]
                    for t in range(2, TT):
                        act.wait_ge(d_x, 2 if t < TT - 1 else 3)
                        n = rows_of(t)
                        f(junk[0:n], src[t - 2], ACT.Square, accum_out=ssq[0:n, t:t + 1], s=d_ss)
                        act.wait_ge(d_ss, t + 1)
                    f(rstd[:, 2:TT], ssq[:, 2:TT], ACT.Sqrt, scale=1.0 / D, bias=eps2[:, :], s=d_rt)
                    for t in range(2, TT):
                        n = rows_of(t)
                        f(x2t[0:n, t, :], src[t - 2], s=d_xc)
                    act.wait_ge(d_ll, 1)
                    f(ex, ll, ACT.Exp, s=d_ex)
                    act.wait_ge(d_rc, 2)
                    act.wait_ge(d_xc, TT)
                    act.wait_ge(d_u2w[0], 16)
                    for t in range(2, TT):
                        n = rows_of(t)
                        f(u2_rows(t), x2t[0:n, t, :], ACT.Copy, scale=rstd[0:n, t:t + 1], s=d_u2)

        @block.vector
        def _(dve):
            v = nc.vector
            own = [0]
            counts = {}

            def run(ins, s=None):
                s = s_dve if s is None else s
                counts[s.name] = counts.get(s.name, 0) + 1
                ins.then_inc(s, 1)
                if s.name in alone:
                    dve.wait_ge(s, counts[s.name])

            alone = {x.name for x in (s_dve, s_sq, s_eps, s_u, s_shift, s_kq, s_vb, s_sn, s_od, s_osq, s_ph, s_kkt,
                                      s_bont, s_ab, s_abp, s_tri, s_tt, s_st, s_smt, s_ws, s_on, s_xl, s_ys, s_vsd, s_ya,
                                      s_mg, d_wr, d_rc, d_ll, d_sel, d_n)}

            def tt(out, a, b, op=ALU.mult, s=None):
                run(v.tensor_tensor(out, a, b, op), s)

            def stt(out, a, sc_, b, op0, op1, s=None):
                run(v.scalar_tensor_tensor(out, a, sc_, b, op0, op1), s)

            def ts(out, a, s1, s2, op0, op1=None, s=None):
                run(v.tensor_scalar(out, a, s1, s2, op0, op1) if op1 is not None
                    else v.tensor_scalar(out, a, s1, None, op0), s)

            def decayed(c):
                _, w, _, _ = wk(c, 0)
                q = c % 2
                for i in range(2):
                    tt(bkp[:, i, :, 0:w], bk[:, q, i, :, 0:w], bc(ep[:, q, :, w], w), s=s_abp if i else None)

            run(v.memset(eps, EPS), s_eps)
            run(v.memset(lnx_eps, LNX_EPS))
            nsig = 0
            for step in STEPS:
                kind = step[0]
                free = s_free[JOBS[step] % 2] if step in JOBS else None
                if kind == "sq":
                    for k in range(0, KD, 2):
                        dve.wait_ge(s_x[step[1]][k // 2], 16)
                        x = u[:, k, cols(step[1])]
                        tt(merged[:, k, cols(step[1])], x, x, s=s_sq)
                elif kind == "j_norm":
                    hf = step[2]
                    if hf == 0:
                        dve.wait_ge(s_load, 32)
                    job_read(dve, step)
                    run(v.reciprocal(tmp[:, 1, cols(hf)], tmp[:, 0, cols(hf)]))
                    for k in range(KD):
                        x = u[:, k, cols(hf)]
                        stt(x, x, vv("norm1_g", k), tmp[:, 1, cols(hf)], ALU.mult, ALU.mult, s=s_u)
                elif kind == "j_proj":
                    _, m, hf = step
                    if m < SHIFT_TILES and hf:
                        i = SHIFT_ORDER.index(m)
                        x = raw[:, i % 2, :]
                        o = shifted(m)
                        dve.wait_ge(s_raw, i + 1)
                        tt(dif[:, 0:TP], x[:, 0:TP], x[:, 1:TP + 1], ALU.subtract)
                        tt(shd[:, m, :], shs[:, m, :], sh[:, m, 1:9], ALU.subtract)
                        stt(o[:, TP:T], shd[:, m, :], vv("mu", m), sh[:, m, 1:9], ALU.mult, ALU.add)
                        stt(o[:, 0:TP], dif[:, 0:TP], vv("mu", m), x[:, 1:TP + 1], ALU.mult, ALU.add, s=s_shift)
                    elif RET0 + 12 <= m < GA0:
                        nsig += 1
                        dve.wait_ge(s_sig, nsig)
                        tt(ret[:, m - RET0, cols(hf)], job_ps(step), ret[:, m - RET0, cols(hf)], s=free)
                elif kind == "j_rope":
                    _, j, hf = step
                    a = 1.0 if j < RH else P ** -0.5
                    dve.wait_ge(s_load2, 80)
                    x = ret[:, j, cols(hf)]
                    job_done(dve, step)
                    stt(tmp[:, 2, 0:HT], job_ps(step), a, cc("sin")[:, cols(hf)], ALU.mult, ALU.mult, s=free)
                    stt(tmp[:, 3, 0:HT], x, a, cc("cos")[:, cols(hf)], ALU.mult, ALU.mult)
                    job_read(dve, step)
                    tt(x, tmp[:, 2, 0:HT], tmp[:, 3, 0:HT], ALU.add, s=s_kq)
                elif kind == "j_kt":
                    t = step[1]
                    n = LASTT if t == TT - 1 else P
                    ps = bank(bank_of(step), 512, n).rearrange("p (h v) -> p h v", h=RH)
                    job_done(dve, step)
                    if t == TT - 1:
                        run(v.tensor_copy(k_smp[0:n], ps))
                    tt(k_tok[0:n, t, :, :], ps, bc(cc("dend", TT, RH, rows=n)[:, t, :], P), s=free)
                elif kind == "rs_v":
                    h = step[1]
                    if h == 0:
                        job_read(dve, ("j_vt", TT - 1))
                        dve.wait_ge(s_rets, 16)
                    else:
                        dve.wait_ge(s_rsp, h)
                    tt(vb[0:LASTT], v_tok[0:LASTT, TT - 1, h, :].unsqueeze(1).broadcast_to([LASTT, NB, P]),
                       bc(cc("smask", rows=LASTT), P), s=s_vb)
                elif kind == "rs_a":
                    h = step[1]
                    dve.wait_ge(s_rsp, h + 1)
                    stt(s_new[:, h].rearrange("p b v -> p (b v)"), s_new[:, h].rearrange("p b v -> p (b v)"),
                        GAMMA[h], psum[:, 2048:3072], ALU.mult, ALU.add, s=s_sn)
                elif kind == "rs_b":
                    h = step[1]
                    dve.wait_ge(s_roq, h + 1)
                    tt(o_diag[0:NB], psum[0:NB, 3072:4096].rearrange("p (b v) -> p b v", b=NB),
                       bc(ident[0:NB, 0:NB], P))
                    run(v.tensor_reduce(o_smp[0:NB, h, :], o_diag[0:NB].rearrange("p b v -> p v b"), AX.X, ALU.add),
                        s_od)
                elif kind == "j_score":
                    n_ = step[1]
                    h, r, j, i0, i1, first, last_ = RB[n_]
                    n = min(P, TP - j * P)
                    job_done(dve, step)
                    if n_ >= 3:
                        dve.wait_ge(s_att, n_ - 2)
                    d = cc("dec", RH, TP, rows=n)[:, h, i0 - j * P:i1 - j * P]
                    tt(sc[0:n, n_ % 3, 0:i1 - i0], job_ps(step, i1 - i0, n), d, s=free)
                elif kind == "osq":
                    h = step[1]
                    job_read(dve, ("j_ros", h))
                    for g in range(2):
                        dve.wait_ge(s_atf[g], h + 1)
                    tt(tmp[:, h, :], ret_o[:, h, :], ret_o[:, h, :], s=s_osq)
                    for q in range(2):
                        job_read(dve, ("j_proj", RET0 + 12 + h, q))
                    tt(ret_o[:, h, :], ret_o[:, h, :], ret[:, 12 + h, :])
                elif kind == "phase2":
                    dve.wait_ge(s_out, 32)
                    dve.wait_ge(s_att, len(RB))
                    run(v.memset(raw[:, :, 0:1], 0.0), s_ph)
                elif kind == "j_orms" and step[2]:
                    h = step[1]
                    job_read(dve, ("j_orms", h, 0))
                    job_read(dve, step)
                    run(v.reciprocal(tmp[:, h, :], tmp[:, h, :]))
                    tt(ret_o[:, h, :], ret_o[:, h, :], tmp[:, h, :], s=s_on)
                elif kind == "kk_in":
                    p = step[1]
                    for hf in range(2):
                        job_read(dve, ("j_lora", "w", p, hf))
                    run(v.tensor_tensor_scan(ly[:, p, 0:TP], cc("reset"), ly[:, p, 0:TP], 0.0, ALU.mult, ALU.add))
                    ts(kk_f[:, p, :], k_f[:, p, :], vv("kk", p), None, ALU.mult)
                    tt(tmp[:, p, :], kk_f[:, p, :], kk_f[:, p, :], s=s_kkt)
                elif kind == "j_kkn" and step[2]:
                    p = step[1]
                    for hf in range(2):
                        job_read(dve, ("j_kkn", p, hf))
                    ts(tmp[:, p, :], tmp[:, p, :], 1e-12, None, ALU.max)
                    run(v.reciprocal(tmp[:, p, :], tmp[:, p, :]))
                    tt(kk_f[:, p, :], kk_f[:, p, :], tmp[:, p, :])
                elif kind == "bon_in":
                    p = step[1]
                    for hf in range(2):
                        job_read(dve, ("j_lora", "a", p, hf))
                    ts(tmp[:, p, :], b_f[:, p, :], -1.0, vv("ka", p), ALU.add, ALU.mult)
                    stt(k_f[:, p, :], tmp[:, p, :], 1.0, k_f[:, p, :], ALU.add, ALU.mult)
                    tt(b_f[:, p, :], kk_f[:, p, :], b_f[:, p, :])
                    stt(tmp[:, p, :], r_f[:, p, :], vv("rk", p), k_f[:, p, :], ALU.mult, ALU.mult, s=s_bont)
                elif kind == "j_bon":
                    _, p, hf = step
                    job_done(dve, step)
                    tt(bon[:, p, cols(hf)], job_ps(step), v_f[:, p, cols(hf)], s=free)
                elif kind == "wk_prep":
                    c = step[1]
                    q = c % 2
                    t0, w, _, _ = wk(c, 0)
                    if c == 0:
                        run(v.memset(ep[:, :, :, 0:1], 1.0))
                        run(v.memset(st[:, 0], 0.0), s_st)
                    dve.wait_ge(s_e, 2 * c + 2)
                    if c >= 2:
                        dve.wait_ge(s_ps, 2 * c - 2)
                    x = slice(t0, t0 + w)
                    tt(bk[:, q, 0, :, 0:w], b_f[:, :, x], en[:, :, 0:w])
                    tt(bk[:, q, 1, :, 0:w], k_f[:, :, x], en[:, :, 0:w])
                    stt(ar[:, q, :, 0, 0:w], kk_f[:, :, x], -1.0, ep[:, q, :, 0:w], ALU.mult, ALU.mult)
                    tt(ar[:, q, :, 1, 0:w], r_f[:, :, x], ep[:, q, :, 1:w + 1], s=s_ab)
                    if c == 0:
                        decayed(0)
                elif kind == "wk_k":
                    if step[1] + 1 < NCH:
                        dve.wait_ge(s_px, 3 * step[1] + 3)
                        decayed(step[1] + 1)
                elif kind == "wk_a":
                    c = step[1]
                    t0, w, _, _ = wk(c, 0)
                    dve.wait_ge(s_pab, c + 1)
                    if c:
                        dve.wait_ge(s_ps, 2 * c)
                    b2 = bank(2).rearrange("t (p a k) -> t p a k", p=NP, a=2)
                    ai = pairs(cc("ai", 2, C)[:, :, 0:w])
                    tt(tp[:, 1, :, 0:w], b2[:, :, 0, 0:w], pairs(cc("lev0t")[:, 0:w]))
                    tt(tp[:, 0, :, 0:w], bank(4, 256).rearrange("t (p k) -> t p k", p=NP)[:, :, 0:w],
                       pairs(cc("lev", 6, C)[:, 0, 0:w]))
                    for i in range(2):
                        tt(tp[:, i, :, 0:w], tp[:, i, :, 0:w], pairs(cc("eye")[:, 0:w]), ALU.add, s=s_tri if i else None)
                    tt(ab[:, :, :, 0:w], b2[:, :, :, 0:w], ai, s=s_tri)
                elif kind == "wk_x":
                    _, c, b = step
                    l = LEVELS.index(b)
                    _, w, _, _ = wk(c, 0)
                    dve.wait_ge(s_pt, LEV0[c] + l)
                    tt(xl[:, :, 0:w], bank(4, 256).rearrange("t (p k) -> t p k", p=NP)[:, :, 0:w],
                       pairs(cc("lev", 6, C)[:, l, 0:w]), s=s_xl)
                    if b == 2:
                        tt(kq[:, :, :, 0:w], bank(3).rearrange("t (p a k) -> t p a k", p=NP, a=2)[:, :, :, 0:w],
                           pairs(cc("ai", 2, C)[:, :, 0:w]), s=s_tri)
                elif kind == "wk_t":
                    _, c, b = step
                    l = LEVELS.index(b)
                    _, w, _, _ = wk(c, 0)
                    dve.wait_ge(s_pr, LEV0[c] + l)
                    f0 = 0 if 2 * b < w else 1
                    ps = bank(5).rearrange("t (a p k) -> t a p k", a=2, p=NP)
                    tt(tp[:, f0:2, :, 0:w], ps[:, f0:2, :, 0:w], tp[:, f0:2, :, 0:w], ALU.add, s=s_tt)
                elif kind == "wk_s":
                    c = step[1]
                    q = c % 2
                    _, w, _, _ = wk(c, 0)
                    tt(stp, st[:, q], bc(ep[:, q, :, w], C))
                    dve.wait_ge(s_ps, 2 * c + 1)
                    tt(st[:, 1 - q], bank(7, 256).rearrange("t (p k) -> t p k", p=NP), stp, ALU.add, s=s_st)
                elif kind == "j_bb":
                    _, m, hf = step
                    job_read(dve, ("j_proj", GB0 + m, hf))
                    job_done(dve, step)
                    tt(merged[:, m, cols(hf)], job_ps(step), merged[:, m, cols(hf)], s=free)
                elif kind in ("sm_in", "j_sk", "j_sv", "sm_y", "j_sy"):
                    p = step[1]

                    def tok_bc(a):
                        return bc(a[:, p, TP:T], 64)

                    w_, a1, a2 = ws[:, p], t1, t2
                    eye = cc("eye").unsqueeze(1).broadcast_to([P, NB, 64])
                    if kind == "sm_in":
                        if p == 0:
                            dve.wait_ge(s_sld, 16)
                            dve.wait_ge(s_sw, 1)
                        tt(a1, w_, tok_bc(kk_f), s=s_smt)
                        tt(a2, eye, tok_bc(v_f), s=s_smt)
                        tt(w_, w_, bc(wsmp[:, p, :], 64))
                    elif kind == "sm_y":
                        tt(a1, w_, tok_bc(r_f), s=s_smt)
                    else:
                        ps = job_ps(step, 512).rearrange("k (b v) -> k b v", b=NB)
                        job_done(dve, step)
                        if kind == "j_sk":
                            tt(a1, ps, tok_bc(b_f), s=free)
                            job_read(dve, step)
                            tt(w_, w_, a1, ALU.subtract)
                        elif kind == "j_sv":
                            tt(a1, ps, tok_bc(k_f), s=free)
                            job_read(dve, step)
                            tt(w_, w_, a1, ALU.add, s=s_ws)
                        else:
                            tt(a2, ps, eye, s=free)
                            job_read(dve, step)
                            run(v.tensor_reduce(ly[:, p, TP:T], a2, AX.X, ALU.add), s_ys)
                elif kind == "j_mean":
                    _, p, hf = step
                    job_done(dve, step)
                    x = ly[:, p, cols(hf)]
                    stt(x, job_ps(step), -1.0 / 64, x, ALU.mult, ALU.add, s=free)
                    job_read(dve, step)
                    tt(tmp[:, p, cols(hf)], x, x, s=s_vsd)
                elif kind == "j_var":
                    _, p, hf = step
                    job_read(dve, step)
                    x, y = tmp[:, p, cols(hf)], ly[:, p, cols(hf)]
                    run(v.reciprocal(x, x))
                    stt(y, y, vv("lnw", p), x, ALU.mult, ALU.mult)
                    stt(y, y, vv("lnb", p), bon[:, p, cols(hf)], ALU.add, ALU.add)
                    tt(y, y, g_f[:, p, cols(hf)], s=s_ya)
                elif kind == "j_ba":
                    _, m, hf = step
                    job_done(dve, step)
                    if hf == 0:
                        for q in range(2):
                            job_read(dve, ("j_proj", GA0 + m, q))
                            job_read(dve, ("j_bb", m, q))
                    tt(sga[:, m, cols(hf)], job_ps(step), sga[:, m, cols(hf)], s=free)
                    job_read(dve, step)
                    tt(merged[:, m, cols(hf)], merged[:, m, cols(hf)], sga[:, m, cols(hf)], ALU.add, s=s_mg)
                elif kind == "j_out":
                    _, m, hf = step
                    dve.wait_ge(s_xr, 16)
                    job_done(dve, step)
                    tt(u[:, m, cols(hf)], job_ps(step), u[:, m, cols(hf)], ALU.add, s=free)
                elif kind == "rt_in":
                    run(v.memset(eps2[:, :], EPS))
                    run(v.memset(ssq, 1.0))
                    run(v.memset(lg, 0.0))
                    run(v.tensor_copy(trib[:, :], cc("tri")))
                    run(v.tensor_copy(oneb[:, :], ones))
                    dve.wait_ge(d_ld, 48)
                    o2 = VEC["norm2_g"]
                    tt(wr, wr, bc(vec[:, o2:o2 + KD], 20), s=d_wr)
                elif kind == "x2":
                    dve.wait_ge(d_rt, 1)
                    run(v.reciprocal(rstd[:, 0:2], rstd[:, 0:2]), d_rc)
                elif kind == "route":
                    route(dve, v, run, tt)

        @block.gpsimd
        def _(pool):
            for t in range(TT):
                pool.wait_ge(d_u2, t + 1)
                pool.dma_start(u2_dram[t * P:t * P + rows_of(t), :], u2_rows(t))\
                    .then_inc(d_u2w[t % 2], 16)
            pool.wait_ge(d_u2w[0], 16 * 3)
            pool.wait_ge(d_u2w[1], 16 * 2)

        mixer.__exit__(None, None, None)

        q_oh = sem("q_oh")
        q_pid = sem("q_pid")
        q_id = sem("q_id")
        q_g = [sem(f"q_g{i}") for i in range(2)]
        q_tr = sem("q_tr")
        q_ue = sem("q_ue")
        q_gu = sem("q_gu")
        q_sig = sem("q_sig")
        q_h1 = sem("q_h1")
        q_h = sem("q_h")
        q_ht = sem("q_ht")
        q_hte = sem("q_hte")
        q_dn = sem("q_dn")
        q_yo = sem("q_yo")
        q_yd = [sem(f"q_yd{i}") for i in range(2)]
        q_ix = sem("q_ix")
        q_yg = [sem(f"q_yg{i}") for i in range(NYG)]
        q_cb = sem("q_cb")
        q_dv = sem("q_dv")
        NDV = 19
        z_ss = sem("z_ss")
        z_rt = sem("z_rt")
        z_rc = sem("z_rc")
        z_y = sem("z_y")
        z_out = [sem(f"z_out{i}") for i in range(2)]

        rounds = nc.values_load(n_rounds[0:1, 0:1], min_val=1, max_val=ROUNDS)
        with nc.Fori(0, rounds) as r:
            def at_least(eng, s, per, n):
                assert n > 0
                eng.wait_ge(s, r * per + n)

            with nc.Block() as block:
                @block.sync
                def _(sp):
                    for q in range(2):
                        at_least(sp, q_g[q], 8 * 16, 16)
                    for e in range(2, NE):
                        if e >= NWE:
                            at_least(sp, q_dn, NE, e - NWE + 1)
                        else:
                            sp.nop(nofuse=True)
                        load_expert(sp, e)
                    for t in range(TT):
                        at_least(sp, z_y, TT, t + 1)
                        sp.nop(nofuse=True)
                        n = rows_of(t)
                        sp.dma_start(O["y"][t * P:t * P + n, :], yo[0:n, t % 2, :]).then_inc(z_out[t % 2], 16)
                    at_least(sp, z_out[0], 48, 48)
                    at_least(sp, z_out[1], 32, 32)
                    sp.nop(nofuse=True)
                    with sp.If(r + 1 < rounds):
                        for e in range(2):
                            load_expert(sp, e)

                @block.gpsimd
                def _(pool):
                    def then(s, per, n):
                        at_least(pool, s, per, n)
                        pool.nop(nofuse=True)

                    then(q_id, 1, 1)
                    for e in range(NE):
                        if e >= 2:
                            then(q_tr, NE, e - 1)
                        pool.indirect_dma_start(ug[:, e % 2, :], None, u2_dram,
                                                bass.IndirectOffsetOnAxis(ap=ids[:, e:e + 1], axis=0))\
                            .then_inc(q_g[e % 2], 16)
                    then(q_ix, 1, 1)
                    for i in range(2):
                        then(q_yd[i], 8 * 16, 8 * 16)
                    for j in range(2 * TT):
                        t, i = j // 2, j % 2
                        n = rows_of(t)
                        if j >= NYG:
                            then(q_cb, 2 * TT, j - NYG + 1)
                        pool.indirect_dma_start(yg[0:n, j % NYG, :], None, y_dram,
                                                bass.IndirectOffsetOnAxis(ap=d_i[0:n, i, t:t + 1], axis=0))\
                            .then_inc(q_yg[j % NYG], 16)

                @block.tensor
                def _(pe):
                    mm = nc.tensor.matmul

                    def to_channels(e):
                        at_least(pe, q_g[e % 2], 8 * 16, 16 * (e // 2 + 1))
                        if e:
                            at_least(pe, q_ue, NE, e)
                        for k in range(KD):
                            last = nc.tensor.transpose(psum[:, P * k:P * (k + 1)], ug[:, e % 2, P * k:P * (k + 1)], ident)
                        last.then_inc(q_tr, 1)

                    for j in range(2 * TT):
                        at_least(pe, q_oh, 2 * TT, j + 1)
                        for part in range(2):
                            last = mm(bank(5, NE), onehot[:, j, :], toke[:, part, j % 2, j // 2, :],
                                      start=(j + part == 0), stop=(j == 2 * TT - 1 and part == 1))
                    last.then_inc(q_pid, 1)
                    to_channels(0)
                    for i in range(NE + 1):
                        if i < NE:
                            at_least(pe, q_ue, NE, i + 1)
                            at_least(pe, s_we[i % NWE], 4 * 32, 32 * (i // NWE + 1))
                            if i >= 2:
                                at_least(pe, q_h, NE, i - 1)
                            for k in range(KD):
                                last = mm(bank(2 + i % 2), ue[:, i % 2, k, :], w_gu[i % NWE][:, k, :], start=(k == 0),
                                          stop=(k == KD - 1))
                            last.then_inc(q_gu, 1)
                        if i:
                            e = i - 1
                            at_least(pe, q_h, NE, e + 1)
                            if e:
                                at_least(pe, q_hte, NE, e)
                            for f in range(2):
                                last = nc.tensor.transpose(bank(4)[:, P * f:P * f + P], hh[:, P * f:P * f + P], ident)
                            last.then_inc(q_ht, 1)
                        if i + 1 < NE:
                            to_channels(i + 1)
                        if i:
                            e = i - 1
                            at_least(pe, q_hte, NE, e + 1)
                            if e:
                                at_least(pe, q_yo, NE, e)
                            for f in range(2):
                                for q in range(2):
                                    last = mm(bank(6 + q), hht[:, f, :], w_dn[e % NWE][:, f, 512 * q:512 * q + 512],
                                              start=(f == 0), stop=(f == 1))
                            last.then_inc(q_dn, 1)

                @block.scalar
                def _(act):
                    a = nc.scalar.activation
                    for i in range(NE + 1):
                        if i < NE:
                            at_least(act, q_gu, NE, i + 1)
                            if i:
                                at_least(act, q_h, NE, i)
                            a(sig, bank(2 + i % 2, FF), ACT.Sigmoid).then_inc(q_sig, 1)
                        if i:
                            at_least(act, q_ht, NE, i)
                            a(hht.rearrange("p f t -> p (f t)"), bank(4, 256), ACT.Copy).then_inc(q_hte, 1)
                        if i:
                            e = i - 1
                            at_least(act, q_dn, NE, e + 1)
                            if e >= 2:
                                at_least(act, q_yd[e % 2], 8 * 16, 16 * (e // 2))
                            a(yo[:, e % 2, :], psum[:, 3072:4096], ACT.Copy).then_inc(q_yo, 1)
                            at_least(act, q_yo, NE, e + 1)
                            act.dma_start(y_view[:, e, :], yo[:, e % 2, :]).then_inc(q_yd[e % 2], 16)

                    for t in range(TT):
                        n = rows_of(t)
                        at_least(act, q_cb, 2 * TT, 2 * t + 2)
                        if t:
                            at_least(act, z_ss, TT, t)
                        a(junk[0:n], x2t[0:n, t, :], ACT.Square, accum_out=fs[0:n, t:t + 1]).then_inc(z_ss, 1)
                        at_least(act, z_ss, TT, t + 1)
                        a(fs[0:n, TT + t:TT + t + 1], fs[0:n, t:t + 1], ACT.Sqrt, scale=1.0 / D,
                          bias=eps2[0:n, :]).then_inc(z_rt, 1)

                @block.vector
                def _(dve):
                    v = nc.vector

                    def tt(out, x, y, op, s):
                        v.tensor_tensor(out, x, y, op).then_inc(s, 1)

                    def rows_in(e):
                        at_least(dve, q_tr, NE, e + 1)
                        tt(ue[:, e % 2], psum[:, 0:1024].rearrange("p (k t) -> p k t", k=KD),
                           bc(vec[:, o2:o2 + KD], P), ALU.mult, q_ue)

                    o2 = VEC["norm2_g"]
                    for j in range(2 * TT):
                        v.tensor_scalar(onehot[:, j, :], cc("slot"), place[:, j % 2, j // 2:j // 2 + 1], None,
                                        ALU.is_equal).then_inc(q_oh, 1)
                    at_least(dve, q_pid, 1, 1)
                    v.tensor_copy(ids[:, :], bank(5, NE)).then_inc(q_id, 1)
                    steps = [0]

                    def run(ins):
                        steps[0] += 1
                        ins.then_inc(q_dv, 1)
                        at_least(dve, q_dv, NDV, steps[0])

                    def mul(out, x, y):
                        run(v.tensor_tensor(out, x, y, ALU.mult))

                    run(v.tensor_reduce(sm[:, 0:TT], ex[:, 0:TT, :], AX.X, ALU.add))
                    run(v.tensor_scalar(sel, rank[:, TT:NS, :], 1.5, None, ALU.is_lt))
                    mul(exs, ex[:, TT:NS, :], sel)
                    run(v.tensor_reduce(sm[:, TT:NS], exs, AX.X, ALU.add))
                    run(v.reciprocal(sm, sm))
                    mul(gw, ga, bc(sm[:, 0:TT], 4))
                    mul(exs, exs, bc(sm[:, TT:NS], 4))
                    mul(wts.rearrange("p t (g e) -> p (t g) e", g=NG), exs, bc(gw.rearrange("p t g -> p (t g)"), 4))
                    mul(tq, ff, wts.unsqueeze(1).broadcast_to([P, 2, TT, NE]))
                    run(v.tensor_reduce(c_w[:, :, :], tq, AX.X, ALU.add))
                    mul(tq, ff, cc("expert").unsqueeze(1).unsqueeze(1).broadcast_to([P, 2, TT, NE]))
                    run(v.tensor_reduce(ei, tq, AX.X, ALU.add))
                    run(v.scalar_tensor_tensor(d_f[:, :, :], place[:, :, :], float(NE), ei, ALU.mult, ALU.add))
                    run(v.tensor_scalar(place[:, :, :], place[:, :, :], -float(SLOTS), None, ALU.add))
                    run(v.tensor_scalar(in_r[:, :, :], d_f[:, :, :], 0.0, None, ALU.is_ge))
                    mul(cw_r[:, :, :], c_w[:, :, :], in_r[:, :, :])
                    run(v.tensor_scalar(in_r[:, :, :], d_f[:, :, :], float(ROWS), None, ALU.is_lt))
                    mul(cw_r[:, :, :], cw_r[:, :, :], in_r[:, :, :])
                    run(v.tensor_scalar(dcl[:, :, :], d_f[:, :, :], 0.0, float(ROWS - 1), ALU.max, ALU.min))
                    v.tensor_copy(d_i[:, :, :], dcl[:, :, :]).then_inc(q_ix, 1)
                    assert steps[0] == NDV
                    rows_in(0)
                    for i in range(NE + 1):
                        if i < NE:
                            e = i
                            at_least(dve, q_sig, NE, e + 1)
                            if e:
                                at_least(dve, q_ht, NE, e)
                            b = bank(2 + e % 2)
                            tt(hh, b[:, 0:FF], sig, ALU.mult, q_h1)
                            at_least(dve, q_h1, NE, e + 1)
                            tt(hh, b[:, FF:2 * FF], hh, ALU.mult, q_h)
                        if i + 1 < NE:
                            rows_in(i + 1)
                    def final(t):
                        if t < 0:
                            return
                        n = rows_of(t)
                        at_least(dve, z_rt, TT, t + 1)
                        v.reciprocal(fs[0:n, TT + t:TT + t + 1], fs[0:n, TT + t:TT + t + 1]).then_inc(z_rc, 1)
                        at_least(dve, z_rc, TT, t + 1)
                        if t < 2:
                            at_least(dve, q_yd[t], 8 * 16, 8 * 16)
                        else:
                            at_least(dve, z_out[t % 2], 16 * len(range(t % 2, TT, 2)), 16 * (t // 2))
                        v.scalar_tensor_tensor(yo[0:n, t % 2, :], x2t[0:n, t, :], fs[0:n, TT + t:TT + t + 1],
                                               g_row[0:n, :], ALU.mult, ALU.mult).then_inc(z_y, 1)

                    for j in range(2 * TT):
                        t, i = j // 2, j % 2
                        n = rows_of(t)
                        at_least(dve, q_yg[j % NYG], 16 * len(range(j % NYG, 2 * TT, NYG)), 16 * (j // NYG + 1))
                        v.scalar_tensor_tensor(x2t[0:n, t, :], yg[0:n, j % NYG, :], cw_r[0:n, i, t:t + 1], x2t[0:n, t, :],
                                               ALU.mult, ALU.add).then_inc(q_cb, 1)
                        if j % 2:
                            final(t - 1)
                        else:
                            at_least(dve, q_cb, 2 * TT, j + 1)
                    final(TT - 1)


def host_inputs(x):
    c = np.ascontiguousarray
    out = {}
    xs = np.concatenate([x["meta_tokens"], x["x_prompt"][0], x["x_sample"][:, 0]], 0)
    out["x"] = c(xs.T.reshape(KD, P, T).transpose(1, 0, 2))
    out["con"] = constants()
    vec = np.concatenate([x[n][0].reshape(-1, P) for n in ("norm1_g", "shift_mu", "decay_w0", "aaa_a0", "k_k", "k_a", "r_k", "lnx_w", "lnx_b", "norm2_g")], 0)
    out["vec"] = c(vec.T)
    out["sh0"] = c(x["state_shift"][0].reshape(8, 14, P).transpose(2, 1, 0))
    out["up_wa"] = c(np.concatenate([x["decay_up"][0], x["aaa_up"][0]], 0))
    out["up_g"] = c(x["gate_up"][0])
    def tiles(w):
        return c(w.reshape(w.shape[0] // P, P, w.shape[1] // P, P).transpose(2, 1, 0, 3))
    out["w_in"] = tiles(x["w_in"][0])
    out["w_bb"] = tiles(x["w_branch_b"][0])
    out["w_ba"] = tiles(x["w_branch_a"][0])
    out["w_out"] = tiles(x["w_out"][0])
    out["wkv0"] = c(x["state_wkv"][0].reshape(8, 4, 2, 64, 64).transpose(2, 4, 1, 0, 3).reshape(P, 4, 8, 64))
    out["rets0"] = c(x["state_ret"][0].transpose(2, 1, 0, 3))
    w = np.concatenate([x["expert_w_gate"][0], x["expert_w_up"][0]], 2)
    out["w_gu"] = c(w.reshape(16, KD, P, 512).transpose(0, 2, 1, 3).reshape(16, P, 4096))
    out["w_dn"] = c(x["expert_w_down"][0].reshape(16, 2, P, D).transpose(0, 2, 1, 3).reshape(16, P, 2048))
    out["w_r"] = c(np.concatenate([x["router_group_w"][0], x["router_expert_w"][0]], 1).reshape(KD, P, 20).transpose(1, 0, 2))
    out["b_r"] = c(np.broadcast_to(np.concatenate([x["router_group_b"][0], x["router_expert_b"][0]]), (P, 20)))
    out["gfrow"] = c(np.broadcast_to(x["final_norm_g"], (P, D)))
    return out

def host_outputs(o):
    r = {}
    r["wkvp"] = o["wkvp"].reshape(2, 64, 4, 64).transpose(2, 0, 3, 1).reshape(1, 1, 8, 64, 64)
    r["wkvs"] = o["wkvs"].reshape(2, 64, 4, 8, 64).transpose(3, 2, 0, 4, 1).reshape(1, 8, 8, 64, 64)
    sh = o["shift"].transpose(2, 1, 0).reshape(9, 14 * P)
    r["shiftp"], r["shifts"] = sh[0].reshape(1, 1, -1), sh[1:].reshape(1, 8, -1)
    r["retp"] = o["retp"].transpose(1, 0, 2)[None, None]
    r["rets"] = o["rets"].transpose(2, 1, 0, 3)[None]
    return r


OUTS = {"y": (T, D), "wkvp": (P, NP, 64), "shift": (P, SHIFT_TILES, 9), "retp": (P, RH, P),
        "wkvs": (P, NP, NB, 64), "rets": (P, RH, NB, P)}


def kernel(**inputs):
    import concourse.bacc as bacc
    from concourse.bass_utils import run_bass_kernel_spmd

    nc = bacc.Bacc("TRN2", target_bir_lowering=False, num_devices=1)
    arrays = host_inputs({n: np.asarray(a) for n, a in inputs.items()})
    ins = {n: nc.dram_tensor(f"in_{n}", a.shape, F32, kind="ExternalInput").ap() for n, a in arrays.items()}
    outs = {n: nc.dram_tensor(f"out_{n}", s, F32, kind="ExternalOutput").ap() for n, s in OUTS.items()}
    hybrid_step(nc, ins, outs)
    r = run_bass_kernel_spmd(nc, [{f"in_{n}": a for n, a in arrays.items()}], core_ids=[0]).results[0]
    o = host_outputs({n: r[f"out_{n}"] for n in OUTS})
    y = r["out_y"]
    return (y[None, META:TP], y[TP:T, None], o["wkvp"], o["shiftp"], o["retp"], o["wkvs"], o["shifts"], o["rets"])
```
